# Optimizing a Trainium2 kernel written in Bass

```python
import math
import jax, jax.numpy as jnp
from jax import lax
import numpy as np

D_MODEL = 1024
BATCH = 1
SEQ = 512
DEPTH = 1
DEC_BATCH = 1
DEC_SEQ = 2048
PAST_LEN = 128

GRID_W = 64
HEAD_DIM = 64
RWKV_WIDTH = 512
RWKV_HEADS = RWKV_WIDTH // HEAD_DIM
ATTN_WIDTH = D_MODEL - RWKV_WIDTH
ATTN_Q_HEADS = ATTN_WIDTH // HEAD_DIM
ATTN_KV_HEADS = 2
KV_WIDTH = ATTN_KV_HEADS * HEAD_DIM
W_LORA = 64
A_LORA = 64
G_LORA = 128
RWKV_COLS = 3 * RWKV_WIDTH + W_LORA + A_LORA + G_LORA
IN_COLS = RWKV_COLS + ATTN_WIDTH + 2 * KV_WIDTH
Q_BLOCK = 128
ROPE_THETA = 10000.0
ROPE_PAIRS = HEAD_DIM // 4
N_EXPERTS = 16
CAPACITY_FACTOR = 2
D_EXPERT = 1024
NORM_EPS = 1e-6
GN_EPS = 64e-5

kernel_name = "hymba_rwkv7_gqa_axial_ec_moe_encoder"

def rms_norm(x, gain, eps=NORM_EPS):
    xf = x.astype(jnp.float32)
    y = xf * lax.rsqrt(jnp.mean(xf * xf, axis=-1, keepdims=True) + eps)
    return (y * gain.astype(jnp.float32)).astype(x.dtype)

def axial_angles(n):
    rows = n // GRID_W
    row = jnp.repeat(jnp.arange(rows, dtype=jnp.float32), GRID_W)
    col = jnp.tile(jnp.arange(GRID_W, dtype=jnp.float32), rows)
    inv_freq = ROPE_THETA ** (-jnp.arange(ROPE_PAIRS, dtype=jnp.float32) / ROPE_PAIRS)
    return row[:, None] * inv_freq, col[:, None] * inv_freq

def rope_half(x, ang):
    cos = jnp.cos(ang)[None, :, None, :]
    sin = jnp.sin(ang)[None, :, None, :]
    x1, x2 = x[..., :ROPE_PAIRS], x[..., ROPE_PAIRS:]
    return jnp.concatenate([x1 * cos - x2 * sin, x2 * cos + x1 * sin], axis=-1)

def axial_rope(x, ang_row, ang_col):
    xf = x.astype(jnp.float32)
    half = HEAD_DIM // 2
    out = jnp.concatenate([rope_half(xf[..., :half], ang_row), rope_half(xf[..., half:], ang_col)], axis=-1)
    return out.astype(x.dtype)

def block_attention(q, k, v):
    b, n, hq, dh = q.shape
    hkv = k.shape[2]
    grp = hq // hkv
    nblk = n // Q_BLOCK
    qb = q.reshape(b, nblk, Q_BLOCK, hkv, grp, dh).transpose(1, 0, 2, 3, 4, 5)
    scale = 1.0 / math.sqrt(dh)

    def one_block(qi):
        s = jnp.einsum('bqkgd,bskd->bkgqs', qi, k).astype(jnp.float32) * scale
        p = jax.nn.softmax(s, axis=-1).astype(v.dtype)
        return jnp.einsum('bkgqs,bskd->bqkgd', p, v)

    out = lax.map(one_block, qb)
    return out.transpose(1, 0, 2, 3, 4, 5).reshape(b, n, hq * dh)

def centred_shift(x, taps):
    prev = jnp.pad(x[:, :-1], ((0, 0), (1, 0), (0, 0)))
    nxt = jnp.pad(x[:, 1:], ((0, 0), (0, 1), (0, 0)))
    return taps[0] * prev + taps[1] * x + taps[2] * nxt

def wkv7_scan(r, decay, k, v, kk_neg, kk_b, reverse):
    b, n, h, d = r.shape

    def step(state, inp):
        r_t, w_t, k_t, v_t, an_t, b_t = inp
        sa = jnp.einsum('bhij,bhj->bhi', state, an_t)
        state = (state * w_t[:, :, None, :] + sa[..., None] * b_t[:, :, None, :]
                 + v_t[..., None] * k_t[:, :, None, :])
        return state, jnp.einsum('bhij,bhj->bhi', state, r_t)

    s0 = jnp.zeros((b, h, d, d), jnp.float32)
    xs = tuple(jnp.swapaxes(t, 0, 1) for t in (r, decay, k, v, kk_neg, kk_b))
    _, ys = lax.scan(step, s0, xs, reverse=reverse)
    return jnp.swapaxes(ys, 0, 1)

def rwkv7_mix(feat, w0, w_lora_up, a0, a_lora_up, k_k, k_a, r_k, g_lora_up, ln_g, ln_b):
    f32 = jnp.float32
    b, n, _ = feat.shape
    feat = feat.astype(f32)
    splits = [RWKV_WIDTH, 2 * RWKV_WIDTH, 3 * RWKV_WIDTH,
              3 * RWKV_WIDTH + W_LORA, 3 * RWKV_WIDTH + W_LORA + A_LORA]
    r, k, v, wd, ad, gd = jnp.split(feat, splits, axis=-1)
    heads = lambda t: t.reshape(b, n, RWKV_HEADS, HEAD_DIM)
    kk = heads(k * k_k.astype(f32))
    kk = kk / jnp.maximum(jnp.linalg.norm(kk, axis=-1, keepdims=True), 1e-12)
    gate = jax.nn.sigmoid(gd) @ g_lora_up.astype(f32)
    tw = jnp.tanh(wd)
    y = jnp.zeros((b, n, RWKV_HEADS, HEAD_DIM), f32)
    k_bonus = jnp.zeros_like(k)
    for direction, reverse in ((0, False), (1, True)):
        w_log = -jax.nn.softplus(-(w0[direction].astype(f32) + tw @ w_lora_up[direction].astype(f32))) - 0.5
        decay = jnp.exp(-jnp.exp(w_log))
        a = jax.nn.sigmoid(a0[direction].astype(f32) + ad @ a_lora_up[direction].astype(f32))
        k_dir = k * (1.0 + (a - 1.0) * k_a.astype(f32))
        y = y + wkv7_scan(heads(r), heads(decay), heads(k_dir), heads(v), -kk, kk * heads(a), reverse)
        k_bonus = k_bonus + 0.5 * k_dir
    mu = jnp.mean(y, axis=-1, keepdims=True)
    var = jnp.mean(jnp.square(y - mu), axis=-1, keepdims=True)
    y = ((y - mu) * lax.rsqrt(var + GN_EPS)).reshape(b, n, RWKV_WIDTH) * ln_g.astype(f32) + ln_b.astype(f32)
    bonus = jnp.sum(heads(r) * heads(k_bonus) * r_k.astype(f32), axis=-1, keepdims=True) * heads(v)
    return (y + bonus.reshape(b, n, RWKV_WIDTH)) * gate

def expert_choice_moe(x, w_router, w_gate, w_up, w_down):
    b, n, d = x.shape
    num = b * n
    tokens = x.reshape(num, d)
    cap = CAPACITY_FACTOR * num // N_EXPERTS
    aff = jax.nn.softmax((tokens @ w_router).astype(jnp.float32), axis=-1)
    gates, idx = lax.top_k(aff.T, cap)
    xs = tokens[idx]
    hid = jax.nn.silu(jnp.einsum('ecd,edf->ecf', xs, w_gate)) * jnp.einsum('ecd,edf->ecf', xs, w_up)
    out = jnp.einsum('ecf,efd->ecd', hid, w_down) * gates[..., None].astype(x.dtype)
    y = jnp.zeros_like(tokens).at[idx.reshape(-1)].add(out.reshape(-1, d))
    return y.reshape(b, n, d)

def encoder_layer(x, norm1, w_in, shift_taps, w0, w_lora_up, a0, a_lora_up, k_k, k_a, r_k,
                  g_lora_up, ln_g, ln_b, q_norm, k_norm, w_out, norm2, w_router,
                  expert_w_gate, expert_w_up, expert_w_down):
    b, n, _ = x.shape
    proj = rms_norm(x, norm1) @ w_in
    rwkv_feat = centred_shift(proj[..., :RWKV_COLS], shift_taps)
    q, k, v = jnp.split(proj[..., RWKV_COLS:], [ATTN_WIDTH, ATTN_WIDTH + KV_WIDTH], axis=-1)
    ang_row, ang_col = axial_angles(n)
    q = axial_rope(rms_norm(q.reshape(b, n, ATTN_Q_HEADS, HEAD_DIM), q_norm), ang_row, ang_col)
    k = axial_rope(rms_norm(k.reshape(b, n, ATTN_KV_HEADS, HEAD_DIM), k_norm), ang_row, ang_col)
    v = v.reshape(b, n, ATTN_KV_HEADS, HEAD_DIM)
    attn_out = block_attention(q, k, v)
    rwkv_out = rwkv7_mix(rwkv_feat, w0, w_lora_up, a0, a_lora_up, k_k, k_a, r_k,
                         g_lora_up, ln_g, ln_b).astype(x.dtype)
    h = x + jnp.concatenate([rwkv_out, attn_out], axis=-1) @ w_out
    return h + expert_choice_moe(rms_norm(h, norm2), w_router, expert_w_gate, expert_w_up, expert_w_down)

def run_trunk(x, layer_params):
    for l in range(DEPTH):
        x = encoder_layer(x, *(p[l] for p in layer_params))
    return x

def setup_inputs(seed: int = 0) -> dict:
    key = jax.random.key(seed)
    ks = jax.random.split(key, 24)
    nrm = lambda i, shape: jax.random.normal(ks[i], shape, jnp.float32)
    base_taps = jnp.array([0.25, 0.5, 0.25], jnp.float32)[None, :, None]
    return {
        "x_prompt": nrm(0, (BATCH, SEQ, D_MODEL)),
        "x_sample": nrm(1, (DEC_BATCH, DEC_SEQ, D_MODEL)),
        "norm1": 1.0 + 0.1 * nrm(2, (DEPTH, D_MODEL)),
        "w_in": nrm(3, (DEPTH, D_MODEL, IN_COLS)) * D_MODEL ** -0.5,
        "shift_taps": base_taps + 0.05 * nrm(4, (DEPTH, 3, RWKV_COLS)),
        "w0": 0.5 * nrm(5, (DEPTH, 2, RWKV_WIDTH)),
        "w_lora_up": nrm(6, (DEPTH, 2, W_LORA, RWKV_WIDTH)) * 0.5 * W_LORA ** -0.5,
        "a0": 0.5 * nrm(7, (DEPTH, 2, RWKV_WIDTH)),
        "a_lora_up": nrm(8, (DEPTH, 2, A_LORA, RWKV_WIDTH)) * 0.5 * A_LORA ** -0.5,
        "k_k": 1.0 + 0.1 * nrm(9, (DEPTH, RWKV_WIDTH)),
        "k_a": 1.0 + 0.1 * nrm(10, (DEPTH, RWKV_WIDTH)),
        "r_k": 0.1 * nrm(11, (DEPTH, RWKV_HEADS, HEAD_DIM)),
        "g_lora_up": nrm(12, (DEPTH, G_LORA, RWKV_WIDTH)) * G_LORA ** -0.5,
        "ln_g": 1.0 + 0.1 * nrm(13, (DEPTH, RWKV_WIDTH)),
        "ln_b": 0.02 * nrm(14, (DEPTH, RWKV_WIDTH)),
        "q_norm": 1.0 + 0.1 * nrm(15, (DEPTH, HEAD_DIM)),
        "k_norm": 1.0 + 0.1 * nrm(16, (DEPTH, HEAD_DIM)),
        "w_out": nrm(17, (DEPTH, D_MODEL, D_MODEL)) * D_MODEL ** -0.5,
        "norm2": 1.0 + 0.1 * nrm(18, (DEPTH, D_MODEL)),
        "w_router": nrm(19, (DEPTH, D_MODEL, N_EXPERTS)) * D_MODEL ** -0.5,
        "expert_w_gate": nrm(20, (DEPTH, N_EXPERTS, D_MODEL, D_EXPERT)) * D_MODEL ** -0.5,
        "expert_w_up": nrm(21, (DEPTH, N_EXPERTS, D_MODEL, D_EXPERT)) * D_MODEL ** -0.5,
        "expert_w_down": nrm(22, (DEPTH, N_EXPERTS, D_EXPERT, D_MODEL)) * D_EXPERT ** -0.5,
    }

def reference(x_prompt, x_sample, norm1, w_in, shift_taps, w0, w_lora_up, a0, a_lora_up,
              k_k, k_a, r_k, g_lora_up, ln_g, ln_b, q_norm, k_norm, w_out, norm2, w_router,
              expert_w_gate, expert_w_up, expert_w_down):
    layer_params = (norm1, w_in, shift_taps, w0, w_lora_up, a0, a_lora_up, k_k, k_a, r_k,
                    g_lora_up, ln_g, ln_b, q_norm, k_norm, w_out, norm2, w_router,
                    expert_w_gate, expert_w_up, expert_w_down)
    y_prompt = run_trunk(x_prompt, layer_params)
    y_sample = run_trunk(x_sample, layer_params)
    return (y_prompt, y_sample)


_drawn_inputs = setup_inputs


def setup_inputs(seed=0):
    import zlib

    import numpy as np

    out = dict(_drawn_inputs(seed))
    spreads = {}
    factors = {'k_k': 2.928, 'ln_b': 6.368, 'q_norm': 6.8, 'k_norm': 5.412}
    for name, (base, spread) in spreads.items():
        noise = np.random.default_rng([zlib.crc32(name.encode()), seed]).standard_normal(out[name].shape)
        drawn = base * np.exp(spread * noise) if base else spread * noise
        out[name] = __import__('jax').numpy.asarray(drawn.astype(out[name].dtype))
    for name, factor in factors.items():
        out[name] = (out[name] * factor).astype(out[name].dtype)
    return out
```

```python
from contextlib import ExitStack
import numpy as np
import concourse.bass as bass
from concourse import mybir

F32 = mybir.dt.float32
F32R = mybir.dt.float32r
BF16 = mybir.dt.bfloat16
I32 = mybir.dt.int32
U32 = mybir.dt.uint32
ALU = mybir.AluOpType
ACT = mybir.ActivationFunctionType
AX = mybir.AxisListType

P = 128
D = 1024
DC = D // P
NS, NP_ = 2048, 512
N = NS + NP_
NT = N // P
HD = 64
RW = 512
RC = 1792
FT = RC // P
QH, KVH = 8, 2
NH = QH + KVH
QK = NH * HD
AC = QK + KVH * HD
NCOL = N + 4
EPS = 1e-6


def opened(nc, ctx):
    def sb(name, shape, dt=F32):
        return ctx.enter_context(nc.sbuf_tensor(name, shape, dt))

    def ps(name, shape=(P, 512), dt=F32):
        return ctx.enter_context(nc.psum_tensor(name, list(shape), dt))

    def sems(names, prefix=""):
        handles = {n: nc.alloc_semaphore(name=prefix + n) for n in names.split()}
        ctx.callback(clear, nc, list(handles.values()))
        return handles

    return sb, ps, sems


def clear(nc, handles):
    nc.clear_and_free_semaphores(handles)
    nc.all_engine_barrier()


def bc(ap, shape):
    return ap.to_broadcast(shape)


def identity(nc, pool, tile, done):
    pool.memset(tile, 0.0).then_inc(done, 1)
    pool.wait_ge(done, 1)
    pool.affine_select(out=tile, in_=tile, compare_op=ALU.not_equal, fill=1.0, base=0,
                       pattern=[[-1, P]], channel_multiplier=1).then_inc(done, 1)


def attention_inputs(nc, x, norm1, w_in, q_norm, k_norm, rope, xT_hi, xT_lo, qT, KT, VS):
    with ExitStack() as ctx:
        sb, ps, sems = opened(nc, ctx)
        w_raw = sb("w_raw", [P, AC])
        w_hi = sb("w_hi", [P, DC, AC], F32R)
        w_lo = sb("w_lo", [P, DC, AC], F32R)
        gain = sb("gain", [P, D])
        qk_gain = sb("qk_gain", [P, NH, HD])
        eps = sb("eps", [P, 1])
        zero_col = sb("zero_col", [P, DC])
        zf = sb("zf", [P, DC])
        ident = sb("ident", [P, P])
        x_in = sb("x_in", [P, 2, D])
        junk = sb("junk", [P, D])
        ss = sb("ss", [P, 2])
        sd = sb("sd", [P, 2])
        rs = sb("rs", [P, 2])
        xn = sb("xn", [P, 2, D])
        xh = sb("xh", [P, 2, DC, P], F32R)
        xl = sb("xl", [P, 2, DC, P], F32R)
        cs = sb("cs", [P, 2, 2, HD])
        qkv = sb("qkv", [P, 2, AC])
        sq = sb("sq", [P, QK])
        hss = sb("hss", [P, NH])
        hsd = sb("hsd", [P, NH])
        hrs = sb("hrs", [P, NH])
        qn = sb("qn", [P, NH, HD])
        qg = sb("qg", [P, NH, HD])
        rot = sb("rot", [P, NH, HD])
        qc = sb("qc", [P, NH, HD])
        qr = sb("qr", [P, NH, HD])
        hl = sb("hl", [P, QH, 2, HD], F32R)
        kd = sb("kd", [P, KVH, 2, 2, HD], F32R)
        q_out = sb("q_out", [P, 2, QH, P], F32R)
        pT = [ps(f"pT{k}") for k in range(2)]
        pQ = ps("pQ")
        pKV = ps("pKV")
        pR = [ps(f"pR{k}") for k in range(3)]
        s = sems("a_id a_const a_gain a_wl0 a_wl1 a_whi a_wlo a_x0 a_x1 a_cs0 a_cs1 a_ss a_sd a_rs a_xn a_tr a_xh a_xl a_proj a_q"
                 " a_kv a_sq a_hss a_hsd a_hrs a_qn a_qg a_rotA a_rotB a_qc a_qr a_hi a_lo a_khi a_klo a_vhi a_vlo"
                 " a_rtr a_qo0 a_qo1 a_ko a_st0 a_st1 a_zero a_xfree a_csfree")
        block = ctx.enter_context(nc.Block())
        Q0 = qkv

        @block.sync
        def _(sp):
            sp.dma_start(gain[:], norm1.partition_broadcast(P)).then_inc(s["a_gain"], 16)
            for h in range(QH):
                sp.dma_start(qk_gain[:, h, :], q_norm.partition_broadcast(P)).then_inc(s["a_gain"], 16)
            for h in range(KVH):
                sp.dma_start(qk_gain[:, QH + h, :], k_norm.partition_broadcast(P)).then_inc(s["a_gain"], 16)
            with sp.Fori(0, NT // 2) as i:
                for b in range(2):
                    t = 2 * i + b
                    sp.wait_ge(s["a_xfree"], t + 1)
                    sp.dma_start(x_in[:, b, :], x[bass.ds(t * P, P), :]).then_inc(s[f"a_x{b}"], 16)
                    sp.wait_ge(s["a_csfree"], t + 1)
                    sp.dma_start(cs[:, b, :, :], rope[bass.ds(t * P, P), :, :]).then_inc(s[f"a_cs{b}"], 16)

        @block.gpsimd
        def _(pool):
            pool.memset(eps[:], EPS).then_inc(s["a_const"], 1)
            pool.memset(zf[:], 0.0).then_inc(s["a_const"], 1)
            pool.wait_ge(s["a_const"], 2)
            pool.tensor_copy(zero_col[:], zf[:]).then_inc(s["a_const"], 1)
            pool.wait_ge(s["a_const"], 3)
            for col in (0, NS + 1, N + 2):
                for dst in (xT_hi, xT_lo):
                    pool.dma_start(dst[:, :, col:col + 1].rearrange("c p o -> p c o"), zero_col[:].rearrange("p (c o) -> p c o", o=1), allow_slow_non_contiguous=True).then_inc(s["a_zero"], 16)
            identity(nc, pool, ident[:], s["a_id"])
            for c in range(DC):
                pool.dma_start(w_raw[:], w_in[c * P:(c + 1) * P, RC:]).then_inc(s["a_wl0"], 16)
                pool.wait_ge(s["a_whi"], c + 1)
                pool.tensor_tensor(w_lo[:, c, :], w_raw[:], w_hi[:, c, :].bitcast(F32), ALU.subtract).then_inc(s["a_wlo"], 1)
                pool.wait_ge(s["a_wlo"], c + 1)
            with pool.Fori(0, NT // 2) as i:
                for b in range(2):
                    t = 2 * i + b
                    pool.wait_ge(s["a_kv"], t + 1)
                    pool.tensor_copy(VS[:, bass.ds(t, 1), :, 0:HD], qkv[:, b:b + 1, QK:].rearrange("p o (g d) -> p o g d", g=KVH)).then_inc(s["a_vhi"], 1)
                    pool.wait_ge(s["a_q"], t + 1)
                    pool.tensor_tensor(sq[:], qkv[:, b, 0:QK], qkv[:, b, 0:QK], ALU.mult).then_inc(s["a_sq"], 1)
                    pool.wait_ge(s["a_vhi"], t + 1)
                    pool.tensor_tensor(VS[:, bass.ds(t, 1), :, HD:], qkv[:, b:b + 1, QK:].rearrange("p o (g d) -> p o g d", g=KVH),
                                       VS[:, bass.ds(t, 1), :, 0:HD].bitcast(F32), ALU.subtract).then_inc(s["a_vlo"], 1)
                    pool.wait_ge(s["a_qn"], t + 1)
                    pool.tensor_tensor(qg[:], qn[:], qk_gain[:], ALU.mult).then_inc(s["a_qg"], 1)
                    pool.wait_ge(s["a_qg"], t + 1)
                    pool.wait_ge(s[f"a_cs{b}"], 16 * (i + 1))
                    pool.tensor_tensor(qc[:], qg[:], bc(cs[:, b, 0:1, :], [P, NH, HD]), ALU.mult).then_inc(s["a_qc"], 1)

        @block.scalar
        def _(act):
            for c in range(DC):
                act.wait_ge(s["a_wl0"], 16 * (c + 1))
                act.activation(w_hi[:, c, :], w_raw[:], ACT.Copy).then_inc(s["a_whi"], 1)
            act.wait_ge(s["a_const"], 3)
            for b in range(2):
                act.sem_inc(s[f"a_st{b}"], 48)
            with act.Fori(0, NT // 2) as i:
                for b in range(2):
                    t = 2 * i + b
                    act.wait_ge(s[f"a_x{b}"], 16 * (i + 1))
                    act.activation(junk[:], x_in[:, b, :], ACT.Square, accum_out=ss[:, b:b + 1]).then_inc(s["a_ss"], 1)
                    act.wait_ge(s["a_ss"], t + 1)
                    act.activation(sd[:, b:b + 1], ss[:, b:b + 1], ACT.Sqrt, bias=eps[:, 0:1], scale=1.0 / D).then_inc(s["a_sd"], 1)
                    act.wait_ge(s[f"a_st{b}"], 48 * (i + 1))
                    act.wait_ge(s["a_tr"], t + 1)
                    for k in range(2):
                        last = act.activation(xh[:, b, 4 * k:4 * k + 4, :], pT[k][:].rearrange("p (c t) -> p c t", c=4), ACT.Copy)
                    last.then_inc(s["a_xh"], 1)
                    act.wait_ge(s["a_proj"], t + 1)
                    act.activation(qkv[:, b, QH * HD:], pKV[:, 0:AC - QH * HD], ACT.Copy).then_inc(s["a_kv"], 1)
                    act.activation(qkv[:, b, 0:QH * HD], pQ[:], ACT.Copy).then_inc(s["a_q"], 1)
                    act.wait_ge(s["a_hss"], t + 1)
                    act.activation(hsd[:], hss[:], ACT.Sqrt, bias=eps[:, 0:1], scale=1.0 / HD).then_inc(s["a_hsd"], 1)
                    act.wait_ge(s["a_rtr"], t + 1)
                    for k in range(2):
                        last = act.activation(q_out[:, b, 4 * k:4 * k + 4, :], pR[k][:].rearrange("p (c t) -> p c t", c=4), ACT.Copy)
                    last.then_inc(s[f"a_qo{b}"], 1)
                    act.wait_ge(s[f"a_qo{b}"], i + 1)
                    act.wait_ge(s["a_xl"], t + 1)
                    for dst, src in ((xT_hi, xh), (xT_lo, xl)):
                        act.dma_start(dst[:, :, bass.ds(t * P + 1 + (t >> 4), P)].rearrange("c p t -> p c t"), src[:, b, :, :].bitcast(F32)).then_inc(s[f"a_st{b}"], 16)
                    act.dma_start(qT[bass.ds(t, 1), :, :].rearrange("o p n -> (o p) n"), q_out[:, b, :, :].rearrange("p h t -> p (h t)").bitcast(F32)).then_inc(s[f"a_st{b}"], 16)
            act.wait_ge(s["a_zero"], 96)
            for b in range(2):
                act.wait_ge(s[f"a_st{b}"], 48 * (NT // 2 + 1))

        @block.vector
        def _(dve):
            dve.sem_inc(s["a_xfree"], 2)
            dve.sem_inc(s["a_csfree"], 2)
            dve.wait_ge(s["a_gain"], 16 * (1 + NH))
            with dve.Fori(0, NT // 2) as i:
                for b in range(2):
                    t = 2 * i + b
                    dve.wait_ge(s["a_sd"], t + 1)
                    dve.reciprocal(rs[:, b:b + 1], sd[:, b:b + 1]).then_inc(s["a_rs"], 1)
                    dve.wait_ge(s["a_rs"], t + 1)
                    dve.scalar_tensor_tensor(out=xn[:, b, :], in0=x_in[:, b, :], scalar=rs[:, b:b + 1], in1=gain[:],
                                             op0=ALU.mult, op1=ALU.mult).then_inc(s["a_xn"], 1)
                    dve.wait_ge(s["a_xn"], t + 1)
                    dve.sem_inc(s["a_xfree"], 1)
                    dve.wait_ge(s["a_xh"], t + 1)
                    for k in range(2):
                        last = dve.tensor_tensor(xl[:, b, 4 * k:4 * k + 4, :], pT[k][:].rearrange("p (c t) -> p c t", c=4),
                                                 xh[:, b, 4 * k:4 * k + 4, :].bitcast(F32), ALU.subtract)
                    last.then_inc(s["a_xl"], 1)
                    dve.wait_ge(s["a_sq"], t + 1)
                    dve.tensor_reduce(hss[:], sq[:].rearrange("p (h d) -> p h d", h=NH), AX.X, ALU.add).then_inc(s["a_hss"], 1)
                    dve.wait_ge(s["a_hsd"], t + 1)
                    dve.reciprocal(hrs[:], hsd[:]).then_inc(s["a_hrs"], 1)
                    dve.wait_ge(s["a_hrs"], t + 1)
                    dve.tensor_tensor(qn[:], qkv[:, b, 0:QK].rearrange("p (h d) -> p h d", h=NH),
                                      bc(hrs[:].rearrange("p (h o) -> p h o", o=1), [P, NH, HD]), ALU.mult).then_inc(s["a_qn"], 1)
                    dve.wait_ge(s["a_qg"], t + 1)
                    dve.wait_ge(s[f"a_cs{b}"], 16 * (i + 1))
                    halves = [m[:].rearrange("p h (a x j) -> p h a x j", a=2, x=2) for m in (rot, qg)]
                    sin = cs[:, b, 1:2, :].rearrange("p o (a x j) -> p o a x j", a=2, x=2)
                    for k in range(2):
                        last = dve.tensor_tensor(halves[0][:, :, :, k, :], halves[1][:, :, :, 1 - k, :],
                                                 bc(sin[:, :, :, k, :], [P, NH, 2, 16]), ALU.mult)
                    last.then_inc(s["a_rotA"], 1)
                    dve.wait_ge(s["a_rotA"], t + 1)
                    dve.wait_ge(s["a_qc"], t + 1)
                    dve.tensor_tensor(qr[:], qc[:], rot[:], ALU.add).then_inc(s["a_qr"], 1)
                    dve.wait_ge(s["a_qr"], t + 1)
                    dve.sem_inc(s["a_csfree"], 1)
                    dve.tensor_copy(hl[:, :, 0, :], qr[:, 0:QH, :])
                    dve.tensor_copy(kd[:, :, 0, :, :], bc(qr[:, QH:, :].rearrange("p g (o d) -> p g o d", o=1), [P, KVH, 2, HD])).then_inc(s["a_hi"], 1)
                    dve.wait_ge(s["a_hi"], t + 1)
                    dve.tensor_tensor(hl[:, :, 1, :], qr[:, 0:QH, :], hl[:, :, 0, :].bitcast(F32), ALU.subtract)
                    dve.tensor_tensor(kd[:, :, 1, :, :], bc(qr[:, QH:, :].rearrange("p g (o d) -> p g o d", o=1), [P, KVH, 2, HD]),
                                      kd[:, :, 0, :, :].bitcast(F32), ALU.subtract).then_inc(s["a_lo"], 1)
                    dve.wait_ge(s["a_rtr"], t + 1)
                    dve.tensor_copy(KT[:, :, bass.ds(t * P, P)], pR[2][:].rearrange("p (c t) -> p c t", c=4)).then_inc(s["a_ko"], 1)

        @block.tensor
        def _(pe):
            pe.wait_ge(s["a_id"], 2)
            pe.wait_ge(s["a_wlo"], DC)
            with pe.Fori(0, NT // 2) as i:
                for b in range(2):
                    t = 2 * i + b
                    pe.wait_ge(s["a_xn"], t + 1)
                    for c in range(DC):
                        last = pe.transpose(pT[c // 4][:, (c % 4) * P:(c % 4 + 1) * P], xn[:, b, c * P:(c + 1) * P], ident[:])
                    last.then_inc(s["a_tr"], 1)
                    pe.wait_ge(s["a_xl"], t + 1)
                    pe.wait_ge(s["a_xh"], t + 1)
                    for out, a, z in ((pKV, QH * HD, AC), (pQ, 0, QH * HD)):
                        for c in range(DC):
                            for k, (l, r) in enumerate(((xh, w_hi), (xh, w_lo), (xl, w_hi))):
                                last = pe.matmul(out[:, 0:z - a], l[:, b, c, :], r[:, c, a:z], start=(c == 0 and k == 0),
                                                 stop=(c == DC - 1 and k == 2))
                    last.then_inc(s["a_proj"], 1)
                    pe.wait_ge(s["a_lo"], t + 1)
                    for h in range(QH):
                        pe.transpose(pR[h // 4][:, (h % 4) * P:(h % 4 + 1) * P], hl[:, h, :, :].rearrange("p a d -> p (a d)").bitcast(F32), ident[:])
                    for k in range(4):
                        last = pe.transpose(pR[2][:, k * P:(k + 1) * P], kd[:, k // 2, k % 2, :, :].rearrange("p a d -> p (a d)").bitcast(F32), ident[:])
                    last.then_inc(s["a_rtr"], 1)


GH = QH // KVH
SCALE = HD ** -0.5


def attention(nc, qT, KT, VS, mixT, first_tile, n_tiles, name):
    nb = n_tiles // 4
    nk = n_tiles * P
    key0 = first_tile * P
    with ExitStack() as ctx:
        sb, ps, sems = opened(nc, ctx)
        identf = sb(name + "identf", [P, P])
        fold = sb(name + "fold", [P, HD])
        q = sb(name + "q", [P, 2, QH, P], F32R)
        mx = sb(name + "mx", [P, 2, nb])
        nm = sb(name + "nm", [P, 2])
        prob = sb(name + "prob", [P, 2, nk])
        den = sb(name + "den", [P, 2, nb])
        dsum = sb(name + "dsum", [P, 2])
        rden = sb(name + "rden", [P, 2])
        ph = sb(name + "ph", [P, n_tiles, GH, P], F32R)
        pl = sb(name + "pl", [P, n_tiles, GH, P], F32R)
        o_sb = sb(name + "o_sb", [P, GH * P])
        o_out = sb(name + "o_out", [HD, 2, GH * P])
        pS = [ps(f"{name}pS{k}") for k in range(nb)]
        pT = [ps(f"{name}pT{k}") for k in range(2)]
        pO = ps(name + "pO")
        pF = ps(name + "pF")
        s = sems("id q0 q1 qfree score mx nm exp ds rd norm tr hi lo pv osb fold oout st0 st1 seen", name + "_")
        block = ctx.enter_context(nc.Block())

        @block.sync
        def _(sp):
            with sp.Fori(0, n_tiles // 2) as i:
                for b in range(2):
                    t = 2 * i + b
                    sp.wait_ge(s["qfree"], t + 1)
                    sp.dma_start(q[:, b, :, :].rearrange("p h t -> p (h t)").bitcast(F32),
                                 qT[bass.ds(first_tile + t, 1), :, :].rearrange("o p n -> (o p) n")).then_inc(s[f"q{b}"], 16)
                    for g in range(KVH):
                        sp.wait_ge(s["oout"], KVH * t + g + 1)
                        rows = mixT[RW + g * GH * HD:RW + (g + 1) * GH * HD, bass.ds(key0 + t * P, P)]
                        sp.dma_start(rows.rearrange("(h d) t -> d h t", h=GH),
                                     o_out[:, g, :].rearrange("d (h t) -> d h t", h=GH)).then_inc(s[f"st{g}"], 16)
            for g in range(2):
                sp.wait_ge(s[f"st{g}"], 16 * (n_tiles + 1))

        @block.gpsimd
        def _(pool):
            identity(nc, pool, identf[:], s["id"])
            pool.memset(fold[:], 0.0).then_inc(s["id"], 1)
            pool.wait_ge(s["id"], 3)
            for h in range(2):
                pool.affine_select(out=fold[:], in_=fold[:], compare_op=ALU.not_equal, fill=1.0, base=-HD * h,
                                   pattern=[[-1, HD]], channel_multiplier=1).then_inc(s["id"], 1)
                pool.wait_ge(s["id"], 4 + h)
            with pool.Fori(0, n_tiles) as t:
                for h in range(QH):
                    n = QH * t + h
                    pool.wait_ge(s["rd"], n + 1)
                    pool.sem_inc(s["seen"], 1)
                    pool.tensor_scalar(prob[:, h % 2, :], prob[:, h % 2, :], rden[:, h % 2:h % 2 + 1], 1.0, ALU.mult, ALU.mult).then_inc(s["norm"], 1)

        @block.scalar
        def _(act):
            for g in range(2):
                act.sem_inc(s[f"st{g}"], 16)
            with act.Fori(0, n_tiles) as t:
                for h in range(QH + 1):
                    if h < QH:
                        n = QH * t + h
                        act.wait_ge(s["nm"], n + 1)
                        for k in range(nb):
                            act.activation(prob[:, h % 2, k * 512:(k + 1) * 512], pS[k][:], ACT.Exp, bias=nm[:, h % 2:h % 2 + 1],
                                           scale=SCALE, accum_out=den[:, h % 2, k:k + 1]).then_inc(s["exp"], 1)
                    if h:
                        g, hh = divmod(h - 1, GH)
                        for k in range(nb):
                            act.wait_ge(s["tr"], nb * (QH * t + h - 1) + k + 1)
                            act.activation(ph[:, 4 * k:4 * k + 4, hh, :], pT[k % 2][:].rearrange("p (c t) -> p c t", c=4), ACT.Copy).then_inc(s["hi"], 1)
                        if hh == GH - 1:
                            act.wait_ge(s["pv"], KVH * t + g + 1)
                            act.activation(o_sb[:], pO[:], ACT.Copy).then_inc(s["osb"], 1)
                            act.wait_ge(s["fold"], KVH * t + g + 1)
                            act.wait_ge(s[f"st{g}"], 16 * (t + 1))
                            act.activation(o_out[:, g, :], pF[0:HD, :], ACT.Copy).then_inc(s["oout"], 1)

        @block.vector
        def _(dve):
            with dve.Fori(0, n_tiles) as t:
                for h in range(QH + 1):
                    if h < QH:
                        n = QH * t + h
                        for k in range(nb):
                            dve.wait_ge(s["score"], nb * n + k + 1)
                            last = dve.tensor_reduce(mx[:, h % 2, k:k + 1], pS[k][:], AX.X, ALU.max)
                        last.then_inc(s["mx"], 1)
                        dve.wait_ge(s["mx"], 2 * n + 1)
                        dve.tensor_reduce(dsum[:, h % 2:h % 2 + 1], mx[:, h % 2, :], AX.X, ALU.max).then_inc(s["mx"], 1)
                        dve.wait_ge(s["mx"], 2 * n + 2)
                        dve.tensor_scalar(nm[:, h % 2:h % 2 + 1], dsum[:, h % 2:h % 2 + 1], -SCALE, None, ALU.mult).then_inc(s["nm"], 1)
                    if h:
                        g, hh = divmod(h - 1, GH)
                        for k in range(nb):
                            n = nb * (QH * t + h - 1) + k
                            dve.wait_ge(s["hi"], n + 1)
                            dve.tensor_tensor(pl[:, 4 * k:4 * k + 4, hh, :], pT[k % 2][:].rearrange("p (c t) -> p c t", c=4),
                                              ph[:, 4 * k:4 * k + 4, hh, :].bitcast(F32), ALU.subtract).then_inc(s["lo"], 1)
                    if h < QH:
                        n = QH * t + h
                        dve.wait_ge(s["exp"], nb * (n + 1))
                        dve.tensor_reduce(dsum[:, h % 2:h % 2 + 1], den[:, h % 2, :], AX.X, ALU.add).then_inc(s["ds"], 1)
                        dve.wait_ge(s["ds"], n + 1)
                        dve.reciprocal(rden[:, h % 2:h % 2 + 1], dsum[:, h % 2:h % 2 + 1]).then_inc(s["rd"], 1)

        @block.tensor
        def _(pe):
            pe.sem_inc(s["qfree"], 2)
            pe.wait_ge(s["id"], 5)
            with pe.Fori(0, n_tiles // 2) as i:
                for b in range(2):
                    t = 2 * i + b
                    for h in range(QH + 1):
                        if h < QH:
                            n = QH * t + h
                            if h == 0:
                                pe.wait_ge(s[f"q{b}"], 16 * (i + 1))
                            for k in range(nb):
                                if h:
                                    pe.wait_ge(s["exp"], nb * (n - 1) + k + 1)
                                for p in range(2):
                                    mm = pe.matmul(pS[k][:], q[:, b, h, :], KT[:, 2 * (h // GH) + p, key0 + k * 512:key0 + (k + 1) * 512],
                                                   start=(p == 0), stop=(p == 1))
                                mm.then_inc(s["score"], 1)
                            if h == QH - 1:
                                pe.wait_ge(s["score"], nb * (n + 1))
                                pe.sem_inc(s["qfree"], 1)
                        if h:
                            g, hh = divmod(h - 1, GH)
                            n = QH * t + h - 1
                            pe.wait_ge(s["norm"], n + 1)
                            for k in range(nb):
                                if k >= 2:
                                    pe.wait_ge(s["lo"], nb * n + k - 1)
                                for c in range(4):
                                    m = 4 * k + c
                                    mm = pe.transpose(pT[k % 2][:, c * P:(c + 1) * P], prob[:, (h - 1) % 2, m * P:(m + 1) * P], identf[:])
                                mm.then_inc(s["tr"], 1)
                            pe.wait_ge(s["lo"], nb * (n + 1))
                            if hh == GH - 1:
                                for m in range(n_tiles):
                                    for k, r in enumerate((ph, pl)):
                                        mm = pe.matmul(pO[:], VS[:, first_tile + m, g, :], r[:, m, :, :].rearrange("p h t -> p (h t)"),
                                                       start=(m == 0 and k == 0), stop=(m == n_tiles - 1 and k == 1))
                                mm.then_inc(s["pv"], 1)
                                pe.wait_ge(s["osb"], KVH * t + g + 1)
                                pe.matmul(pF[0:HD, :], fold[:], o_sb[:], start=True, stop=True).then_inc(s["fold"], 1)


C = 64
NCH = N // C
TB = 256
NB = N // TB
RT = RW // P
KAPPA = float(np.exp(-0.5))
W_R, W_K, W_V, W_WA, W_G = 0, 4, 8, 12, 13


def rwkv_inputs(nc, w_in, shift_taps, w0, w_lora_up, a0, a_lora_up, k_k, k_a, r_k, g_lora_up, xT_hi, xT_lo, ops, vals, gateT, bonusT, WC):
    with ExitStack() as ctx:
        sb, ps, sems = opened(nc, ctx)
        w_hi = sb("c_whi", [P, DC, RC], F32R)
        w_lo = sb("c_wlo", [P, DC, RC], F32R)
        xh = sb("c_xh", [P, DC, TB + 2], F32R)
        xl = sb("c_xl", [P, DC, TB + 2], F32R)
        taps = sb("c_taps", [P, 3, FT])
        dirp = sb("c_dirp", [P, 2, 2, RT])
        chp = sb("c_chp", [P, 3, RT])
        wa_up = sb("c_wa", [P, 2, 2, RW])
        g_up = sb("c_gup", [P, RW])
        ones = sb("c_ones", [P, P])
        notfirst = sb("c_nf", [P, RT * TB])
        f = sb("c_f", [P, FT, TB])
        big = lambda n: sb("c_" + n, [P, RT, TB])
        nkk, kka, tmp, sg, aa, c, u, e, ei, bb, kd, kk2 = [big(n) for n in "nkk kka tmp sg aa c u e ei bb kd kdsum".split()]
        pP = [ps(f"c_pP{k}") for k in range(3)]
        pX = ctx.enter_context(nc.psum_tensor("c_pX", [P, RT, TB], F32))
        pY = ctx.enter_context(nc.psum_tensor("c_pY", [P, RT, TB], F32))
        s = sems("c_const c_par c_wraw c_whi c_wlo c_x c_xfree c_proj c_mid c_shift c_sq c_ss c_nrm c_th c_lora"
                 " c_sig c_scan c_v c_exp c_gate c_gs c_st c_bon c_p c_dch c_outfree c_wc c_bst c_kk c_kk2 c_cdve c_seen")
        block = ctx.enter_context(nc.Block())
        w_raw = f[:].rearrange("p a b -> p (a b)")[:, 0:RC]
        flat = lambda m: m[:].rearrange("p j t -> p (j t)")
        ch = lambda m: m[:].rearrange("p j (w t) -> p (j w) t", t=C)

        @block.sync
        def _(sp):
            col = lambda ap: ap.rearrange("(j p) -> p j", p=P)
            for k in range(3):
                sp.dma_start(taps[:, k, :], col(shift_taps[k]), allow_slow_non_contiguous=True).then_inc(s["c_par"], 16)
            for d in range(2):
                for k, v in enumerate((w0, a0)):
                    sp.dma_start(dirp[:, d, k, :], col(v[d]), allow_slow_non_contiguous=True).then_inc(s["c_par"], 16)
                sp.wait_ge(s["c_const"], 1)
                sp.dma_start(wa_up[0:64, d, 0, :], w_lora_up[d]).then_inc(s["c_par"], 16)
                sp.dma_start(wa_up[64:P, d, 1, :], a_lora_up[d]).then_inc(s["c_par"], 16)
            for k, v in enumerate((k_k, k_a, r_k)):
                sp.dma_start(chp[:, k, :], col(v), allow_slow_non_contiguous=True).then_inc(s["c_par"], 16)
            sp.dma_start(g_up[:], g_lora_up).then_inc(s["c_par"], 16)
            for m in range(DC):
                if m:
                    sp.wait_ge(s["c_wlo"], m)
                sp.dma_start(w_raw, w_in[m * P:(m + 1) * P, 0:RC]).then_inc(s["c_wraw"], 16)
            with sp.Fori(0, NB) as i:
                sp.wait_ge(s["c_xfree"], i + 1)
                sp.sem_inc(s["c_seen"], 1)
                for dst, src in ((xh, xT_hi), (xl, xT_lo)):
                    sp.dma_start(dst[:].bitcast(F32), src[:, :, bass.ds(TB * i + (i >> 3), TB + 2)].rearrange("c p t -> p c t")).then_inc(s["c_x"], 16)
                for k, o in ((0, gateT), (1, bonusT)):
                    sp.wait_ge(s["c_gs"], 2 * i + 1 + k)
                    sp.sem_inc(s["c_seen"], 1)
                    src = (tmp, kk2)[k]
                    sp.dma_start(o[:, :, bass.ds(TB * i, TB)].rearrange("j p t -> p j t"), src[:]).then_inc(s["c_bst"], 16)
            sp.wait_ge(s["c_bst"], 32 * NB)

        @block.gpsimd
        def _(pool):
            pool.memset(wa_up[:], 0.0).then_inc(s["c_const"], 1)
            for m in range(DC):
                pool.wait_ge(s["c_whi"], m + 1)
                pool.tensor_tensor(w_lo[:, m, :], w_raw, w_hi[:, m, :].bitcast(F32), ALU.subtract).then_inc(s["c_wlo"], 1)
            with pool.Fori(0, NB) as i:
                pool.wait_ge(s["c_shift"], FT * (i + 1) + 1)
                pool.tensor_tensor(kka[:], f[:, W_K:W_V, :], bc(chp[:, 1, :].rearrange("p (j o) -> p j o", o=1), [P, RT, TB]), ALU.mult).then_inc(s["c_p"], 1)
                for d in range(2):
                    n = 2 * i + d
                    pool.wait_ge(s["c_v"], 3 * n + 3)
                    pool.wait_ge(s["c_exp"], n + 1)
                    pool.tensor_tensor(c[:], kd[:], ei[:], ALU.mult)
                    pool.tensor_tensor(u[:], f[:, W_R:W_K, :], u[:], ALU.mult)
                    pool.tensor_tensor(e[:], nkk[:], e[:], ALU.mult)
                    pool.tensor_tensor(bb[:], bb[:], ei[:], ALU.mult).then_inc(s["c_p"], 1)
                    pool.wait_ge(s["c_p"], 3 * i + 2 + d)
                    for w in range(TB // C):
                        for k, m in enumerate((e, u, bb, c)):
                            pool.dma_start(ops[d, bass.ds((TB // C) * i + w, 1), :, k, :, :].rearrange("o p j t -> (o p) j t"),
                                           m[:, :, w * C:(w + 1) * C]).then_inc(s["c_st"], 16)
                        if d == 0:
                            pool.dma_start(vals[bass.ds((TB // C) * i + w, 1), :, :, :].rearrange("o p j t -> (o p) j t"),
                                           f[:, W_V:W_WA, w * C:(w + 1) * C]).then_inc(s["c_st"], 16)
            pool.wait_ge(s["c_st"], 16 * 36 * NB)

        @block.scalar
        def _(act):
            for m in range(DC):
                act.wait_ge(s["c_wraw"], 16 * (m + 1))
                act.activation(w_hi[:, m, :], w_raw, ACT.Copy).then_inc(s["c_whi"], 1)
            act.wait_ge(s["c_par"], 16 * 15)
            act.wait_ge(s["c_wlo"], DC)
            with act.Fori(0, NB) as i:
                act.wait_ge(s["c_outfree"], i + 1)
                for m in range(FT):
                    act.wait_ge(s["c_proj"], FT * i + m + 1)
                    act.activation(f[:, m, :], pP[m % 3][:, 1:TB + 1], ACT.Copy, scale=taps[:, 1, m:m + 1]).then_inc(s["c_mid"], 1)
                act.wait_ge(s["c_ss"], i + 1)
                act.activation(sg[:], pX[:], ACT.Sqrt).then_inc(s["c_nrm"], 1)
                act.wait_ge(s["c_shift"], FT * (i + 1) + 1)
                act.activation(f[0:64, W_WA, :], f[0:64, W_WA, :], ACT.Tanh)
                act.activation(f[:, W_G, :], f[:, W_G, :], ACT.Sigmoid).then_inc(s["c_th"], 1)
                act.wait_ge(s["c_kk"], i + 1)
                for d in range(2):
                    n = 2 * i + d
                    act.wait_ge(s["c_lora"], n + 1)
                    if d:
                        act.wait_ge(s["c_p"], 3 * i + 2)
                    for j in range(RT):
                        act.activation(sg[:, j, :], pX[:, j, :], ACT.Sigmoid, bias=dirp[:, d, 0, j:j + 1])
                    for j in range(RT):
                        last = act.activation(aa[:, j, :], pY[:, j, :], ACT.Sigmoid, bias=dirp[:, d, 1, j:j + 1])
                    last.then_inc(s["c_sig"], 1)
                    act.wait_ge(s["c_v"], 3 * n + 3)
                    act.activation(ei[:], u[:], ACT.Exp, scale=KAPPA)
                    act.wait_ge(s["c_scan"], n + 1)
                    act.activation(WC[:, d, bass.ds(i, 1), :], c[:].rearrange("p j (w t) -> p (j w) t", t=C)[:, :, C - 1:C].rearrange("p a o -> p o a"), ACT.Exp, scale=-KAPPA).then_inc(s["c_wc"], 1)
                    act.activation(e[:], e[:], ACT.Exp, scale=-KAPPA)
                    act.activation(u[:], u[:], ACT.Exp, scale=-KAPPA).then_inc(s["c_exp"], 1)
                act.wait_ge(s["c_gate"], i + 1)
                act.activation(tmp[:], pX[:], ACT.Copy).then_inc(s["c_gs"], 1)

        @block.vector
        def _(dve):
            for h in range(2):
                for g in range(2):
                    dve.memset(ones[h * HD:h * HD + HD, g * HD:g * HD + HD], float(h == g))
            dve.memset(notfirst[:].rearrange("p (w t) -> p w t", t=C)[:, :, 1:], 1.0)
            dve.memset(notfirst[:].rearrange("p (w t) -> p w t", t=C)[:, :, 0:1], 0.0).then_inc(s["c_cdve"], 1)
            dve.wait_ge(s["c_cdve"], 1)
            dve.wait_ge(s["c_par"], 16 * 15)
            dve.sem_inc(s["c_outfree"], 1)
            dve.sem_inc(s["c_shift"], 1)
            with dve.Fori(0, NB) as i:
                def step(k):
                    dve.wait_ge(s["c_dch"], DSTEPS * i + k)
                k = 0
                for m in range(FT):
                    dve.wait_ge(s["c_mid"], FT * i + m + 1)
                    dve.scalar_tensor_tensor(out=f[:, m, :], in0=pP[m % 3][:, 0:TB], scalar=taps[:, 0, m:m + 1], in1=f[:, m, :],
                                             op0=ALU.mult, op1=ALU.add).then_inc(s["c_dch"], 1)
                    k += 1
                    step(k)
                    dve.scalar_tensor_tensor(out=f[:, m, :], in0=pP[m % 3][:, 2:TB + 2], scalar=taps[:, 2, m:m + 1], in1=f[:, m, :],
                                             op0=ALU.mult, op1=ALU.add).then_inc(s["c_shift"], 1)
                dve.wait_ge(s["c_shift"], FT * (i + 1) + 1)
                dve.tensor_tensor(bb[:], f[:, W_K:W_V, :], bc(chp[:, 0, :].rearrange("p (j o) -> p j o", o=1), [P, RT, TB]), ALU.mult).then_inc(s["c_dch"], 1)
                k += 1
                step(k)
                dve.tensor_tensor(tmp[:], bb[:], bb[:], ALU.mult).then_inc(s["c_sq"], 1)
                dve.wait_ge(s["c_nrm"], i + 1)
                dve.tensor_scalar(sg[:], sg[:], 1e-12, None, ALU.max).then_inc(s["c_dch"], 1)
                k += 1
                step(k)
                dve.reciprocal(sg[:], sg[:]).then_inc(s["c_dch"], 1)
                k += 1
                step(k)
                dve.scalar_tensor_tensor(out=nkk[:], in0=bb[:], scalar=-1.0, in1=sg[:], op0=ALU.mult, op1=ALU.mult).then_inc(s["c_kk"], 1)
                for d in range(2):
                    n = 2 * i + d
                    dve.wait_ge(s["c_sig"], n + 1)
                    if d:
                        dve.wait_ge(s["c_st"], 16 * (36 * i + 20))
                    dve.tensor_tensor_scan(flat(c), notfirst[:], flat(sg), 0.0, ALU.mult, ALU.add).then_inc(s["c_dch"], 1)
                    k += 1
                    step(k)
                    if d == 0:
                        dve.tensor_tensor(e[:], c[:], sg[:], ALU.subtract)
                        dve.tensor_copy(u[:], c[:]).then_inc(s["c_v"], 1)
                    else:
                        dve.tensor_tensor(ch(e), bc(ch(c)[:, :, C - 1:C], [P, RT * TB // C, C]), ch(c), ALU.subtract).then_inc(s["c_dch"], 1)
                        k += 1
                        step(k)
                        dve.tensor_tensor(u[:], e[:], sg[:], ALU.add).then_inc(s["c_v"], 1)
                    dve.wait_ge(s["c_v"], 3 * n + 1)
                    dve.sem_inc(s["c_scan"], 1)
                    dve.scalar_tensor_tensor(out=bb[:], in0=nkk[:], scalar=-1.0, in1=aa[:], op0=ALU.mult, op1=ALU.mult).then_inc(s["c_v"], 1)
                    if d == 0:
                        dve.wait_ge(s["c_p"], 3 * i + 1)
                    dve.scalar_tensor_tensor(out=kd[:], in0=aa[:], scalar=-1.0, in1=kka[:], op0=ALU.add, op1=ALU.mult).then_inc(s["c_dch"], 1)
                    k += 1
                    step(k)
                    dve.tensor_tensor(kd[:], kd[:], f[:, W_K:W_V, :], ALU.add).then_inc(s["c_v"], 1)
                    dve.wait_ge(s["c_v"], 3 * n + 3)
                    if d == 0:
                        dve.tensor_copy(kk2[:], kd[:]).then_inc(s["c_dch"], 1)
                        dve.wait_ge(s["c_exp"], n + 1)
                        dve.wait_ge(s["c_wc"], 2 * i + 1)
                    else:
                        dve.tensor_tensor(kk2[:], kk2[:], kd[:], ALU.add).then_inc(s["c_dch"], 1)
                    k += 1
                    step(k)
                dve.tensor_tensor(kk2[:], kk2[:], f[:, W_R:W_K, :], ALU.mult).then_inc(s["c_dch"], 1)
                k += 1
                step(k)
                dve.scalar_tensor_tensor(out=kk2[:], in0=kk2[:], scalar=0.5, in1=bc(chp[:, 2, :].rearrange("p (j o) -> p j o", o=1), [P, RT, TB]),
                                         op0=ALU.mult, op1=ALU.mult).then_inc(s["c_kk2"], 1)
                dve.wait_ge(s["c_bon"], i + 1)
                dve.tensor_tensor(kk2[:], pY[:], f[:, W_V:W_WA, :], ALU.mult).then_inc(s["c_dch"], 1)
                k += 1
                dve.wait_ge(s["c_gs"], 2 * i + 1)
                step(k)
                dve.sem_inc(s["c_gs"], 1)
                assert k == DSTEPS
                dve.wait_ge(s["c_bst"], 32 * (i + 1))
                dve.wait_ge(s["c_st"], 16 * 36 * (i + 1))
                dve.sem_inc(s["c_outfree"], 1)

        @block.tensor
        def _(pe):
            pe.sem_inc(s["c_xfree"], 1)
            pe.wait_ge(s["c_wlo"], DC)
            pe.wait_ge(s["c_const"], 1)
            pe.wait_ge(s["c_cdve"], 1)
            pe.wait_ge(s["c_par"], 16 * 15)
            with pe.Fori(0, NB) as i:
                pe.wait_ge(s["c_x"], 32 * (i + 1))
                for m in range(FT):
                    if m < 3:
                        pe.wait_ge(s["c_shift"], FT * i + 1)
                    else:
                        pe.wait_ge(s["c_shift"], FT * i + m - 1)
                    for q in range(DC):
                        for k, (w, x) in enumerate(((w_hi, xh), (w_hi, xl), (w_lo, xh))):
                            mm = pe.matmul(pP[m % 3][:, 0:TB + 2], w[:, q, m * P:(m + 1) * P], x[:, q, :], start=(q == 0 and k == 0),
                                           stop=(q == DC - 1 and k == 2))
                    mm.then_inc(s["c_proj"], 1)
                pe.wait_ge(s["c_proj"], FT * (i + 1))
                pe.sem_inc(s["c_xfree"], 1)
                pe.wait_ge(s["c_sq"], i + 1)
                for j in range(RT):
                    mm = pe.matmul(pX[:, j, :], ones[:], tmp[:, j, :], start=True, stop=True)
                mm.then_inc(s["c_ss"], 1)
                pe.wait_ge(s["c_th"], i + 1)
                for d in range(2):
                    if d:
                        pe.wait_ge(s["c_sig"], 2 * i + 1)
                    for k, o in enumerate((pX, pY)):
                        for j in range(RT):
                            mm = pe.matmul(o[:, j, :], wa_up[:, d, k, j * P:(j + 1) * P], f[:, W_WA, :], start=True, stop=True)
                    mm.then_inc(s["c_lora"], 1)
                pe.wait_ge(s["c_sig"], 2 * i + 2)
                for j in range(RT):
                    mm = pe.matmul(pX[:, j, :], g_up[:, j * P:(j + 1) * P], f[:, W_G, :], start=True, stop=True)
                mm.then_inc(s["c_gate"], 1)
                pe.wait_ge(s["c_kk2"], i + 1)
                for j in range(RT):
                    mm = pe.matmul(pY[:, j, :], ones[:], kk2[:, j, :], start=True, stop=True)
                mm.then_inc(s["c_bon"], 1)


DSTEPS = FT + 3 + 2 + 1 + 2 + 2 + 2


LEVELS = [2, 4, 8, 16, 32]
NL = len(LEVELS)
OP_A, OP_R, OP_B, OP_K, OP_V = range(5)


def recurrence(nc, ops, vals, WC, yT):
    with ExitStack() as ctx:
        sb, ps, sems = opened(nc, ctx)
        ident = sb("d_id", [P, 1, P])
        strict = sb("d_strict", [P, 2, P])
        upto = sb("d_upto", [P, 2, P])
        beside = sb("d_beside", [P, 2, NL + 1, P])
        decay = sb("d_decay", [P, 2, NCH, RT])
        bd = sb("d_bd", [P, 2, 2, 5, RT, P])
        mat = lambda n: [sb(f"d_{n}{g}", [P, RT, P]) for g in range(2)]
        bm, ak, rb, rk, tb, tk, tv, zz, yy, pm, zs, uu, st, tmp = [mat(n) for n in "bm ak rb rk tb tk tv zz yy pm zs uu st tmp".split()]
        y_out = sb("d_yo", [P, 2, 2, RT, C])
        bank = [[ps(f"d_p{g}{k}") for k in range(4)] for g in range(2)]
        s = sems("d_m d_dm d_ld00 d_ld01 d_ld10 d_ld11 d_ab d_rest d_bm d_craw d_mask d_ta d_tt d_tc d_init d_dch d_P d_Pe d_ZY d_ZYe d_zs d_zsc"
                 " d_u d_uc d_yo d_ye d_sn d_S d_tmp d_yst00 d_yst01 d_yst10 d_yst11 d_z d_seen")
        block = ctx.enter_context(nc.Block())
        q4 = lambda m: m[:].rearrange("p (j t) -> p j t", j=RT)
        b4 = lambda m: bc(m, [P, RT, P])
        pcs = [(0, 0), (64, 64)]

        @block.sync
        def _(sp):
            sp.wait_ge(s["d_z"], 1)
            with sp.Fori(0, NCH // 2) as i:
                for par in range(2):
                    n = 2 * i + par
                    for g in range(2):
                        w = n if g == 0 else NCH - 1 - n
                        sp.wait_ge(s["d_S"], 2 * n + g + 1)
                        sp.sem_inc(s["d_seen"], 1)
                        for h in range(2):
                            r = slice(h * HD, (h + 1) * HD)
                            sp.dma_start(bd[r, par, g, 0:4, :, r].rearrange("p k j t -> p (k j) t"), ops[g, bass.ds(w, 1), r, :, :, :].rearrange("o p k j t -> (o p) (k j) t"))\
                              .then_inc(s[f"d_ld{par}{g}"], 16)
                            sp.dma_start(bd[r, par, g, OP_V, :, r], vals[bass.ds(w, 1), r, :, :].rearrange("o p j t -> (o p) j t"))\
                              .then_inc(s[f"d_ld{par}{g}"], 16)

        @block.gpsimd
        def _(pool):
            identity(nc, pool, ident[:, 0, :], s["d_m"])
            k = 2
            for d in range(2):
                for tile, op in ((strict[:, d, :], ALU.is_gt), (upto[:, d, :], ALU.is_ge)):
                    pool.memset(tile, 1.0).then_inc(s["d_m"], 1)
                    k += 1
                    pool.wait_ge(s["d_m"], k)
                    sg = 1 - 2 * d
                    pool.affine_select(out=tile, in_=tile, compare_op=op, fill=0.0, base=0, pattern=[[sg, P]], channel_multiplier=-sg).then_inc(s["d_m"], 1)
                    k += 1
                for l, m in enumerate([1] + LEVELS):
                    tile = beside[:, d, l, :].rearrange("p (b x s) -> p b x s", x=2, s=m)
                    for x in range(2):
                        pool.memset(tile[:, :, x, :], float(x == d)).then_inc(s["d_m"], 1)
                        k += 1
                        pool.wait_ge(s["d_m"], k)
                    lo = m * (1 - d)
                    flat = beside[:, d, l, :]
                    for base, sg in ((-lo, 1), (lo + m - 1, -1)):
                        pool.affine_select(out=flat, in_=flat, compare_op=ALU.is_ge, fill=0.0, base=base,
                                           pattern=[[-sg * 2 * m, P // (2 * m)], [0, 2 * m]], channel_multiplier=sg).then_inc(s["d_m"], 1)
                        k += 1
                        pool.wait_ge(s["d_m"], k)
            pool.wait_ge(s["d_m"], k)
            pool.engine_nop().then_inc(s["d_dm"], 1)
            with pool.Fori(0, NCH) as n:
                for g in range(2):
                    pool.wait_ge(s["d_craw"], 2 * n + g + 1)
                    for m, k in ((ak, strict), (rb, upto), (rk, upto)):
                        last = pool.tensor_tensor(m[g][:], m[g][:], b4(k[:, g:g + 1, :]), ALU.mult)
                    last.then_inc(s["d_mask"], 1)

        @block.scalar
        def _(act):
            for k in ("00", "01", "10", "11"):
                act.sem_inc(s["d_yst" + k], 16)
            act.sem_inc(s["d_ye"], 2)
            with act.Fori(0, NCH // 2) as i:
                for par in range(2):
                    n = 2 * i + par
                    for g in range(2):
                        act.wait_ge(s["d_rest"], 2 * n + g + 1)
                        for k, m in ((1, rb), (2, ak), (3, rk)):
                            last = act.activation(m[g][:], q4(bank[g][k]), ACT.Copy)
                        last.then_inc(s["d_craw"], 1)
                    for g in range(2):
                        act.wait_ge(s["d_tt"], 2 * n + g + 1)
                        for k, m in ((1, tb), (2, tk), (3, tv)):
                            last = act.activation(m[g][:], q4(bank[g][k]), ACT.Copy)
                        last.then_inc(s["d_tc"], 1)
                    for g in range(2):
                        act.wait_ge(s["d_zs"], 2 * n + g + 1)
                        act.activation(zs[g][:], q4(bank[g][3]), ACT.Copy).then_inc(s["d_zsc"], 1)
                    for g in range(2):
                        act.wait_ge(s["d_u"], 2 * n + g + 1)
                        act.activation(uu[g][:], q4(bank[g][0]), ACT.Copy).then_inc(s["d_uc"], 1)
                    for g in range(2):
                        act.wait_ge(s["d_yo"], 2 * n + g + 1)
                        act.wait_ge(s[f"d_yst{par}{g}"], 16 * (i + 1))
                        for h in range(2):
                            r = slice(h * HD, (h + 1) * HD)
                            last = act.activation(y_out[r, par, g, :, :], q4(bank[g][1])[r, :, r], ACT.Copy)
                        last.then_inc(s["d_ye"], 1)
                        act.wait_ge(s["d_ye"], 2 * n + g + 3)
                        w = n if g == 0 else NCH - 1 - n
                        act.dma_start(yT[g, :, :, bass.ds(C * w, C)].rearrange("j p t -> p j t"), y_out[:, par, g, :, :]).then_inc(s[f"d_yst{par}{g}"], 16)
            for k in ("00", "01", "10", "11"):
                act.wait_ge(s["d_yst" + k], 16 * (NCH // 2 + 1))

        @block.vector
        def _(dve):
            dve.memset(bd[:].rearrange("p a b c d e -> p (a b c d e)"), 0.0)
            for g in range(2):
                dve.memset(st[g][:], 0.0)
            for d in range(2):
                last = dve.tensor_copy(decay[:, d, :, :].rearrange("p (b w) j -> p b w j", w=TB // C), WC[:, d, :, :].rearrange("p b (j w) -> p b w j", w=TB // C))
            last.then_inc(s["d_z"], 1)
            dve.wait_ge(s["d_z"], 1)
            for d, w in ((0, NS // C - 1), (1, NS // C)):
                last = dve.memset(decay[:, d, w, :], 0.0)
            last.then_inc(s["d_z"], 1)
            dve.wait_ge(s["d_z"], 2)
            dve.sem_inc(s["d_S"], 4)
            dve.wait_ge(s["d_dm"], 1)
            with dve.Fori(0, NCH) as n:
                for g in range(2):
                    dve.wait_ge(s["d_ab"], 2 * n + g + 1)
                    dve.tensor_tensor(bm[g][:], q4(bank[g][0]), b4(strict[:, g:g + 1, :]), ALU.mult).then_inc(s["d_bm"], 1)
                for g in range(2):
                    dve.wait_ge(s["d_bm"], 2 * n + g + 1)
                    dve.tensor_tensor(yy[g][:], bm[g][:], b4(beside[:, 1 - g, 0:1, :]), ALU.mult)
                    dve.wait_ge(s["d_ta"], 2 * n + g + 1)
                    dve.tensor_tensor(zz[g][:], q4(bank[g][0]), b4(beside[:, g, 0:1, :]), ALU.mult).then_inc(s["d_dch"], 1)
                    dve.wait_ge(s["d_dch"], 2 * n + g + 1)
                    dve.tensor_tensor(yy[g][:], yy[g][:], b4(ident[:]), ALU.add)
                    dve.tensor_tensor(zz[g][:], zz[g][:], b4(ident[:]), ALU.add).then_inc(s["d_init"], 1)
                dve.wait_ge(s["d_init"], 2 * n + 2)
                for l in range(NL):
                    for g in range(2):
                        dve.wait_ge(s["d_P"], 2 * NL * n + 2 * l + g + 1)
                        dve.tensor_tensor(pm[g][:], q4(bank[g][0]), b4(beside[:, g, l + 1:l + 2, :]), ALU.mult).then_inc(s["d_Pe"], 1)
                    for g in range(2):
                        dve.wait_ge(s["d_ZY"], 2 * NL * n + 2 * l + g + 1)
                        if l < NL - 1:
                            dve.tensor_tensor(zz[g][:], zz[g][:], q4(bank[g][1]), ALU.add)
                        dve.tensor_tensor(yy[g][:], yy[g][:], q4(bank[g][2]), ALU.add).then_inc(s["d_ZYe"], 1)
                for g in range(2):
                    dve.wait_ge(s["d_sn"], 2 * n + g + 1)
                    dve.tensor_tensor(tmp[g][:], st[g][:], q4(bank[g][2]), ALU.add).then_inc(s["d_tmp"], 1)
                    dve.wait_ge(s["d_tmp"], 2 * n + g + 1)
                    w = n if g == 0 else NCH - 1 - n
                    dve.sem_inc(s["d_seen"], 1)
                    dve.tensor_tensor(st[g][:], tmp[g][:], bc(decay[:, g, bass.ds(w, 1), :].rearrange("p o j -> p j o"), [P, RT, P]), ALU.mult).then_inc(s["d_S"], 1)

        @block.tensor
        def _(pe):
            pe.wait_ge(s["d_z"], 1)
            pe.wait_ge(s["d_dm"], 1)
            with pe.Fori(0, NCH // 2) as i:
                for par in range(2):
                    n = 2 * i + par
                    ln = 2 * NL * n
                    op = [[bd[:, par, g, k, :, :] for k in range(5)] for g in range(2)]

                    def products(g, to, pairs):
                        for j in range(RT):
                            for k, (l, r) in enumerate(pairs):
                                mm = pe.matmul(bank[g][to][:, j * P:(j + 1) * P], l[:, j, :], r[:, j, :], start=(k == 0), stop=(k == len(pairs) - 1))
                        return mm

                    def turned(g, to, a):
                        for j in range(RT):
                            mm = pe.transpose(bank[g][to][:, j * P:(j + 1) * P], a[:, j, :], ident[:, 0, :])
                        return mm

                    for g in range(2):
                        pe.wait_ge(s[f"d_ld{par}{g}"], 64 * (i + 1))
                        pe.wait_ge(s["d_ye"], 2 * n + g + 1)
                        pe.wait_ge(s["d_S"], 2 * n + g + 3)
                        products(g, 0, [(op[g][OP_B], op[g][OP_A])]).then_inc(s["d_ab"], 1)
                        products(g, 1, [(op[g][OP_B], op[g][OP_R])])
                        products(g, 2, [(op[g][OP_K], op[g][OP_A])])
                        products(g, 3, [(op[g][OP_K], op[g][OP_R])]).then_inc(s["d_rest"], 1)
                    for g in range(2):
                        pe.wait_ge(s["d_bm"], 2 * n + g + 1)
                        turned(g, 0, bm[g]).then_inc(s["d_ta"], 1)
                        pe.wait_ge(s["d_craw"], 2 * n + g + 1)
                        turned(g, 1, op[g][OP_B])
                        turned(g, 2, op[g][OP_K])
                        turned(g, 3, op[g][OP_V]).then_inc(s["d_tt"], 1)
                    for g in range(2):
                        pe.wait_ge(s["d_tc"], 2 * n + g + 1)
                        pe.wait_ge(s["d_mask"], 2 * n + g + 1)
                        products(g, 3, [(op[g][OP_A], st[g]), (ak[g], tv[g])]).then_inc(s["d_zs"], 1)
                    for l in range(NL):
                        for g in range(2):
                            if l == 0:
                                pe.wait_ge(s["d_init"], 2 * n + g + 1)
                            else:
                                pe.wait_ge(s["d_ZYe"], ln + 2 * (l - 1) + g + 1)
                            products(g, 0, [(bm[g], zz[g])]).then_inc(s["d_P"], 1)
                        for g in range(2):
                            pe.wait_ge(s["d_Pe"], ln + 2 * l + g + 1)
                            if l < NL - 1:
                                products(g, 1, [(yy[g], pm[g])])
                            products(g, 2, [(pm[g], yy[g])]).then_inc(s["d_ZY"], 1)
                    for g in range(2):
                        pe.wait_ge(s["d_ZYe"], ln + 2 * (NL - 1) + g + 1)
                        pe.wait_ge(s["d_zsc"], 2 * n + g + 1)
                        products(g, 0, [(yy[g], zs[g])]).then_inc(s["d_u"], 1)
                    for g in range(2):
                        pe.wait_ge(s["d_uc"], 2 * n + g + 1)
                        products(g, 1, [(st[g], op[g][OP_R]), (uu[g], rb[g]), (tv[g], rk[g])]).then_inc(s["d_yo"], 1)
                        products(g, 2, [(tb[g], uu[g]), (tk[g], tv[g])]).then_inc(s["d_sn"], 1)


NE = 16
GN_EPS = 64e-5


def mix_and_route(nc, x, w_out, ln_g, ln_b, norm2, w_router, yT, gateT, bonusT, mixT, out, hn_rows, logits):
    with ExitStack() as ctx:
        sb, ps, sems = opened(nc, ctx)
        w_raw = sb("e_wraw", [P, D])
        w_hi = sb("e_whi", [P, DC, D], F32R)
        w_lo = sb("e_wlo", [P, DC, D], F32R)
        gain = sb("e_gain", [P, D])
        wr = sb("e_wr", [P, DC, NE])
        ln = sb("e_ln", [P, 2, RT])
        eps = sb("e_eps", [P, 2])
        ident = sb("e_id", [P, P])
        mean1 = sb("e_mean1", [P, P])
        y2 = sb("e_y2", [P, 2, 2, RT, P])
        gb = sb("e_gb", [P, 2, 2, RT, P])
        at = sb("e_at", [P, 2, RT, P])
        x_in = sb("e_x", [P, 2, D])
        y = sb("e_y", [P, RT, P])
        dv = sb("e_dv", [P, RT, P])
        sq = sb("e_sq", [P, RT, P])
        sdv = sb("e_sdv", [P, RT, P])
        rw = sb("e_rw", [P, RT, P])
        mh = sb("e_mh", [P, DC, P], F32R)
        ml = sb("e_ml", [P, DC, P], F32R)
        h = sb("e_h", [P, 2, D])
        junk = sb("e_junk", [P, D])
        sm = sb("e_sm", [P, 4])
        hn = sb("e_hn", [P, 2, D])
        hT = sb("e_hT", [P, DC, P])
        lt = sb("e_lt", [P, P])
        pM = ps("e_pM")
        pV = ps("e_pV")
        pO = [ps(f"e_pO{k}") for k in range(2)]
        pT = [ps(f"e_pT{k}") for k in range(2)]
        pL = ps("e_pL")
        pR = ps("e_pR")
        s = sems("e_par e_cst e_wr e_hi e_lo e_ld0 e_ld1 e_free e_y e_mean e_dv e_sq e_var e_sd e_d1 e_d2 e_d3 e_d4 e_d5 e_rw e_mh e_ml e_ah e_al"
                 " e_o e_h e_ss e_sd2 e_rs e_hn e_st0 e_st1 e_tr e_hT e_lg e_lt e_lt2 e_lout e_mid e_mc")
        block = ctx.enter_context(nc.Block())
        flat = lambda m: m.rearrange("p j t -> p (j t)")
        pj = lambda k: bc(ln[:, k, :].rearrange("p (j o) -> p j o", o=1), [P, RT, P])

        @block.sync
        def _(sp):
            sp.dma_start(gain[:], norm2.partition_broadcast(P)).then_inc(s["e_par"], 16)
            sp.dma_start(wr[:], w_router.rearrange("(c p) e -> p c e", p=P)).then_inc(s["e_par"], 16)
            for k, v in enumerate((ln_g, ln_b)):
                sp.dma_start(ln[:, k, :], v.rearrange("(j p) -> p j", p=P), allow_slow_non_contiguous=True).then_inc(s["e_par"], 16)
            for c in range(DC):
                if c:
                    sp.wait_ge(s["e_lo"], c)
                sp.dma_start(w_raw[:], w_out[c * P:(c + 1) * P, :]).then_inc(s["e_wr"], 16)
            with sp.Fori(0, NT // 2) as i:
                for b in range(2):
                    t = 2 * i + b
                    sp.wait_ge(s["e_free"], t + 1)
                    sp.sem_inc(s["e_mid"], 1)
                    tok = bass.ds(t * P, P)
                    ld = s[f"e_ld{b}"]
                    for d in range(2):
                        sp.dma_start(y2[:, b, d, :, :], yT[d, :, :, tok].rearrange("j p t -> p j t")).then_inc(ld, 16)
                    for k, v in enumerate((gateT, bonusT)):
                        sp.dma_start(gb[:, b, k, :, :], v[:, :, tok].rearrange("j p t -> p j t")).then_inc(ld, 16)
                    sp.dma_start(at[:, b, :, :], mixT[RW:, tok].rearrange("(j p) t -> p j t", p=P)).then_inc(ld, 16)
                    sp.dma_start(x_in[:, b, :], x[tok, :]).then_inc(ld, 16)

        @block.gpsimd
        def _(pool):
            pool.memset(eps[:, 0:1], EPS).then_inc(s["e_cst"], 1)
            pool.memset(eps[:, 1:2], GN_EPS).then_inc(s["e_cst"], 1)
            identity(nc, pool, ident[:], s["e_mc"])
            for c in range(DC):
                pool.wait_ge(s["e_hi"], c + 1)
                pool.tensor_tensor(w_lo[:, c, :], w_raw[:], w_hi[:, c, :].bitcast(F32), ALU.subtract).then_inc(s["e_lo"], 1)
            with pool.Fori(0, NT // 2) as i:
                for b in range(2):
                    t = 2 * i + b
                    pool.wait_ge(s[f"e_ld{b}"], 96 * (i + 1))
                    pool.tensor_tensor(y[:], y2[:, b, 0, :, :], y2[:, b, 1, :, :], ALU.add).then_inc(s["e_y"], 1)
                    pool.wait_ge(s["e_dv"], t + 1)
                    pool.tensor_tensor(sq[:], dv[:], dv[:], ALU.mult).then_inc(s["e_sq"], 1)
                    pool.wait_ge(s["e_ah"], t + 1)
                    pool.tensor_tensor(ml[:, RT:, :], at[:, b, :, :], mh[:, RT:, :].bitcast(F32), ALU.subtract).then_inc(s["e_al"], 1)

        @block.scalar
        def _(act):
            for c in range(DC):
                act.wait_ge(s["e_wr"], 16 * (c + 1))
                act.activation(w_hi[:, c, :], w_raw[:], ACT.Copy).then_inc(s["e_hi"], 1)
            act.wait_ge(s["e_cst"], 2)
            act.wait_ge(s["e_d5"], 1)
            for b in range(2):
                act.sem_inc(s[f"e_st{b}"], 32)
            with act.Fori(0, NT // 2) as i:
                for b in range(2):
                    t = 2 * i + b
                    act.wait_ge(s[f"e_ld{b}"], 96 * (i + 1))
                    act.activation(mh[:, RT:, :], at[:, b, :, :], ACT.Copy).then_inc(s["e_ah"], 1)
                    act.wait_ge(s["e_var"], t + 1)
                    act.activation(flat(sdv[:]), pV[:], ACT.Sqrt, bias=eps[:, 1:2]).then_inc(s["e_sd"], 1)
                    act.wait_ge(s["e_rw"], t + 1)
                    act.activation(mh[:, 0:RT, :], rw[:], ACT.Copy).then_inc(s["e_mh"], 1)
                    act.wait_ge(s["e_h"], t + 1)
                    act.activation(junk[:], h[:, b, :], ACT.Square, accum_out=sm[:, 0:1]).then_inc(s["e_ss"], 1)
                    act.wait_ge(s["e_ss"], t + 1)
                    act.activation(sm[:, 1:2], sm[:, 0:1], ACT.Sqrt, bias=eps[:, 0:1], scale=1.0 / D).then_inc(s["e_sd2"], 1)
                    act.wait_ge(s["e_hn"], t + 1)
                    tok = bass.ds(t * P, P)
                    act.dma_start(out[tok, :], h[:, b, :]).then_inc(s[f"e_st{b}"], 16)
                    act.dma_start(hn_rows[tok, :], hn[:, b, :]).then_inc(s[f"e_st{b}"], 16)
                    act.wait_ge(s["e_tr"], t + 1)
                    for k in range(2):
                        last = act.activation(hT[:, 4 * k:4 * k + 4, :], pT[k][:].rearrange("p (c t) -> p c t", c=4), ACT.Copy)
                    last.then_inc(s["e_hT"], 1)
                    act.wait_ge(s["e_lg"], t + 1)
                    act.activation(lt[0:NE, :], pL[0:NE, 0:P], ACT.Copy).then_inc(s["e_lt"], 1)
            for b in range(2):
                act.wait_ge(s[f"e_st{b}"], 32 * (NT // 2 + 1))

        @block.vector
        def _(dve):
            for a in range(2):
                for g in range(2):
                    last = dve.memset(mean1[a * HD:a * HD + HD, g * HD:g * HD + HD], (a == g) / HD)
            dve.memset(lt[:], 0.0)
            last = dve.memset(sm[:], 0.0)
            last.then_inc(s["e_d5"], 1)
            dve.sem_inc(s["e_free"], 2)
            dve.wait_ge(s["e_par"], 64)
            with dve.Fori(0, NT // 2) as i:
                for b in range(2):
                    t = 2 * i + b
                    dve.wait_ge(s["e_mean"], t + 1)
                    dve.tensor_tensor(flat(dv[:]), flat(y[:]), pM[:], ALU.subtract).then_inc(s["e_dv"], 1)
                    dve.wait_ge(s["e_sd"], t + 1)
                    dve.reciprocal(sdv[:], sdv[:]).then_inc(s["e_d1"], 1)
                    dve.wait_ge(s["e_d1"], t + 1)
                    dve.tensor_tensor(rw[:], dv[:], sdv[:], ALU.mult).then_inc(s["e_d2"], 1)
                    dve.wait_ge(s["e_d2"], 4 * t + 1)
                    dve.tensor_tensor(rw[:], rw[:], pj(0), ALU.mult).then_inc(s["e_d2"], 1)
                    dve.wait_ge(s["e_d2"], 4 * t + 2)
                    dve.tensor_tensor(rw[:], rw[:], pj(1), ALU.add).then_inc(s["e_d2"], 1)
                    dve.wait_ge(s["e_d2"], 4 * t + 3)
                    dve.tensor_tensor(rw[:], rw[:], gb[:, b, 1, :, :], ALU.add).then_inc(s["e_d2"], 1)
                    dve.wait_ge(s["e_d2"], 4 * t + 4)
                    dve.tensor_tensor(rw[:], rw[:], gb[:, b, 0, :, :], ALU.mult).then_inc(s["e_rw"], 1)
                    dve.wait_ge(s["e_rw"], t + 1)
                    dve.wait_ge(s["e_mh"], t + 1)
                    dve.tensor_tensor(ml[:, 0:RT, :], rw[:], mh[:, 0:RT, :].bitcast(F32), ALU.subtract).then_inc(s["e_ml"], 1)
                    dve.wait_ge(s["e_o"], t + 1)
                    dve.wait_ge(s[f"e_st{b}"], 32 * (i + 1))
                    for k in range(2):
                        last = dve.tensor_tensor(h[:, b, k * 512:(k + 1) * 512], x_in[:, b, k * 512:(k + 1) * 512], pO[k][:], ALU.add)
                    last.then_inc(s["e_h"], 1)
                    dve.wait_ge(s["e_sd2"], t + 1)
                    dve.wait_ge(s["e_al"], t + 1)
                    dve.sem_inc(s["e_free"], 1)
                    dve.reciprocal(sm[:, 2:3], sm[:, 1:2]).then_inc(s["e_rs"], 1)
                    dve.wait_ge(s["e_rs"], t + 1)
                    dve.scalar_tensor_tensor(out=hn[:, b, :], in0=h[:, b, :], scalar=sm[:, 2:3], in1=gain[:], op0=ALU.mult, op1=ALU.mult)\
                       .then_inc(s["e_hn"], 1)
                    dve.wait_ge(s["e_lt2"], t + 1)
                    dve.tensor_copy(logits[:, bass.ds(t, 1), :], pR[:, 0:NE].rearrange("p (o e) -> p o e", o=1)).then_inc(s["e_lout"], 1)

        @block.tensor
        def _(pe):
            pe.wait_ge(s["e_d5"], 1)
            pe.wait_ge(s["e_mc"], 2)
            pe.wait_ge(s["e_lo"], DC)
            pe.wait_ge(s["e_par"], 64)
            with pe.Fori(0, NT // 2) as i:
                for b in range(2):
                    t = 2 * i + b
                    pe.wait_ge(s["e_y"], t + 1)
                    pe.matmul(pM[:], mean1[:], flat(y[:]), start=True, stop=True).then_inc(s["e_mean"], 1)
                    pe.wait_ge(s["e_sq"], t + 1)
                    pe.matmul(pV[:], mean1[:], flat(sq[:]), start=True, stop=True).then_inc(s["e_var"], 1)
                    pe.wait_ge(s["e_ml"], t + 1)
                    pe.wait_ge(s["e_al"], t + 1)
                    for k in range(2):
                        for c in range(DC):
                            for q, (l, r) in enumerate(((mh, w_hi), (mh, w_lo), (ml, w_hi))):
                                mm = pe.matmul(pO[k][:], l[:, c, :], r[:, c, k * 512:(k + 1) * 512], start=(c == 0 and q == 0), stop=(c == DC - 1 and q == 2))
                    mm.then_inc(s["e_o"], 1)
                    pe.wait_ge(s["e_hn"], t + 1)
                    for c in range(DC):
                        mm = pe.transpose(pT[c // 4][:, (c % 4) * P:(c % 4 + 1) * P], hn[:, b, c * P:(c + 1) * P], ident[:])
                    mm.then_inc(s["e_tr"], 1)
                    pe.wait_ge(s["e_hT"], t + 1)
                    for c in range(DC):
                        mm = pe.matmul(pL[0:NE, 0:P], wr[:, c, :], hT[:, c, :], start=(c == 0), stop=(c == DC - 1))
                    mm.then_inc(s["e_lg"], 1)
                    pe.wait_ge(s["e_lt"], t + 1)
                    pe.transpose(pR[:, 0:P], lt[:], ident[:]).then_inc(s["e_lt2"], 1)


F = 1024
CAP_S, CAP_P = 2 * NS // NE, 2 * NP_ // NE
CAP = CAP_S + CAP_P
TS, TP = NS // P, NP_ // P
G2 = 2 * NE
BITS = 30
FAR = 4096.0


def choose(nc, logits, aff_rows, index):
    with ExitStack() as ctx:
        sb, ps, sems = opened(nc, ctx)
        aff = sb("f_aff", [P, NT, NE])
        mxv = sb("f_mx", [P, NT])
        den = sb("f_den", [P, NT])
        A = sb("f_A", [P, G2, TS])
        cmp_ = sb("f_cmp", [P, G2, TS])
        cnt = sb("f_cnt", [P, G2])
        cap = sb("f_cap", [P, G2])
        low = sb("f_low", [P, G2], I32)
        cand = sb("f_cand", [P, G2], I32)
        bit = sb("f_bit", [P, 2], I32)
        bits = sb("f_bits", [P, G2], I32)
        ge = sb("f_ge", [P, G2])
        mask = sb("f_mask", [P, G2], I32)
        onesf = sb("f_ones", [P, P])
        onesb = sb("f_onesb", [P, P], BF16)
        before = sb("f_before", [P, P], BF16)
        beforef = sb("f_beforef", [P, P])
        notfirst = sb("f_nf", [P, G2 * TS])
        selb = sb("f_selb", [P, G2, TS], BF16)
        cum = sb("f_cum", [P, G2, TS])
        cumb = sb("f_cumb", [P, G2, TS], BF16)
        gt = sb("f_gt", [P, G2, TS])
        eq = sb("f_eq", [P, G2, TS])
        need = sb("f_need", [P, G2])
        pos = sb("f_pos", [P, G2, TS])
        iota_i = sb("f_iota", [P, CAP_S], I32)
        slots = sb("f_slots", [P, CAP_S], BF16)
        ids_i = sb("f_idsi", [P, NT, 2], I32)
        ids = sb("f_ids", [P, NT, 2], BF16)
        hot = sb("f_hot", [P, 2, TS + TP, CAP_S], BF16)
        two = sb("f_two", [P, 3, 2])
        idf = sb("f_idf", [P, 3])
        pC = ps("f_pC")
        pP = ps("f_pP")
        pI = [ps(f"f_pI{k}") for k in range(3)]
        s = sems("f_c f_v f_mx f_sub f_exp f_count f_cnt f_pre f_pos f_hot f_id f_idv f_st f_hused f_idd")
        block = ctx.enter_context(nc.Block())
        g3 = lambda m: bc(m.rearrange("p (g o) -> p g o", o=1), [P, G2, TS])
        fl = lambda m: m[:].rearrange("p g t -> p (g t)")

        @block.gpsimd
        def _(pool):
            pool.iota(iota_i[:], pattern=[[1, CAP_S]], base=0, channel_multiplier=0).then_inc(s["f_c"], 1)
            pool.iota(ids_i[:, :, 0:1], pattern=[[1, NT], [0, 1]], base=0, channel_multiplier=0).then_inc(s["f_c"], 1)
            pool.iota(ids_i[:, :, 1:2], pattern=[[0, NT], [0, 1]], base=0, channel_multiplier=1).then_inc(s["f_c"], 1)
            pool.memset(beforef[:], 1.0).then_inc(s["f_c"], 1)
            pool.wait_ge(s["f_c"], 4)
            pool.affine_select(out=beforef[:], in_=beforef[:], compare_op=ALU.is_gt, fill=0.0, base=0, pattern=[[1, P]], channel_multiplier=-1).then_inc(s["f_c"], 1)

        @block.sync
        def _(sp):
            sp.wait_ge(s["f_sub"], 2)
            sp.dma_start(aff_rows.rearrange("(t p) e -> p t e", p=P), aff[:]).then_inc(s["f_st"], 16)
            sp.wait_ge(s["f_st"], 16)

        @block.scalar
        def _(act):
            act.wait_ge(s["f_sub"], 1)
            act.activation(aff[:], aff[:], ACT.Exp).then_inc(s["f_exp"], 1)

        @block.vector
        def _(dve):
            v = 0

            def did(ins):
                nonlocal v
                v += 1
                ins.then_inc(s["f_v"], 1)
                dve.wait_ge(s["f_v"], v)

            dve.memset(cap[:, 0:NE], float(CAP_S))
            dve.memset(cap[:, NE:], float(CAP_P))
            dve.memset(onesf[:], 1.0)
            dve.memset(low[:], 0)
            dve.memset(bit[:], 1 << (BITS - 1))
            dve.memset(two[:], 0.0)
            dve.memset(notfirst[:].rearrange("p (g t) -> p g t", t=TS)[:, :, 1:], 1.0)
            dve.memset(notfirst[:].rearrange("p (g t) -> p g t", t=TS)[:, :, 0:1], 0.0)
            did(dve.memset(A[:, NE:, TP:], -1.0))
            dve.tensor_copy(onesb[:], onesf[:])
            dve.wait_ge(s["f_c"], 5)
            dve.tensor_copy(before[:], beforef[:])
            dve.tensor_copy(slots[:], iota_i[:])
            dve.tensor_copy(ids[:], ids_i[:])
            did(dve.tensor_reduce(mxv[:], logits[:], AX.X, ALU.max))
            dve.tensor_tensor(aff[:], logits[:], bc(mxv[:].rearrange("p (t o) -> p t o", o=1), [P, NT, NE]), ALU.subtract).then_inc(s["f_sub"], 1)
            dve.wait_ge(s["f_exp"], 1)
            did(dve.tensor_reduce(den[:], aff[:], AX.X, ALU.add))
            did(dve.reciprocal(den[:], den[:]))
            dve.tensor_tensor(aff[:], aff[:], bc(den[:].rearrange("p (t o) -> p t o", o=1), [P, NT, NE]), ALU.mult).then_inc(s["f_sub"], 1)
            dve.wait_ge(s["f_sub"], 2)
            dve.tensor_copy(A[:, 0:NE, :], aff[:, 0:TS, :].rearrange("p t e -> p e t"))
            did(dve.tensor_copy(A[:, NE:, 0:TP], aff[:, TS:, :].rearrange("p t e -> p e t")))
            base = v
            with dve.Fori(0, BITS) as r:
                def at(k):
                    dve.wait_ge(s["f_v"], 8 * r + base + k)
                dve.scalar_tensor_tensor(out=cand[:], in0=low[:], scalar=bit[:, 0:1], in1=low[:], op0=ALU.bitwise_or, op1=ALU.bitwise_or).then_inc(s["f_v"], 1)
                at(1)
                dve.tensor_tensor(cmp_[:], A[:], g3(cand[:].bitcast(F32)), ALU.is_ge).then_inc(s["f_v"], 1)
                at(2)
                dve.tensor_reduce(cnt[:], cmp_[:], AX.X, ALU.add).then_inc(s["f_cnt"], 1)
                dve.wait_ge(s["f_count"], r + 1)
                dve.tensor_tensor(ge[:], pC[:, 0:G2], cap[:], ALU.is_ge).then_inc(s["f_v"], 1)
                at(3)
                dve.tensor_scalar(mask[:], ge[:], -1.0, None, ALU.mult).then_inc(s["f_v"], 1)
                at(4)
                dve.tensor_scalar(bits[:], mask[:], bit[:, 0:1], None, ALU.bitwise_and).then_inc(s["f_v"], 1)
                at(5)
                dve.tensor_tensor(low[:], low[:], bits[:], ALU.bitwise_or).then_inc(s["f_v"], 1)
                at(6)
                dve.tensor_scalar(bit[:, 1:2], bit[:, 0:1], 1, None, ALU.logical_shift_right).then_inc(s["f_v"], 1)
                at(7)
                dve.tensor_copy(bit[:, 0:1], bit[:, 1:2]).then_inc(s["f_v"], 1)
                at(8)
            v = base + 8 * BITS
            least = g3(low[:].bitcast(F32))
            dve.tensor_tensor(gt[:], A[:], least, ALU.is_gt)
            did(dve.tensor_tensor(eq[:], A[:], least, ALU.is_equal))
            dve.tensor_reduce(cnt[:], gt[:], AX.X, ALU.add).then_inc(s["f_cnt"], 1)

            def prefix(m, k):
                did(dve.tensor_tensor_scan(fl(cum), notfirst[:], fl(m), 0.0, ALU.mult, ALU.add))
                dve.tensor_copy(selb[:], m[:])
                dve.tensor_tensor(cumb[:], cum[:], m[:], ALU.subtract).then_inc(s["f_pre"], 1)
                dve.wait_ge(s["f_pos"], k)

            prefix(eq, 1)
            dve.wait_ge(s["f_count"], BITS + 1)
            did(dve.tensor_tensor(need[:], cap[:], pC[:, 0:G2], ALU.subtract))
            did(dve.tensor_tensor(pos[:], g3(need[:]), pP[:].rearrange("p (g t) -> p g t", g=G2), ALU.is_gt))
            did(dve.tensor_tensor(eq[:], eq[:], pos[:], ALU.mult))
            did(dve.tensor_tensor(gt[:], gt[:], eq[:], ALU.add))
            prefix(gt, 2)
            did(dve.tensor_scalar(pos[:], pP[:].rearrange("p (g t) -> p g t", g=G2), -FAR, None, ALU.add))
            did(dve.tensor_tensor(pos[:], pos[:], gt[:], ALU.mult))
            did(dve.tensor_scalar(pos[:], pos[:], FAR, None, ALU.add))
            dve.sem_inc(s["f_idd"], 1)
            with dve.Fori(0, NE // 2) as i:
                for b in range(2):
                    e = 2 * i + b
                    dve.wait_ge(s["f_hused"], e + 1)
                    for t in range(TS):
                        dve.tensor_scalar(hot[:, b, t, :], slots[:], pos[:, bass.ds(e, 1), t:t + 1].rearrange("p a b -> p (a b)"), None, ALU.is_equal)
                    for t in range(TP):
                        last = dve.tensor_scalar(hot[:, b, TS + t, 0:CAP_P], slots[:, 0:CAP_P], pos[:, bass.ds(NE + e, 1), t:t + 1].rearrange("p a b -> p (a b)"), None, ALU.is_equal)
                    last.then_inc(s["f_hot"], 1)
                    dve.wait_ge(s["f_id"], e + 1)
                    dve.tensor_copy(two[:, 0, :], pI[0][:, 0:2])
                    dve.tensor_copy(two[:, 1, :], pI[1][:, 0:2])
                    dve.tensor_copy(two[0:CAP_P, 2, :], pI[2][0:CAP_P, 0:2]).then_inc(s["f_idv"], 1)
                    dve.wait_ge(s["f_idv"], e + 1)
                    dve.scalar_tensor_tensor(out=idf[:], in0=two[:, :, 0], scalar=float(P), in1=two[:, :, 1], op0=ALU.mult, op1=ALU.add).then_inc(s["f_idd"], 1)
                    dve.wait_ge(s["f_idd"], 2 * e + 2)
                    dve.tensor_copy(index[:, bass.ds(e, 1), :], idf[:].rearrange("p (o k) -> p o k", o=1)).then_inc(s["f_idd"], 1)

        @block.tensor
        def _(pe):
            pe.wait_ge(s["f_v"], 1)
            with pe.Fori(0, BITS) as r:
                pe.wait_ge(s["f_cnt"], r + 1)
                pe.matmul(pC[:, 0:G2], onesf[:], cnt[:], start=True, stop=True).then_inc(s["f_count"], 1)
            pe.wait_ge(s["f_cnt"], BITS + 1)
            pe.matmul(pC[:, 0:G2], onesf[:], cnt[:], start=True, stop=True).then_inc(s["f_count"], 1)
            for k in range(2):
                pe.wait_ge(s["f_pre"], k + 1)
                pe.matmul(pP[:], before[:], fl(selb), start=True, stop=False)
                pe.matmul(pP[:], onesb[:], fl(cumb), start=False, stop=True).then_inc(s["f_pos"], 1)
            pe.sem_inc(s["f_hused"], 2)
            with pe.Fori(0, NE // 2) as i:
                for b in range(2):
                    e = 2 * i + b
                    pe.wait_ge(s["f_hot"], e + 1)
                    pe.wait_ge(s["f_idd"], 2 * e + 1)
                    for k in range(2):
                        for t in range(TS):
                            pe.matmul(pI[k][:, 0:2], hot[:, b, t, k * P:(k + 1) * P], ids[:, t, :], start=(t == 0), stop=(t == TS - 1))
                    for t in range(TP):
                        mm = pe.matmul(pI[2][0:CAP_P, 0:2], hot[:, b, TS + t, 0:CAP_P], ids[:, TS + t, :], start=(t == 0), stop=(t == TP - 1))
                    mm.then_inc(s["f_id"], 1)
                    pe.wait_ge(s["f_id"], e + 1)
                    pe.sem_inc(s["f_hused"], 1)


WB = 256
NWB = F // WB
SLOT = [(0, P), (1, P), (2, CAP_P)]


def experts(nc, w_gate, w_up, w_down, hn_rows, aff_rows, index, out):
    with ExitStack() as ctx:
        sb, ps, sems = opened(nc, ctx)
        ident = sb("g_id", [P, P])
        raw = sb("g_raw", [P, 2, DC, WB])
        w_hi = sb("g_whi", [P, 2, DC, WB], F32R)
        w_lo = sb("g_wlo", [P, 2, DC, WB], F32R)
        idx = sb("g_idx", [P, 3], U32)
        idx2 = sb("g_idx2", [P, 2, 3], U32)
        rows = [sb(f"g_x{k}", [P, D]) for k in range(3)]
        gates = [sb(f"g_g{k}", [P, NE]) for k in range(3)]
        gate = sb("g_gate", [P, 2, 3])
        xh = sb("g_xh", [P, DC, CAP], F32R)
        xl = sb("g_xl", [P, DC, CAP], F32R)
        sg = sb("g_sg", [P, 2, CAP])
        hid = sb("g_hid", [P, 2, CAP])
        hh = sb("g_hh", [P, DC, CAP], F32R)
        hl = sb("g_hl", [P, DC, CAP], F32R)
        o = [sb(f"g_o{k}", [P, D]) for k in range(3)]
        pG = [ps(f"g_pG{k}") for k in range(2)]
        pU = [ps(f"g_pU{k}") for k in range(2)]
        pD = [ps(f"g_pD{k}") for k in range(3)]
        pT = ps("g_pT")
        s = sems("g_c g_w0 g_w1 g_hi g_lo g_gu g_sg g_t g_hid g_hh g_hl g_ga g_tr g_xh g_xl g_dn g_dv g_sc g_seen g_idx g_i2 g_gt g_wfree g_rows g_ofree g_mark g_pad")
        block = ctx.enter_context(nc.Block())
        mats = (w_gate, w_up, w_down)
        plan = [(m, c) for c in range(NWB) for m in (0, 1)] + [(2, c) for c in range(NWB)]
        NBK = len(plan)
        NTR = 6
        chunks = [(k, n, c) for k, n in SLOT for c in range(DC)]

        @block.sync
        def _(sp):
            with sp.Fori(0, NE) as e:
                for q, (m, c) in enumerate(plan):
                    sp.wait_ge(s["g_wfree"], NBK * e + q + 1)
                    sp.sem_inc(s["g_seen"], 1)
                    sp.dma_start(raw[:, q % 2, :, :], mats[m][bass.ds(e, 1), :, c * WB:(c + 1) * WB].rearrange("o (k p) f -> p (o k) f", p=P))\
                      .then_inc(s[f"g_w{q % 2}"], 16)

        @block.gpsimd
        def _(pool):
            identity(nc, pool, ident[:], s["g_c"])
            with pool.Fori(0, NE) as e:
                pool.wait_ge(s["g_idx"], e + 1)
                pool.sem_inc(s["g_mark"], 1)
                for k, n in SLOT:
                    pool.indirect_dma_start(rows[k][0:n, :], None, hn_rows, bass.IndirectOffsetOnAxis(ap=idx[0:n, k:k + 1], axis=0)).then_inc(s["g_ga"], 16)
                for k, n in SLOT:
                    pool.indirect_dma_start(gates[k][0:n, :], None, aff_rows, bass.IndirectOffsetOnAxis(ap=idx[0:n, k:k + 1], axis=0)).then_inc(s["g_ga"], 16)
                pool.wait_ge(s["g_dv"], 3 * NWB * (e + 1) + 3)
                pool.sem_inc(s["g_mark"], 1)
                for k, n in SLOT:
                    pool.indirect_dma_start(out, bass.IndirectOffsetOnAxis(ap=idx[0:n, k:k + 1], axis=0), o[k][0:n, :], None,
                                            compute_op=ALU.add).then_inc(s["g_sc"], 16)
                pool.wait_ge(s["g_sc"], 48 * (e + 1))
                pool.sem_inc(s["g_ofree"], 1)

        @block.scalar
        def _(act):
            act.sem_inc(s["g_dv"], 3)
            with act.Fori(0, NE) as e:
                for r in range(NTR):
                    act.wait_ge(s["g_tr"], NTR * e + r + 1)
                    k, n, c = chunks[4 * r]
                    act.activation(xh[:, c:c + 4, k * P:k * P + n], pT[:].rearrange("p (c t) -> p c t", c=4)[:, :, 0:n], ACT.Copy).then_inc(s["g_xh"], 1)
                for q, (m, c) in enumerate(plan):
                    act.wait_ge(s[f"g_w{q % 2}"], 16 * (NBK // 2 * e + q // 2 + 1))
                    if q >= 2:
                        act.wait_ge(s["g_gu"], NBK * e + q - 1)
                    act.activation(w_hi[:, q % 2, :, :], raw[:, q % 2, :, :], ACT.Copy).then_inc(s["g_hi"], 1)
                    if m == 1:
                        act.wait_ge(s["g_gu"], NBK * e + q)
                        for k in range(2):
                            last = act.activation(sg[:, k, :], pG[k][:, 0:CAP], ACT.Sigmoid)
                        last.then_inc(s["g_sg"], 1)
                        act.wait_ge(s["g_hid"], NWB * e + c + 2)
                        act.activation(hh[:, 2 * c:2 * c + 2, :], hid[:], ACT.Copy).then_inc(s["g_hh"], 1)
                    if m == 2:
                        if c == 0:
                            act.wait_ge(s["g_ofree"], e + 1)
                            act.wait_ge(s["g_gt"], e + 1)
                        for k, n in SLOT:
                            act.wait_ge(s["g_dn"], 3 * (NWB * e + c) + k + 1)
                            act.activation(o[k][0:n, c * WB:(c + 1) * WB], pD[k][0:n, 0:WB], ACT.Copy, scale=gate[0:n, 0, k:k + 1]).then_inc(s["g_dv"], 1)

        @block.vector
        def _(dve):
            dve.sem_inc(s["g_wfree"], 2)
            dve.sem_inc(s["g_hid"], 1)
            dve.sem_inc(s["g_xl"], 1)
            dve.sem_inc(s["g_ofree"], 1)
            dve.memset(rows[2][CAP_P:, :], 0.0).then_inc(s["g_pad"], 1)
            with dve.Fori(0, NE) as e:
                dve.wait_ge(s["g_ofree"], e + 1)
                dve.tensor_copy(idx[:, :], index[:, bass.ds(e, 1), :].rearrange("p o k -> p (o k)")).then_inc(s["g_idx"], 1)
                dve.wait_ge(s["g_ga"], 96 * (e + 1))
                for k, n in SLOT:
                    last = dve.tensor_copy(gate[0:n, 0, k:k + 1], gates[k][0:n, bass.ds(e, 1)])
                last.then_inc(s["g_gt"], 1)
                for r in range(NTR):
                    dve.wait_ge(s["g_xh"], NTR * e + r + 1)
                    k, n, c = chunks[4 * r]
                    dve.tensor_tensor(xl[:, c:c + 4, k * P:k * P + n], pT[:].rearrange("p (c t) -> p c t", c=4)[:, :, 0:n],
                                      xh[:, c:c + 4, k * P:k * P + n].bitcast(F32), ALU.subtract).then_inc(s["g_xl"], 1)
                for q, (m, c) in enumerate(plan):
                    dve.wait_ge(s["g_hi"], NBK * e + q + 1)
                    dve.tensor_tensor(w_lo[:, q % 2, :, :], raw[:, q % 2, :, :], w_hi[:, q % 2, :, :].bitcast(F32), ALU.subtract).then_inc(s["g_lo"], 1)
                    dve.wait_ge(s["g_lo"], NBK * e + q + 1)
                    dve.sem_inc(s["g_wfree"], 1)
                    if m == 1:
                        dve.wait_ge(s["g_sg"], NWB * e + c + 1)
                        for k in range(2):
                            last = dve.tensor_tensor(sg[:, k, :], sg[:, k, :], pG[k][:, 0:CAP], ALU.mult)
                        last.then_inc(s["g_t"], 1)
                        dve.wait_ge(s["g_t"], NWB * e + c + 1)
                        dve.wait_ge(s["g_gu"], NBK * e + q + 1)
                        for k in range(2):
                            last = dve.tensor_tensor(hid[:, k, :], sg[:, k, :], pU[k][:, 0:CAP], ALU.mult)
                        last.then_inc(s["g_hid"], 1)
                        dve.wait_ge(s["g_hh"], NWB * e + c + 1)
                        dve.tensor_tensor(hl[:, 2 * c:2 * c + 2, :], hid[:], hh[:, 2 * c:2 * c + 2, :].bitcast(F32), ALU.subtract).then_inc(s["g_hl"], 1)

        @block.tensor
        def _(pe):
            pe.wait_ge(s["g_c"], 2)
            pe.wait_ge(s["g_pad"], 1)
            with pe.Fori(0, NE) as e:
                pe.wait_ge(s["g_ga"], 96 * (e + 1))
                for r in range(NTR):
                    pe.wait_ge(s["g_xl"], NTR * e + r + 1)
                    for j, (k, n, c) in enumerate(chunks[4 * r:4 * r + 4]):
                        mm = pe.transpose(pT[:, j * P:(j + 1) * P], rows[k][:, c * P:(c + 1) * P], ident[:])
                    mm.then_inc(s["g_tr"], 1)
                pe.wait_ge(s["g_xl"], NTR * (e + 1) + 1)
                for q, (m, c) in enumerate(plan):
                    pe.wait_ge(s["g_lo"], NBK * e + q + 1)
                    if m < 2:
                        if m == 0:
                            pe.wait_ge(s["g_hid"], NWB * e + c + 1)
                        for k in range(2):
                            for d in range(DC):
                                for j, (w, x) in enumerate(((w_hi, xh), (w_hi, xl), (w_lo, xh))):
                                    mm = pe.matmul((pG, pU)[m][k][:, 0:CAP], w[:, q % 2, d, k * P:(k + 1) * P], x[:, d, :], start=(d == 0 and j == 0),
                                                   stop=(d == DC - 1 and j == 2))
                        mm.then_inc(s["g_gu"], 1)
                    else:
                        if c == 0:
                            pe.wait_ge(s["g_hl"], NWB * (e + 1))
                        for k, n in SLOT:
                            pe.wait_ge(s["g_dv"], 3 * (NWB * e + c) + k + 1)
                            for d in range(DC):
                                for j, (x, w) in enumerate(((hh, w_hi), (hh, w_lo), (hl, w_hi))):
                                    mm = pe.matmul(pD[k][0:n, 0:WB], x[:, d, k * P:k * P + n], w[:, q % 2, d, :], start=(d == 0 and j == 0),
                                                   stop=(d == DC - 1 and j == 2))
                            mm.then_inc(s["g_dn"], 1)
                        pe.wait_ge(s["g_dn"], 3 * (NWB * e + c + 1))
                        pe.sem_inc(s["g_gu"], 1)


def program(nc, ins, out):
    dram = lambda name, shape: nc.dram_tensor(name, list(shape), F32).ap()
    xT_hi, xT_lo = dram("xT_hi", [DC, P, NCOL]), dram("xT_lo", [DC, P, NCOL])
    qT = dram("qT", [NT, P, QH * P])
    mixT = dram("mixT", [D, N])
    ops = dram("ops", [2, NCH, P, 4, RT, C])
    vals = dram("vals", [NCH, P, RT, C])
    gateT, bonusT = dram("gateT", [RT, P, N]), dram("bonusT", [RT, P, N])
    yT = dram("yT", [2, RT, P, N])
    hn_rows = dram("hn_rows", [N, D])
    aff_rows = dram("aff_rows", [N, NE])
    with ExitStack() as ctx:
        KT = ctx.enter_context(nc.sbuf_tensor("KT", [P, 4, N], F32R))
        VS = ctx.enter_context(nc.sbuf_tensor("VS", [P, NT, KVH, P], F32R))
        attention_inputs(nc, ins["x"], ins["norm1"], ins["w_in"], ins["q_norm"], ins["k_norm"], ins["rope"], xT_hi, xT_lo, qT, KT, VS)
        attention(nc, qT, KT, VS, mixT, 0, NS // P, "sa")
        attention(nc, qT, KT, VS, mixT, NS // P, NP_ // P, "pa")
    with ExitStack() as ctx:
        WC = ctx.enter_context(nc.sbuf_tensor("WC", [P, 2, NB, 16], F32))
        rwkv_inputs(nc, ins["w_in"], ins["shift_taps"], ins["w0"], ins["w_lora_up"], ins["a0"], ins["a_lora_up"], ins["k_k"], ins["k_a"],
                    ins["r_k"], ins["g_lora_up"], xT_hi, xT_lo, ops, vals, gateT, bonusT, WC)
        recurrence(nc, ops, vals, WC, yT)
    with ExitStack() as ctx:
        logits = ctx.enter_context(nc.sbuf_tensor("logits", [P, NT, NE], F32))
        index = ctx.enter_context(nc.sbuf_tensor("index", [P, NE, 3], U32))
        mix_and_route(nc, ins["x"], ins["w_out"], ins["ln_g"], ins["ln_b"], ins["norm2"], ins["w_router"], yT, gateT, bonusT, mixT,
                      out, hn_rows, logits)
        choose(nc, logits, aff_rows, index)
        experts(nc, ins["expert_w_gate"], ins["expert_w_up"], ins["expert_w_down"], hn_rows, aff_rows, index, out)


def rope_table():
    inv_freq = np.float32(10000.0) ** (-np.arange(16, dtype=np.float32) / 16)
    tabs = []
    for n in (NS, NP_):
        row = np.repeat(np.arange(n // 64, dtype=np.float32), 64)[:, None] * inv_freq
        col = np.tile(np.arange(64, dtype=np.float32), n // 64)[:, None] * inv_freq
        cos = np.concatenate([np.cos(row), np.cos(row), np.cos(col), np.cos(col)], 1)
        sin = np.concatenate([-np.sin(row), np.sin(row), -np.sin(col), np.sin(col)], 1)
        tabs.append(np.stack([cos, sin], 1))
    return np.concatenate(tabs, 0).astype(np.float32)


def kernel(x_prompt, x_sample, norm1, w_in, shift_taps, w0, w_lora_up, a0, a_lora_up, k_k, k_a, r_k, g_lora_up, ln_g, ln_b,
           q_norm, k_norm, w_out, norm2, w_router, expert_w_gate, expert_w_up, expert_w_down):
    import concourse.bacc as _bacc
    from concourse.bass_utils import run_bass_kernel_spmd as _run

    arrays = dict(norm1=norm1, w_in=w_in, shift_taps=shift_taps, w0=w0, w_lora_up=w_lora_up, a0=a0, a_lora_up=a_lora_up, k_k=k_k,
                  k_a=k_a, r_k=r_k, g_lora_up=g_lora_up, ln_g=ln_g, ln_b=ln_b, q_norm=q_norm, k_norm=k_norm, w_out=w_out, norm2=norm2,
                  w_router=w_router, expert_w_gate=expert_w_gate, expert_w_up=expert_w_up, expert_w_down=expert_w_down)
    arrays = {name: np.ascontiguousarray(np.asarray(a)[0]) for name, a in arrays.items()}
    arrays["r_k"] = arrays["r_k"].reshape(-1)
    arrays["x"] = np.concatenate([np.asarray(x_sample)[0], np.asarray(x_prompt)[0]], 0)
    arrays["rope"] = rope_table()
    nc = _bacc.Bacc("TRN2", target_bir_lowering=False, num_devices=1)
    ins = {name: nc.dram_tensor(name, a.shape, F32, kind="ExternalInput").ap() for name, a in arrays.items()}
    out = nc.dram_tensor("out", [N, D], F32, kind="ExternalOutput").ap()
    program(nc, ins, out)
    y = np.asarray(_run(nc, [arrays], core_ids=[0]).results[0]["out"])
    return y[NS:].reshape(1, NP_, D), y[:NS].reshape(1, NS, D)
```

```python
from contextlib import ExitStack
import numpy as np
import concourse.bass as bass
from concourse import mybir

F32 = mybir.dt.float32
F32R = mybir.dt.float32r
BF16 = mybir.dt.bfloat16
I32 = mybir.dt.int32
U32 = mybir.dt.uint32
ALU = mybir.AluOpType
ACT = mybir.ActivationFunctionType
AX = mybir.AxisListType

P = 128
D = 1024
DC = D // P
NS, NP_ = 2048, 512
N = NS + NP_
NT = N // P
HD = 64
RW = 512
RC = 1792
FT = RC // P
QH, KVH = 8, 2
NH = QH + KVH
QK = NH * HD
AC = QK + KVH * HD
NCOL = N + 4
EPS = 1e-6


def opened(nc, ctx):
    def sb(name, shape, dt=F32):
        return ctx.enter_context(nc.sbuf_tensor(name, shape, dt))

    def ps(name, shape=(P, 512), dt=F32):
        return ctx.enter_context(nc.psum_tensor(name, list(shape), dt))

    def sems(names, prefix=""):
        handles = {n: nc.alloc_semaphore(name=prefix + n) for n in names.split()}
        ctx.callback(clear, nc, list(handles.values()))
        return handles

    return sb, ps, sems


def clear(nc, handles):
    nc.clear_and_free_semaphores(handles)
    nc.all_engine_barrier()


def bc(ap, shape):
    return ap.to_broadcast(shape)


def identity(nc, pool, tile, done):
    pool.memset(tile, 0.0).then_inc(done, 1)
    pool.wait_ge(done, 1)
    pool.affine_select(out=tile, in_=tile, compare_op=ALU.not_equal, fill=1.0, base=0,
                       pattern=[[-1, P]], channel_multiplier=1).then_inc(done, 1)


def live(i):
    return not isinstance(i, int) or 0 <= i < NT // 2


def lag(i, b, k):
    return i + (b - k) // 2, (b - k) % 2


def steps(engine, step):
    for t in range(4):
        step(t // 2, t % 2)
    with engine.Fori(2, NT // 2 - 1) as i:
        for b in range(2):
            step(i, b)
    for t in range(NT - 2, NT + 4):
        step(t // 2, t % 2)


def attention_inputs(nc, x, norm1, w_in, q_norm, k_norm, rope, xT_hi, xT_lo, qT, KT, VS):
    with ExitStack() as ctx:
        sb, ps, sems = opened(nc, ctx)
        w_raw = sb("w_raw", [P, AC])
        w_hi = sb("w_hi", [P, DC, AC], F32R)
        w_lo = sb("w_lo", [P, DC, AC], F32R)
        gain = sb("gain", [P, D])
        qk_gain = sb("qk_gain", [P, NH, HD])
        eps = sb("eps", [P, 1])
        zero_col = sb("zero_col", [P, DC])
        zf = sb("zf", [P, DC])
        ident = sb("ident", [P, P])
        x_in = sb("x_in", [P, 2, D])
        junk = sb("junk", [P, D])
        ss = sb("ss", [P, 2])
        sd = sb("sd", [P, 2])
        rs = sb("rs", [P, 2])
        xn = sb("xn", [P, 2, D])
        xh = sb("xh", [P, 2, DC, P], F32R)
        xl = sb("xl", [P, 2, DC, P], F32R)
        cs = sb("cs", [P, 2, 2, HD])
        qkv = sb("qkv", [P, 2, AC])
        sq = sb("sq", [P, QK])
        hss = sb("hss", [P, NH])
        hsd = sb("hsd", [P, NH])
        hrs = sb("hrs", [P, NH])
        qn = sb("qn", [P, NH, HD])
        qg = sb("qg", [P, NH, HD])
        rot = sb("rot", [P, NH, HD])
        qc = sb("qc", [P, NH, HD])
        qr = sb("qr", [P, NH, HD])
        hl = sb("hl", [P, QH, 2, HD], F32R)
        kd = sb("kd", [P, KVH, 2, 2, HD], F32R)
        q_out = sb("q_out", [P, 2, QH, P], F32R)
        pT = [ps(f"pT{k}") for k in range(2)]
        pQ = ps("pQ")
        pKV = ps("pKV")
        pR = [ps(f"pR{k}") for k in range(3)]
        s = sems("a_id a_const a_gain a_wl0 a_wl1 a_whi a_wlo a_x0 a_x1 a_cs0 a_cs1 a_ss a_sd a_rs a_xn a_tr a_xh a_xl a_proj a_q"
                 " a_sq a_hss a_hsd a_hrs a_qn a_qg a_rotA a_qc a_qr a_hi a_lo a_vhi a_vlo"
                 " a_rtr a_qo a_qs0 a_qs1 a_ko a_st0 a_st1 a_zero a_xfree a_csfree")
        block = ctx.enter_context(nc.Block())

        @block.sync
        def _(sp):
            sp.dma_start(gain[:], norm1.partition_broadcast(P)).then_inc(s["a_gain"], 16)
            for h in range(QH):
                sp.dma_start(qk_gain[:, h, :], q_norm.partition_broadcast(P)).then_inc(s["a_gain"], 16)
            for h in range(KVH):
                sp.dma_start(qk_gain[:, QH + h, :], k_norm.partition_broadcast(P)).then_inc(s["a_gain"], 16)

            def load_x(i, b):
                if live(i):
                    t = 2 * i + b
                    sp.wait_ge(s["a_xfree"], t + 1)
                    sp.dma_start(x_in[:, b, :], x[bass.ds(t * P, P), :]).then_inc(s[f"a_x{b}"], 16)

            def load_cs(i, b):
                if live(i):
                    t = 2 * i + b
                    sp.wait_ge(s["a_csfree"], t + 1)
                    sp.dma_start(cs[:, b, :, :], rope[bass.ds(t * P, P), :, :]).then_inc(s[f"a_cs{b}"], 16)

            def step(i, b):
                load_x(*lag(i, b, -1))
                load_cs(*lag(i, b, 2))

            load_x(0, 0)
            steps(sp, step)

        @block.gpsimd
        def _(pool):
            pool.memset(eps[:], EPS).then_inc(s["a_const"], 1)
            pool.memset(zf[:], 0.0).then_inc(s["a_const"], 1)
            pool.wait_ge(s["a_const"], 2)
            pool.tensor_copy(zero_col[:], zf[:]).then_inc(s["a_const"], 1)
            pool.wait_ge(s["a_const"], 3)
            for col in (0, NS + 1, N + 2):
                for dst in (xT_hi, xT_lo):
                    pool.dma_start(dst[:, :, col:col + 1].rearrange("c p o -> p c o"), zero_col[:].rearrange("p (c o) -> p c o", o=1), allow_slow_non_contiguous=True).then_inc(s["a_zero"], 16)
            identity(nc, pool, ident[:], s["a_id"])
            for c in range(DC):
                pool.dma_start(w_raw[:], w_in[c * P:(c + 1) * P, RC:]).then_inc(s["a_wl0"], 16)
                pool.wait_ge(s["a_whi"], c + 1)
                pool.tensor_tensor(w_lo[:, c, :], w_raw[:], w_hi[:, c, :].bitcast(F32), ALU.subtract).then_inc(s["a_wlo"], 1)
                pool.wait_ge(s["a_wlo"], c + 1)

            def rotate(i, b):
                if live(i):
                    t = 2 * i + b
                    pool.wait_ge(s["a_q"], t + 2)
                    pool.tensor_tensor(sq[:], qkv[:, b, 0:QK], qkv[:, b, 0:QK], ALU.mult).then_inc(s["a_sq"], 1)
                    pool.tensor_copy(VS[:, bass.ds(t, 1), :, 0:HD], qkv[:, b:b + 1, QK:].rearrange("p o (g d) -> p o g d", g=KVH)).then_inc(s["a_vhi"], 1)
                    pool.wait_ge(s["a_vhi"], t + 1)
                    pool.tensor_tensor(VS[:, bass.ds(t, 1), :, HD:], qkv[:, b:b + 1, QK:].rearrange("p o (g d) -> p o g d", g=KVH),
                                       VS[:, bass.ds(t, 1), :, 0:HD].bitcast(F32), ALU.subtract).then_inc(s["a_vlo"], 1)
                    pool.wait_ge(s["a_qn"], t + 3)
                    pool.tensor_tensor(qg[:], qn[:], qk_gain[:], ALU.mult).then_inc(s["a_qg"], 1)
                    pool.wait_ge(s["a_qg"], t + 1)
                    pool.wait_ge(s[f"a_cs{b}"], 16 * (i + 1))
                    pool.tensor_tensor(qc[:], qg[:], bc(cs[:, b, 0:1, :], [P, NH, HD]), ALU.mult).then_inc(s["a_qc"], 1)

            steps(pool, lambda i, b: rotate(*lag(i, b, 3)))

        @block.scalar
        def _(act):
            for c in range(DC):
                act.wait_ge(s["a_wl0"], 16 * (c + 1))
                act.activation(w_hi[:, c, :], w_raw[:], ACT.Copy).then_inc(s["a_whi"], 1)
            act.wait_ge(s["a_const"], 3)
            for b in range(2):
                act.sem_inc(s[f"a_st{b}"], 32)
                act.sem_inc(s[f"a_qs{b}"], 16)

            def square(i, b):
                if live(i):
                    act.wait_ge(s[f"a_x{b}"], 16 * (i + 1))
                    act.activation(junk[:], x_in[:, b, :], ACT.Square, accum_out=ss[:, b:b + 1]).then_inc(s["a_ss"], 1)
                    act.wait_ge(s["a_ss"], 2 * i + b + 1)
                    act.activation(sd[:, b:b + 1], ss[:, b:b + 1], ACT.Sqrt, bias=eps[:, 0:1], scale=1.0 / D).then_inc(s["a_sd"], 1)

            def high(i, b):
                if live(i):
                    t = 2 * i + b
                    act.wait_ge(s[f"a_st{b}"], 32 * (i + 1))
                    act.wait_ge(s["a_proj"], t + 1)
                    act.wait_ge(s["a_tr"], t + 1)
                    for k in range(2):
                        last = act.activation(xh[:, b, 4 * k:4 * k + 4, :], pT[k][:].rearrange("p (c t) -> p c t", c=4), ACT.Copy)
                    last.then_inc(s["a_xh"], 1)

            def store_x(i, b):
                if live(i):
                    t = 2 * i + b
                    act.wait_ge(s["a_xh"], t + 1)
                    act.wait_ge(s["a_xl"], t + 2)
                    for dst, src in ((xT_hi, xh), (xT_lo, xl)):
                        act.dma_start(dst[:, :, bass.ds(t * P + 1 + (t >> 4), P)].rearrange("c p t -> p c t"), src[:, b, :, :].bitcast(F32)).then_inc(s[f"a_st{b}"], 16)

            def projected(i, b):
                if live(i):
                    t = 2 * i + b
                    act.wait_ge(s["a_proj"], t + 3)
                    act.wait_ge(s["a_qn"], t + 1)
                    act.wait_ge(s["a_vlo"], t + 1)
                    act.activation(qkv[:, b, QH * HD:], pKV[:, 0:AC - QH * HD], ACT.Copy)
                    act.activation(qkv[:, b, 0:QH * HD], pQ[:], ACT.Copy).then_inc(s["a_q"], 1)

            def root(i, b):
                if live(i):
                    act.wait_ge(s["a_hss"], 2 * i + b + 1)
                    act.activation(hsd[:], hss[:], ACT.Sqrt, bias=eps[:, 0:1], scale=1.0 / HD).then_inc(s["a_hsd"], 1)

            def queries_out(i, b):
                if live(i):
                    t = 2 * i + b
                    act.wait_ge(s["a_rtr"], t + 1)
                    act.wait_ge(s[f"a_qs{b}"], 16 * (i + 1))
                    for k in range(2):
                        last = act.activation(q_out[:, b, 4 * k:4 * k + 4, :], pR[k][:].rearrange("p (c t) -> p c t", c=4), ACT.Copy)
                    last.then_inc(s["a_qo"], 1)
                    act.wait_ge(s["a_qo"], t + 2)
                    act.dma_start(qT[bass.ds(t, 1), :, :].rearrange("o p n -> (o p) n"), q_out[:, b, :, :].rearrange("p h t -> p (h t)").bitcast(F32)).then_inc(s[f"a_qs{b}"], 16)

            def step(i, b):
                high(*lag(i, b, 1))
                queries_out(*lag(i, b, 4))
                root(*lag(i, b, 3))
                square(i, b)
                store_x(*lag(i, b, 1))
                projected(*lag(i, b, 2))

            steps(act, step)
            act.wait_ge(s["a_zero"], 96)
            for b in range(2):
                act.wait_ge(s[f"a_st{b}"], 32 * (NT // 2 + 1))
                act.wait_ge(s[f"a_qs{b}"], 16 * (NT // 2 + 1))

        @block.vector
        def _(dve):
            dve.sem_inc(s["a_xfree"], 2)
            dve.sem_inc(s["a_csfree"], 2)
            dve.wait_ge(s["a_gain"], 16 * (1 + NH))
            dve.sem_inc(s["a_qn"], 2)
            dve.sem_inc(s["a_xl"], 1)
            dve.sem_inc(s["a_ko"], 1)

            def norm(i, b):
                if live(i):
                    t = 2 * i + b
                    dve.wait_ge(s["a_sd"], t + 1)
                    dve.reciprocal(rs[:, b:b + 1], sd[:, b:b + 1]).then_inc(s["a_rs"], 1)
                    dve.wait_ge(s["a_rs"], t + 1)
                    dve.scalar_tensor_tensor(out=xn[:, b, :], in0=x_in[:, b, :], scalar=rs[:, b:b + 1], in1=gain[:],
                                             op0=ALU.mult, op1=ALU.mult).then_inc(s["a_xn"], 1)
                    dve.wait_ge(s["a_xn"], t + 1)
                    dve.sem_inc(s["a_xfree"], 1)

            def low(i, b):
                if live(i):
                    dve.wait_ge(s["a_xh"], 2 * i + b + 1)
                    for k in range(2):
                        last = dve.tensor_tensor(xl[:, b, 4 * k:4 * k + 4, :], pT[k][:].rearrange("p (c t) -> p c t", c=4),
                                                 xh[:, b, 4 * k:4 * k + 4, :].bitcast(F32), ALU.subtract)
                    last.then_inc(s["a_xl"], 1)

            def head_norm(i, b):
                if live(i):
                    t = 2 * i + b
                    dve.wait_ge(s["a_sq"], t + 1)
                    dve.tensor_reduce(hss[:], sq[:].rearrange("p (h d) -> p h d", h=NH), AX.X, ALU.add).then_inc(s["a_hss"], 1)
                    dve.wait_ge(s["a_hsd"], t + 1)
                    dve.reciprocal(hrs[:], hsd[:]).then_inc(s["a_hrs"], 1)
                    dve.wait_ge(s["a_hrs"], t + 1)
                    dve.tensor_tensor(qn[:], qkv[:, b, 0:QK].rearrange("p (h d) -> p h d", h=NH),
                                      bc(hrs[:].rearrange("p (h o) -> p h o", o=1), [P, NH, HD]), ALU.mult).then_inc(s["a_qn"], 1)

            def rotate(i, b):
                if live(i):
                    t = 2 * i + b
                    dve.wait_ge(s["a_qg"], t + 1)
                    dve.wait_ge(s[f"a_cs{b}"], 16 * (i + 1))
                    halves = [m[:].rearrange("p h (a x j) -> p h a x j", a=2, x=2) for m in (rot, qg)]
                    sin = cs[:, b, 1:2, :].rearrange("p o (a x j) -> p o a x j", a=2, x=2)
                    for k in range(2):
                        last = dve.tensor_tensor(halves[0][:, :, :, k, :], halves[1][:, :, :, 1 - k, :],
                                                 bc(sin[:, :, :, k, :], [P, NH, 2, 16]), ALU.mult)
                    last.then_inc(s["a_rotA"], 1)
                    dve.wait_ge(s["a_rotA"], t + 1)
                    dve.wait_ge(s["a_qc"], t + 1)
                    dve.tensor_tensor(qr[:], qc[:], rot[:], ALU.add).then_inc(s["a_qr"], 1)
                    dve.wait_ge(s["a_qr"], t + 1)
                    dve.sem_inc(s["a_csfree"], 1)
                    dve.tensor_copy(hl[:, :, 0, :], qr[:, 0:QH, :])
                    dve.tensor_copy(kd[:, :, 0, :, :], bc(qr[:, QH:, :].rearrange("p g (o d) -> p g o d", o=1), [P, KVH, 2, HD])).then_inc(s["a_hi"], 1)
                    dve.wait_ge(s["a_hi"], t + 1)
                    dve.tensor_tensor(hl[:, :, 1, :], qr[:, 0:QH, :], hl[:, :, 0, :].bitcast(F32), ALU.subtract)
                    dve.tensor_tensor(kd[:, :, 1, :, :], bc(qr[:, QH:, :].rearrange("p g (o d) -> p g o d", o=1), [P, KVH, 2, HD]),
                                      kd[:, :, 0, :, :].bitcast(F32), ALU.subtract).then_inc(s["a_lo"], 1)

            def keys_out(i, b):
                if live(i):
                    t = 2 * i + b
                    dve.wait_ge(s["a_rtr"], t + 1)
                    dve.tensor_copy(KT[:, :, bass.ds(t * P, P)], pR[2][:].rearrange("p (c t) -> p c t", c=4)).then_inc(s["a_ko"], 1)

            def step(i, b):
                low(*lag(i, b, 1))
                keys_out(*lag(i, b, 4))
                head_norm(*lag(i, b, 3))
                norm(i, b)
                rotate(*lag(i, b, 3))

            steps(dve, step)

        @block.tensor
        def _(pe):
            pe.wait_ge(s["a_id"], 2)
            pe.wait_ge(s["a_wlo"], DC)
            pe.sem_inc(s["a_proj"], 2)
            pe.sem_inc(s["a_vlo"], 2)
            pe.sem_inc(s["a_q"], 1)
            pe.sem_inc(s["a_qo"], 1)

            def turn(i, b):
                if live(i):
                    t = 2 * i + b
                    pe.wait_ge(s["a_xn"], t + 1)
                    pe.wait_ge(s["a_xl"], t + 1)
                    for c in range(DC):
                        last = pe.transpose(pT[c // 4][:, (c % 4) * P:(c % 4 + 1) * P], xn[:, b, c * P:(c + 1) * P], ident[:])
                    last.then_inc(s["a_tr"], 1)

            def project(i, b):
                if live(i):
                    t = 2 * i + b
                    pe.wait_ge(s["a_xl"], t + 2)
                    pe.wait_ge(s["a_xh"], t + 1)
                    pe.wait_ge(s["a_q"], t + 1)
                    for out, a, z in ((pKV, QH * HD, AC), (pQ, 0, QH * HD)):
                        for c in range(DC):
                            for k, (l, r) in enumerate(((xh, w_hi), (xh, w_lo), (xl, w_hi))):
                                last = pe.matmul(out[:, 0:z - a], l[:, b, c, :], r[:, c, a:z], start=(c == 0 and k == 0),
                                                 stop=(c == DC - 1 and k == 2))
                    last.then_inc(s["a_proj"], 1)

            def turn_heads(i, b):
                if live(i):
                    t = 2 * i + b
                    pe.wait_ge(s["a_lo"], t + 1)
                    pe.wait_ge(s["a_qo"], t + 1)
                    pe.wait_ge(s["a_ko"], t + 1)
                    for h in range(QH):
                        pe.transpose(pR[h // 4][:, (h % 4) * P:(h % 4 + 1) * P], hl[:, h, :, :].rearrange("p a d -> p (a d)").bitcast(F32), ident[:])
                    for k in range(4):
                        last = pe.transpose(pR[2][:, k * P:(k + 1) * P], kd[:, k // 2, k % 2, :, :].rearrange("p a d -> p (a d)").bitcast(F32), ident[:])
                    last.then_inc(s["a_rtr"], 1)

            def step(i, b):
                turn(*lag(i, b, 1))
                turn_heads(*lag(i, b, 4))
                project(*lag(i, b, 2))

            steps(pe, step)


GH = QH // KVH
SCALE = HD ** -0.5


def attention(nc, qT, KT, VS, mixT, first_tile, n_tiles, name):
    nb = n_tiles // 4
    nk = n_tiles * P
    key0 = first_tile * P
    LAG = 7
    with ExitStack() as ctx:
        sb, ps, sems = opened(nc, ctx)
        identf = sb(name + "identf", [P, P])
        fold = sb(name + "fold", [P, HD])
        q = sb(name + "q", [P, 2, GH, P], F32R)
        mx = sb(name + "mx", [P, 2, nb])
        top = sb(name + "top", [P, 2])
        nm = sb(name + "nm", [P, 2])
        prob = sb(name + "prob", [P, 4, nk])
        den = sb(name + "den", [P, 2, nb])
        dsum = sb(name + "dsum", [P, 2])
        rden = sb(name + "rden", [P, 2])
        ph = sb(name + "ph", [P, 2, n_tiles, 2, P], F32R)
        pl = sb(name + "pl", [P, 2, n_tiles, 2, P], F32R)
        o_sb = sb(name + "o_sb", [P, 2, 2 * P])
        o_out = sb(name + "o_out", [HD, 2, 2 * P])
        pS = [ps(f"{name}pS{k}") for k in range(nb)]
        pT = [ps(f"{name}pT{k}") for k in range(2)]
        pO = [ps(f"{name}pO{k}") for k in range(2)]
        s = sems("id q0 q1 qfree score mx nm exp ds rd norm tr hi lo pv osb fold oout st0 st1 seen", name + "_")
        block = ctx.enter_context(nc.Block())
        live = lambda t: not isinstance(t, int) or 0 <= t < n_tiles
        head = lambda t, h: QH * t + h
        pair = lambda t, h: QH // 2 * t + h // 2

        def back(t, h, lag):
            return (t, h - lag) if h >= lag else (t - 1, h - lag + QH)

        def steps(engine, step):
            for h in range(QH):
                step(0, h)
            with engine.Fori(1, n_tiles) as t:
                for h in range(QH):
                    step(t, h)
            for h in range(LAG):
                step(n_tiles, h)

        @block.sync
        def _(sp):
            def load(t, g):
                sp.dma_start(q[:, g, :, :].rearrange("p h t -> p (h t)").bitcast(F32),
                             qT[bass.ds(first_tile + t, 1), :, g * GH * P:(g + 1) * GH * P].rearrange("o p n -> (o p) n")).then_inc(s[f"q{g}"], 16)

            def store(t):
                for k in range(QH // 2):
                    sp.wait_ge(s["oout"], pair(t, 2 * k) + 1)
                    rows = mixT[RW + k * 2 * HD:RW + (k + 1) * 2 * HD, bass.ds(key0 + t * P, P)]
                    sp.dma_start(rows.rearrange("(h d) t -> d h t", h=2),
                                 o_out[:, k % 2, :].rearrange("d (h t) -> d h t", h=2)).then_inc(s[f"st{k % 2}"], 16)

            for g in range(KVH):
                load(0, g)
            with sp.Fori(0, n_tiles - 1) as t:
                for g in range(KVH):
                    sp.wait_ge(s["qfree"], KVH * t + g + 1)
                    load(t + 1, g)
                store(t)
            store(n_tiles - 1)
            for k in range(2):
                sp.wait_ge(s[f"st{k}"], 16 * 2 * n_tiles)

        @block.gpsimd
        def _(pool):
            identity(nc, pool, identf[:], s["id"])
            pool.memset(fold[:], 0.0).then_inc(s["id"], 1)
            pool.wait_ge(s["id"], 3)
            for h in range(2):
                pool.affine_select(out=fold[:], in_=fold[:], compare_op=ALU.not_equal, fill=1.0, base=-HD * h,
                                   pattern=[[-1, HD]], channel_multiplier=1).then_inc(s["id"], 1)
                pool.wait_ge(s["id"], 4 + h)

            def step(t, h):
                if live(t):
                    pool.wait_ge(s["rd"], head(t, h) + 1)
                    pool.sem_inc(s["seen"], 1)
                    pool.tensor_scalar(prob[:, h % 4, :], prob[:, h % 4, :], rden[:, h % 2:h % 2 + 1], 1.0, ALU.mult, ALU.mult).then_inc(s["norm"], 1)

            steps(pool, step)

        @block.scalar
        def _(act):
            def exps(t, h, k):
                if live(t):
                    if k == 0:
                        act.wait_ge(s["nm"], head(t, h) + 1)
                    act.activation(prob[:, h % 4, k * 512:(k + 1) * 512], pS[k][:], ACT.Exp, bias=nm[:, h % 2:h % 2 + 1],
                                   scale=SCALE, accum_out=den[:, h % 2, k:k + 1]).then_inc(s["exp"], 1)

            def high(t, h, k):
                if live(t):
                    if k == 0 and h % 2 == 0 and live(back(t, h, 4)[0]):
                        act.wait_ge(s["pv"], pair(*back(t, h, 4)) + 1)
                    act.wait_ge(s["tr"], nb * head(t, h) + k + 1)
                    act.activation(ph[:, h // 2 % 2, 4 * k:4 * k + 4, h % 2, :], pT[(nb * h + k) % 2][:].rearrange("p (c t) -> p c t", c=4),
                                   ACT.Copy).then_inc(s["hi"], 1)

            def evacuate(t, h):
                if h % 2 == 0 and live(t):
                    p = h // 2 % 2
                    act.wait_ge(s["pv"], pair(t, h) + 1)
                    act.activation(o_sb[:, p, :], pO[p][:, 0:2 * P], ACT.Copy).then_inc(s["osb"], 1)

            def finish(t, h):
                if h % 2 == 0 and live(t):
                    p = h // 2 % 2
                    act.wait_ge(s["fold"], pair(t, h) + 1)
                    ts, hs = back(t, h, 4)
                    if live(ts):
                        act.wait_ge(s[f"st{p}"], 16 * (2 * ts + hs // 4 + 1))
                    act.activation(o_out[:, p, :], pO[p][0:HD, 2 * P:], ACT.Copy).then_inc(s["oout"], 1)

            def step(t, h):
                before = back(t, h, 1)
                exps(t, h, 0)
                if nb > 1:
                    exps(t, h, 1)
                    high(*back(t, h, 2), 2)
                    high(*back(t, h, 2), 3)
                    exps(t, h, 2)
                    exps(t, h, 3)
                    high(*before, 0)
                    high(*before, 1)
                    evacuate(*back(t, h, 5))
                    finish(*back(t, h, 6))
                else:
                    high(*before, 0)
                    evacuate(*back(t, h, 5))
                    finish(*back(t, h, 6))

            steps(act, step)

        @block.vector
        def _(dve):
            def top_of(t, h, k):
                if live(t):
                    dve.wait_ge(s["score"], nb * head(t, h) + k + 1)
                    ins = dve.tensor_reduce(mx[:, h % 2, k:k + 1], pS[k][:], AX.X, ALU.max)
                    if k == nb - 1:
                        ins.then_inc(s["mx"], 1)
                        dve.wait_ge(s["mx"], 2 * head(t, h) + 1)
                        dve.tensor_reduce(top[:, h % 2:h % 2 + 1], mx[:, h % 2, :], AX.X, ALU.max).then_inc(s["mx"], 1)
                        dve.wait_ge(s["mx"], 2 * head(t, h) + 2)
                        dve.tensor_scalar(nm[:, h % 2:h % 2 + 1], top[:, h % 2:h % 2 + 1], -SCALE, None, ALU.mult).then_inc(s["nm"], 1)

            def low(t, h, k):
                if live(t):
                    dve.wait_ge(s["hi"], nb * head(t, h) + k + 1)
                    dve.tensor_tensor(pl[:, h // 2 % 2, 4 * k:4 * k + 4, h % 2, :], pT[(nb * h + k) % 2][:].rearrange("p (c t) -> p c t", c=4),
                                      ph[:, h // 2 % 2, 4 * k:4 * k + 4, h % 2, :].bitcast(F32), ALU.subtract).then_inc(s["lo"], 1)

            def total(t, h):
                if live(t):
                    dve.wait_ge(s["exp"], nb * (head(t, h) + 1))
                    dve.tensor_reduce(dsum[:, h % 2:h % 2 + 1], den[:, h % 2, :], AX.X, ALU.add).then_inc(s["ds"], 1)
                    dve.wait_ge(s["ds"], head(t, h) + 1)
                    dve.reciprocal(rden[:, h % 2:h % 2 + 1], dsum[:, h % 2:h % 2 + 1]).then_inc(s["rd"], 1)

            def step(t, h):
                before = back(t, h, 2)
                top_of(t, h, 0)
                if nb > 1:
                    top_of(t, h, 1)
                    low(*back(t, h, 3), 2)
                    low(*back(t, h, 3), 3)
                    top_of(t, h, 2)
                    top_of(t, h, 3)
                total(*back(t, h, 1))
                low(*before, 0)
                if nb > 1:
                    low(*before, 1)

            steps(dve, step)

        @block.tensor
        def _(pe):
            def score(t, h, k):
                if live(t):
                    if k == 0 and h % GH == 0:
                        pe.wait_ge(s[f"q{h // GH}"], 16 * (t + 1))
                    tb, hb = back(t, h, 1)
                    if live(tb):
                        pe.wait_ge(s["exp"], nb * head(tb, hb) + k + 1)
                    for p in range(2):
                        mm = pe.matmul(pS[k][:], q[:, h // GH, h % GH, :], KT[:, 2 * (h // GH) + p, key0 + k * 512:key0 + (k + 1) * 512],
                                       start=(p == 0), stop=(p == 1))
                    mm.then_inc(s["score"], 1)
                    if k == nb - 1 and h % GH == GH - 1:
                        pe.wait_ge(s["score"], nb * (head(t, h) + 1))
                        pe.sem_inc(s["qfree"], 1)

            def turn(t, h, k):
                if live(t):
                    if k == 0:
                        pe.wait_ge(s["norm"], head(t, h) + 1)
                    if nb * h + k >= 2 or live(t - 1):
                        pe.wait_ge(s["lo"], nb * head(t, h) + k - 1)
                    for c in range(4):
                        m = 4 * k + c
                        mm = pe.transpose(pT[(nb * h + k) % 2][:, c * P:(c + 1) * P], prob[:, h % 4, m * P:(m + 1) * P], identf[:])
                    mm.then_inc(s["tr"], 1)

            def product(t, h, k):
                second = h % 2
                h -= second
                if live(t):
                    p = h // 2 % 2
                    if k == 0 and second == 0:
                        pe.wait_ge(s["lo"], nb * (head(t, h) + 2))
                    tb, hb = back(t, h, 4)
                    if k == 0 and second == 0 and live(tb):
                        pe.wait_ge(s["oout"], pair(tb, hb) + 1)
                    for j in range(2):
                        m = (second * nb + k) * 2 + j
                        for i, r in enumerate((ph, pl)):
                            mm = pe.matmul(pO[p][:, 0:2 * P], VS[:, first_tile + m, h // GH, :], r[:, p, m, :, :].rearrange("p h t -> p (h t)"),
                                           start=(m == 0 and i == 0), stop=(m == n_tiles - 1 and i == 1))
                    if m == n_tiles - 1:
                        mm.then_inc(s["pv"], 1)

            def step(t, h):
                turning, summing = back(t, h, 2), back(t, h, 4)
                if nb == 1:
                    score(t, h, 0)
                    turn(*turning, 0)
                    product(*summing, 0)
                else:
                    late = back(t, h, 3)
                    turn(*late, 2)
                    score(t, h, 0)
                    turn(*late, 3)
                    score(t, h, 1)
                    score(t, h, 2)
                    turn(*turning, 0)
                    score(t, h, 3)
                    turn(*turning, 1)
                    for k in range(nb):
                        product(*summing, k)
                tp, hp = back(t, h, 6)
                if hp % 2 == 0 and live(tp):
                    p = hp // 2 % 2
                    pe.wait_ge(s["osb"], pair(tp, hp) + 1)
                    pe.matmul(pO[p][0:HD, 2 * P:], fold[:], o_sb[:, p, :], start=True, stop=True).then_inc(s["fold"], 1)

            pe.wait_ge(s["id"], 5)
            steps(pe, step)


C = 64
NCH = N // C
TB = 256
NB = N // TB
WPB = TB // C
DMAS = 3 * WPB
RT = RW // P
KAPPA = float(np.exp(-0.5))
W_R, W_K, W_V, W_WA, W_G = 0, 4, 8, 12, 13


def rwkv_inputs(nc, w_in, shift_taps, w0, w_lora_up, a0, a_lora_up, k_k, k_a, r_k, g_lora_up, xT_hi, xT_lo, ops, vals, gateT, bonusT, WC):
    with ExitStack() as ctx:
        sb, ps, sems = opened(nc, ctx)
        w_hi = sb("c_whi", [P, DC, RC], F32R)
        w_lo = sb("c_wlo", [P, DC, RC], F32R)
        xh = sb("c_xh", [P, DC, TB + 2], F32R)
        xl = sb("c_xl", [P, DC, TB + 2], F32R)
        taps = sb("c_taps", [P, 3, FT])
        dirp = sb("c_dirp", [P, 2, 2, RT])
        chp = sb("c_chp", [P, 3, RT])
        wa_up = sb("c_wa", [P, 2, 2, RW])
        g_up = sb("c_gup", [P, RW])
        ones = sb("c_ones", [P, P])
        notfirst = sb("c_nf", [P, RT * TB])
        f = sb("c_f", [P, FT, TB])
        big = lambda n: sb("c_" + n, [P, RT, TB])
        nkk, kka, tmp, sg, aa, ei, kd, kk2 = [big(n) for n in "nkk kka tmp sg aa ei kd kdsum".split()]
        operands = sb("c_ops", [P, 4, RT, TB])
        e, u, bb, c = [operands[:, k, :, :] for k in range(4)]
        pP = [ps(f"c_pP{k}") for k in range(3)]
        pX = ctx.enter_context(nc.psum_tensor("c_pX", [P, RT, TB], F32))
        pY = ctx.enter_context(nc.psum_tensor("c_pY", [P, RT, TB], F32))
        s = sems("c_const c_par c_wraw c_whi c_wlo c_x c_xfree c_proj c_mid c_shift c_sq c_ss c_nrm c_th c_lora"
                 " c_sig c_scan c_v c_exp c_gate c_gs c_st c_bon c_p c_dch c_outfree c_wc c_bst c_kk c_kk2 c_cdve c_seen")
        block = ctx.enter_context(nc.Block())
        w_raw = f[:].rearrange("p a b -> p (a b)")[:, 0:RC]
        flat = lambda m: m[:].rearrange("p j t -> p (j t)")
        ch = lambda m: m[:].rearrange("p j (w t) -> p (j w) t", t=C)

        @block.sync
        def _(sp):
            col = lambda ap: ap.rearrange("(j p) -> p j", p=P)
            for k in range(3):
                sp.dma_start(taps[:, k, :], col(shift_taps[k]), allow_slow_non_contiguous=True).then_inc(s["c_par"], 16)
            for d in range(2):
                for k, v in enumerate((w0, a0)):
                    sp.dma_start(dirp[:, d, k, :], col(v[d]), allow_slow_non_contiguous=True).then_inc(s["c_par"], 16)
                sp.wait_ge(s["c_const"], 1)
                sp.dma_start(wa_up[0:64, d, 0, :], w_lora_up[d]).then_inc(s["c_par"], 16)
                sp.dma_start(wa_up[64:P, d, 1, :], a_lora_up[d]).then_inc(s["c_par"], 16)
            for k, v in enumerate((k_k, k_a, r_k)):
                sp.dma_start(chp[:, k, :], col(v), allow_slow_non_contiguous=True).then_inc(s["c_par"], 16)
            sp.dma_start(g_up[:], g_lora_up).then_inc(s["c_par"], 16)
            for m in range(DC):
                if m:
                    sp.wait_ge(s["c_wlo"], m)
                sp.dma_start(w_raw, w_in[m * P:(m + 1) * P, 0:RC]).then_inc(s["c_wraw"], 16)

            def load(i):
                for dst, src in ((xh, xT_hi), (xl, xT_lo)):
                    sp.dma_start(dst[:].bitcast(F32), src[:, :, bass.ds(TB * i + (i >> 3), TB + 2)].rearrange("c p t -> p c t")).then_inc(s["c_x"], 16)

            def store(i, d):
                sp.wait_ge(s["c_p"], 3 * i + 2 + d)
                sp.sem_inc(s["c_seen"], 1)
                for w in range(WPB):
                    part = slice(w * C, (w + 1) * C)
                    sp.dma_start(ops[d, bass.ds(WPB * i + w, 1), :, :, :, :].rearrange("o p k j t -> (o p) (k j) t"),
                                 operands[:].rearrange("p k j t -> p (k j) t")[:, :, part]).then_inc(s["c_st"], 16)
                    if d == 0:
                        sp.dma_start(vals[bass.ds(WPB * i + w, 1), :, :, :].rearrange("o p j t -> (o p) j t"), f[:, W_V:W_WA, part]).then_inc(s["c_st"], 16)

            def block_out(i, more):
                store(i, 0)
                if more:
                    sp.wait_ge(s["c_xfree"], i + 1)
                    sp.sem_inc(s["c_seen"], 1)
                    load(i + 1)
                store(i, 1)
                for k, o in ((0, gateT), (1, bonusT)):
                    sp.wait_ge(s["c_gs"], 2 * i + 1 + k)
                    sp.sem_inc(s["c_seen"], 1)
                    src = (tmp, kk2)[k]
                    sp.dma_start(o[:, :, bass.ds(TB * i, TB)].rearrange("j p t -> p j t"), src[:]).then_inc(s["c_bst"], 16)

            load(0)
            with sp.Fori(0, NB - 1) as i:
                block_out(i, True)
            block_out(NB - 1, False)
            sp.wait_ge(s["c_bst"], 32 * (NB + 1))
            sp.wait_ge(s["c_st"], 16 * DMAS * (NB + 1))

        @block.gpsimd
        def _(pool):
            pool.memset(wa_up[:], 0.0).then_inc(s["c_const"], 1)
            for m in range(DC):
                pool.wait_ge(s["c_whi"], m + 1)
                pool.tensor_tensor(w_lo[:, m, :], w_raw, w_hi[:, m, :].bitcast(F32), ALU.subtract).then_inc(s["c_wlo"], 1)
            with pool.Fori(0, NB) as i:
                pool.wait_ge(s["c_shift"], FT * (i + 1) + 1)
                pool.tensor_tensor(kka[:], f[:, W_K:W_V, :], bc(chp[:, 1, :].rearrange("p (j o) -> p j o", o=1), [P, RT, TB]), ALU.mult).then_inc(s["c_p"], 1)
                for d in range(2):
                    n = 2 * i + d
                    pool.wait_ge(s["c_v"], 3 * n + 3)
                    pool.wait_ge(s["c_exp"], n + 1)
                    pool.tensor_tensor(c[:], kd[:], ei[:], ALU.mult)
                    pool.tensor_tensor(u[:], f[:, W_R:W_K, :], u[:], ALU.mult)
                    pool.tensor_tensor(e[:], nkk[:], e[:], ALU.mult)
                    pool.tensor_tensor(bb[:], bb[:], ei[:], ALU.mult).then_inc(s["c_p"], 1)

        @block.scalar
        def _(act):
            for m in range(DC):
                act.wait_ge(s["c_wraw"], 16 * (m + 1))
                act.activation(w_hi[:, m, :], w_raw, ACT.Copy).then_inc(s["c_whi"], 1)
            act.wait_ge(s["c_par"], 16 * 15)
            act.wait_ge(s["c_wlo"], DC)
            with act.Fori(0, NB) as i:
                act.wait_ge(s["c_outfree"], i + 1)
                for m in range(FT):
                    act.wait_ge(s["c_proj"], FT * i + m + 1)
                    act.activation(f[:, m, :], pP[m % 3][:, 1:TB + 1], ACT.Copy, scale=taps[:, 1, m:m + 1]).then_inc(s["c_mid"], 1)
                act.wait_ge(s["c_ss"], i + 1)
                act.activation(sg[:], pX[:], ACT.Sqrt).then_inc(s["c_nrm"], 1)
                act.wait_ge(s["c_shift"], FT * (i + 1) + 1)
                act.activation(f[0:64, W_WA, :], f[0:64, W_WA, :], ACT.Tanh)
                act.activation(f[:, W_G, :], f[:, W_G, :], ACT.Sigmoid).then_inc(s["c_th"], 1)
                act.wait_ge(s["c_kk"], i + 1)
                for d in range(2):
                    n = 2 * i + d
                    act.wait_ge(s["c_lora"], n + 1)
                    if d:
                        act.wait_ge(s["c_p"], 3 * i + 2)
                    for j in range(RT):
                        act.activation(sg[:, j, :], pX[:, j, :], ACT.Sigmoid, bias=dirp[:, d, 0, j:j + 1])
                    for j in range(RT):
                        last = act.activation(aa[:, j, :], pY[:, j, :], ACT.Sigmoid, bias=dirp[:, d, 1, j:j + 1])
                    last.then_inc(s["c_sig"], 1)
                    act.wait_ge(s["c_v"], 3 * n + 3)
                    act.activation(ei[:], u[:], ACT.Exp, scale=KAPPA)
                    act.wait_ge(s["c_scan"], n + 1)
                    act.activation(WC[:, d, bass.ds(i, 1), :], c[:].rearrange("p j (w t) -> p (j w) t", t=C)[:, :, C - 1:C].rearrange("p a o -> p o a"), ACT.Exp, scale=-KAPPA).then_inc(s["c_wc"], 1)
                    act.activation(e[:], e[:], ACT.Exp, scale=-KAPPA)
                    act.activation(u[:], u[:], ACT.Exp, scale=-KAPPA).then_inc(s["c_exp"], 1)
                act.wait_ge(s["c_gate"], i + 1)
                act.activation(tmp[:], pX[:], ACT.Copy).then_inc(s["c_gs"], 1)

        @block.vector
        def _(dve):
            for h in range(2):
                for g in range(2):
                    dve.memset(ones[h * HD:h * HD + HD, g * HD:g * HD + HD], float(h == g))
            dve.memset(notfirst[:].rearrange("p (w t) -> p w t", t=C)[:, :, 1:], 1.0)
            dve.memset(notfirst[:].rearrange("p (w t) -> p w t", t=C)[:, :, 0:1], 0.0).then_inc(s["c_cdve"], 1)
            dve.wait_ge(s["c_cdve"], 1)
            dve.wait_ge(s["c_par"], 16 * 15)
            dve.sem_inc(s["c_outfree"], 1)
            dve.sem_inc(s["c_st"], 16 * DMAS)
            dve.sem_inc(s["c_bst"], 32)
            dve.sem_inc(s["c_shift"], 1)
            with dve.Fori(0, NB) as i:
                def step(k):
                    dve.wait_ge(s["c_dch"], DSTEPS * i + k)
                k = 0
                for m in range(FT):
                    dve.wait_ge(s["c_mid"], FT * i + m + 1)
                    dve.scalar_tensor_tensor(out=f[:, m, :], in0=pP[m % 3][:, 0:TB], scalar=taps[:, 0, m:m + 1], in1=f[:, m, :],
                                             op0=ALU.mult, op1=ALU.add).then_inc(s["c_dch"], 1)
                    k += 1
                    step(k)
                    dve.scalar_tensor_tensor(out=f[:, m, :], in0=pP[m % 3][:, 2:TB + 2], scalar=taps[:, 2, m:m + 1], in1=f[:, m, :],
                                             op0=ALU.mult, op1=ALU.add).then_inc(s["c_shift"], 1)
                dve.wait_ge(s["c_shift"], FT * (i + 1) + 1)
                dve.wait_ge(s["c_st"], 16 * DMAS * (i + 1))
                dve.wait_ge(s["c_bst"], 32 * (i + 1))
                dve.tensor_tensor(bb[:], f[:, W_K:W_V, :], bc(chp[:, 0, :].rearrange("p (j o) -> p j o", o=1), [P, RT, TB]), ALU.mult).then_inc(s["c_dch"], 1)
                k += 1
                step(k)
                dve.tensor_tensor(tmp[:], bb[:], bb[:], ALU.mult).then_inc(s["c_sq"], 1)
                dve.wait_ge(s["c_nrm"], i + 1)
                dve.tensor_scalar(sg[:], sg[:], 1e-12, None, ALU.max).then_inc(s["c_dch"], 1)
                k += 1
                step(k)
                dve.reciprocal(sg[:], sg[:]).then_inc(s["c_dch"], 1)
                k += 1
                step(k)
                dve.scalar_tensor_tensor(out=nkk[:], in0=bb[:], scalar=-1.0, in1=sg[:], op0=ALU.mult, op1=ALU.mult).then_inc(s["c_kk"], 1)
                for d in range(2):
                    n = 2 * i + d
                    dve.wait_ge(s["c_sig"], n + 1)
                    if d:
                        dve.wait_ge(s["c_st"], 16 * (DMAS * (i + 1) + 2 * WPB))
                    dve.tensor_tensor_scan(flat(c), notfirst[:], flat(sg), 0.0, ALU.mult, ALU.add).then_inc(s["c_dch"], 1)
                    k += 1
                    step(k)
                    if d == 0:
                        dve.tensor_tensor(e[:], c[:], sg[:], ALU.subtract)
                        dve.tensor_copy(u[:], c[:]).then_inc(s["c_v"], 1)
                    else:
                        dve.tensor_tensor(ch(e), bc(ch(c)[:, :, C - 1:C], [P, RT * TB // C, C]), ch(c), ALU.subtract).then_inc(s["c_dch"], 1)
                        k += 1
                        step(k)
                        dve.tensor_tensor(u[:], e[:], sg[:], ALU.add).then_inc(s["c_v"], 1)
                    dve.wait_ge(s["c_v"], 3 * n + 1)
                    dve.sem_inc(s["c_scan"], 1)
                    dve.scalar_tensor_tensor(out=bb[:], in0=nkk[:], scalar=-1.0, in1=aa[:], op0=ALU.mult, op1=ALU.mult).then_inc(s["c_v"], 1)
                    if d == 0:
                        dve.wait_ge(s["c_p"], 3 * i + 1)
                    dve.scalar_tensor_tensor(out=kd[:], in0=aa[:], scalar=-1.0, in1=kka[:], op0=ALU.add, op1=ALU.mult).then_inc(s["c_dch"], 1)
                    k += 1
                    step(k)
                    dve.tensor_tensor(kd[:], kd[:], f[:, W_K:W_V, :], ALU.add).then_inc(s["c_v"], 1)
                    dve.wait_ge(s["c_v"], 3 * n + 3)
                    if d == 0:
                        dve.tensor_copy(kk2[:], kd[:]).then_inc(s["c_dch"], 1)
                        dve.wait_ge(s["c_exp"], n + 1)
                        dve.wait_ge(s["c_wc"], 2 * i + 1)
                    else:
                        dve.tensor_tensor(kk2[:], kk2[:], kd[:], ALU.add).then_inc(s["c_dch"], 1)
                    k += 1
                    step(k)
                dve.tensor_tensor(kk2[:], kk2[:], f[:, W_R:W_K, :], ALU.mult).then_inc(s["c_dch"], 1)
                k += 1
                step(k)
                dve.scalar_tensor_tensor(out=kk2[:], in0=kk2[:], scalar=0.5, in1=bc(chp[:, 2, :].rearrange("p (j o) -> p j o", o=1), [P, RT, TB]),
                                         op0=ALU.mult, op1=ALU.mult).then_inc(s["c_kk2"], 1)
                dve.wait_ge(s["c_bon"], i + 1)
                dve.tensor_tensor(kk2[:], pY[:], f[:, W_V:W_WA, :], ALU.mult).then_inc(s["c_dch"], 1)
                k += 1
                dve.wait_ge(s["c_gs"], 2 * i + 1)
                step(k)
                dve.sem_inc(s["c_gs"], 1)
                assert k == DSTEPS
                dve.wait_ge(s["c_p"], 3 * i + 3)
                dve.sem_inc(s["c_outfree"], 1)

        @block.tensor
        def _(pe):
            pe.wait_ge(s["c_wlo"], DC)
            pe.wait_ge(s["c_const"], 1)
            pe.wait_ge(s["c_cdve"], 1)
            pe.wait_ge(s["c_par"], 16 * 15)
            with pe.Fori(0, NB) as i:
                pe.wait_ge(s["c_x"], 32 * (i + 1))
                for m in range(FT):
                    if m < 3:
                        pe.wait_ge(s["c_shift"], FT * i + 1)
                    else:
                        pe.wait_ge(s["c_shift"], FT * i + m - 1)
                    for q in range(DC):
                        for k, (w, x) in enumerate(((w_hi, xh), (w_hi, xl), (w_lo, xh))):
                            mm = pe.matmul(pP[m % 3][:, 0:TB + 2], w[:, q, m * P:(m + 1) * P], x[:, q, :], start=(q == 0 and k == 0),
                                           stop=(q == DC - 1 and k == 2))
                    mm.then_inc(s["c_proj"], 1)
                pe.wait_ge(s["c_proj"], FT * (i + 1))
                pe.sem_inc(s["c_xfree"], 1)
                pe.wait_ge(s["c_sq"], i + 1)
                for j in range(RT):
                    mm = pe.matmul(pX[:, j, :], ones[:], tmp[:, j, :], start=True, stop=True)
                mm.then_inc(s["c_ss"], 1)
                pe.wait_ge(s["c_th"], i + 1)
                for d in range(2):
                    if d:
                        pe.wait_ge(s["c_sig"], 2 * i + 1)
                    for k, o in enumerate((pX, pY)):
                        for j in range(RT):
                            mm = pe.matmul(o[:, j, :], wa_up[:, d, k, j * P:(j + 1) * P], f[:, W_WA, :], start=True, stop=True)
                    mm.then_inc(s["c_lora"], 1)
                pe.wait_ge(s["c_sig"], 2 * i + 2)
                for j in range(RT):
                    mm = pe.matmul(pX[:, j, :], g_up[:, j * P:(j + 1) * P], f[:, W_G, :], start=True, stop=True)
                mm.then_inc(s["c_gate"], 1)
                pe.wait_ge(s["c_kk2"], i + 1)
                for j in range(RT):
                    mm = pe.matmul(pY[:, j, :], ones[:], kk2[:, j, :], start=True, stop=True)
                mm.then_inc(s["c_bon"], 1)


DSTEPS = FT + 3 + 2 + 1 + 2 + 2 + 2


LEVELS = [2, 4, 8, 16, 32]
NL = len(LEVELS)
OP_A, OP_R, OP_B, OP_K, OP_V = range(5)


def recurrence(nc, ops, vals, WC, yT):
    with ExitStack() as ctx:
        sb, ps, sems = opened(nc, ctx)
        ident = sb("d_id", [P, 1, P])
        strict = sb("d_strict", [P, 2, P])
        upto = sb("d_upto", [P, 2, P])
        beside = sb("d_beside", [P, 2, NL + 1, P])
        decay = sb("d_decay", [P, 2, NCH, RT])
        bd = sb("d_bd", [P, 2, 2, 5, RT, P])
        mat = lambda n: [sb(f"d_{n}{g}", [P, RT, P]) for g in range(2)]
        bm, ak, rb, rk, tb, tk, tv, zz, yy, pm, zs, uu, st, tmp = [mat(n) for n in "bm ak rb rk tb tk tv zz yy pm zs uu st tmp".split()]
        y_out = sb("d_yo", [P, 2, 2, RT, C])
        bank = [[ps(f"d_p{g}{k}") for k in range(4)] for g in range(2)]
        s = sems("d_m d_dm d_ld00 d_ld01 d_ld10 d_ld11 d_ab d_rest d_bm d_craw d_mask d_ta d_tt d_tc d_init d_dch d_P d_Pe d_ZY d_ZYe d_zs d_zsc"
                 " d_u d_uc d_yo d_ye d_sn d_S d_tmp d_yst00 d_yst01 d_yst10 d_yst11 d_z d_seen")
        block = ctx.enter_context(nc.Block())
        q4 = lambda m: m[:].rearrange("p (j t) -> p j t", j=RT)
        b4 = lambda m: bc(m, [P, RT, P])
        pcs = [(0, 0), (64, 64)]

        @block.sync
        def _(sp):
            sp.wait_ge(s["d_z"], 1)
            with sp.Fori(0, NCH // 2) as i:
                for par in range(2):
                    n = 2 * i + par
                    for g in range(2):
                        w = n if g == 0 else NCH - 1 - n
                        sp.wait_ge(s["d_S"], 2 * n + g + 1)
                        sp.sem_inc(s["d_seen"], 1)
                        for h in range(2):
                            r = slice(h * HD, (h + 1) * HD)
                            sp.dma_start(bd[r, par, g, 0:4, :, r].rearrange("p k j t -> p (k j) t"), ops[g, bass.ds(w, 1), r, :, :, :].rearrange("o p k j t -> (o p) (k j) t"))\
                              .then_inc(s[f"d_ld{par}{g}"], 16)
                            sp.dma_start(bd[r, par, g, OP_V, :, r], vals[bass.ds(w, 1), r, :, :].rearrange("o p j t -> (o p) j t"))\
                              .then_inc(s[f"d_ld{par}{g}"], 16)

        @block.gpsimd
        def _(pool):
            identity(nc, pool, ident[:, 0, :], s["d_m"])
            k = 2
            for d in range(2):
                for tile, op in ((strict[:, d, :], ALU.is_gt), (upto[:, d, :], ALU.is_ge)):
                    pool.memset(tile, 1.0).then_inc(s["d_m"], 1)
                    k += 1
                    pool.wait_ge(s["d_m"], k)
                    sg = 1 - 2 * d
                    pool.affine_select(out=tile, in_=tile, compare_op=op, fill=0.0, base=0, pattern=[[sg, P]], channel_multiplier=-sg).then_inc(s["d_m"], 1)
                    k += 1
                for l, m in enumerate([1] + LEVELS):
                    tile = beside[:, d, l, :].rearrange("p (b x s) -> p b x s", x=2, s=m)
                    for x in range(2):
                        pool.memset(tile[:, :, x, :], float(x == d)).then_inc(s["d_m"], 1)
                        k += 1
                        pool.wait_ge(s["d_m"], k)
                    lo = m * (1 - d)
                    flat = beside[:, d, l, :]
                    for base, sg in ((-lo, 1), (lo + m - 1, -1)):
                        pool.affine_select(out=flat, in_=flat, compare_op=ALU.is_ge, fill=0.0, base=base,
                                           pattern=[[-sg * 2 * m, P // (2 * m)], [0, 2 * m]], channel_multiplier=sg).then_inc(s["d_m"], 1)
                        k += 1
                        pool.wait_ge(s["d_m"], k)
            pool.wait_ge(s["d_m"], k)
            pool.engine_nop().then_inc(s["d_dm"], 1)
            with pool.Fori(0, NCH) as n:
                for g in range(2):
                    pool.wait_ge(s["d_craw"], 2 * n + g + 1)
                    for m, k in ((ak, strict), (rb, upto), (rk, upto)):
                        last = pool.tensor_tensor(m[g][:], m[g][:], b4(k[:, g:g + 1, :]), ALU.mult)
                    last.then_inc(s["d_mask"], 1)

        @block.scalar
        def _(act):
            for k in ("00", "01", "10", "11"):
                act.sem_inc(s["d_yst" + k], 16)
            act.sem_inc(s["d_ye"], 2)
            with act.Fori(0, NCH // 2) as i:
                for par in range(2):
                    n = 2 * i + par
                    for g in range(2):
                        act.wait_ge(s["d_rest"], 2 * n + g + 1)
                        for k, m in ((1, rb), (2, ak), (3, rk)):
                            last = act.activation(m[g][:], q4(bank[g][k]), ACT.Copy)
                        last.then_inc(s["d_craw"], 1)
                    for g in range(2):
                        act.wait_ge(s["d_tt"], 2 * n + g + 1)
                        for k, m in ((1, tb), (2, tk), (3, tv)):
                            last = act.activation(m[g][:], q4(bank[g][k]), ACT.Copy)
                        last.then_inc(s["d_tc"], 1)
                    for g in range(2):
                        act.wait_ge(s["d_zs"], 2 * n + g + 1)
                        act.activation(zs[g][:], q4(bank[g][3]), ACT.Copy).then_inc(s["d_zsc"], 1)
                    for g in range(2):
                        act.wait_ge(s["d_u"], 2 * n + g + 1)
                        act.activation(uu[g][:], q4(bank[g][0]), ACT.Copy).then_inc(s["d_uc"], 1)
                    for g in range(2):
                        act.wait_ge(s["d_yo"], 2 * n + g + 1)
                        act.wait_ge(s[f"d_yst{par}{g}"], 16 * (i + 1))
                        for h in range(2):
                            r = slice(h * HD, (h + 1) * HD)
                            last = act.activation(y_out[r, par, g, :, :], q4(bank[g][1])[r, :, r], ACT.Copy)
                        last.then_inc(s["d_ye"], 1)
                        act.wait_ge(s["d_ye"], 2 * n + g + 3)
                        w = n if g == 0 else NCH - 1 - n
                        act.dma_start(yT[g, :, :, bass.ds(C * w, C)].rearrange("j p t -> p j t"), y_out[:, par, g, :, :]).then_inc(s[f"d_yst{par}{g}"], 16)
            for k in ("00", "01", "10", "11"):
                act.wait_ge(s["d_yst" + k], 16 * (NCH // 2 + 1))

        @block.vector
        def _(dve):
            dve.memset(bd[:].rearrange("p a b c d e -> p (a b c d e)"), 0.0)
            for g in range(2):
                dve.memset(st[g][:], 0.0)
            for d in range(2):
                last = dve.tensor_copy(decay[:, d, :, :].rearrange("p (b w) j -> p b w j", w=TB // C), WC[:, d, :, :].rearrange("p b (j w) -> p b w j", w=TB // C))
            last.then_inc(s["d_z"], 1)
            dve.wait_ge(s["d_z"], 1)
            for d, w in ((0, NS // C - 1), (1, NS // C)):
                last = dve.memset(decay[:, d, w, :], 0.0)
            last.then_inc(s["d_z"], 1)
            dve.wait_ge(s["d_z"], 2)
            dve.sem_inc(s["d_S"], 4)
            dve.wait_ge(s["d_dm"], 1)
            with dve.Fori(0, NCH) as n:
                for g in range(2):
                    dve.wait_ge(s["d_ab"], 2 * n + g + 1)
                    dve.tensor_tensor(bm[g][:], q4(bank[g][0]), b4(strict[:, g:g + 1, :]), ALU.mult).then_inc(s["d_bm"], 1)
                for g in range(2):
                    dve.wait_ge(s["d_bm"], 2 * n + g + 1)
                    dve.tensor_tensor(yy[g][:], bm[g][:], b4(beside[:, 1 - g, 0:1, :]), ALU.mult)
                    dve.wait_ge(s["d_ta"], 2 * n + g + 1)
                    dve.tensor_tensor(zz[g][:], q4(bank[g][0]), b4(beside[:, g, 0:1, :]), ALU.mult).then_inc(s["d_dch"], 1)
                    dve.wait_ge(s["d_dch"], 2 * n + g + 1)
                    dve.tensor_tensor(yy[g][:], yy[g][:], b4(ident[:]), ALU.add)
                    dve.tensor_tensor(zz[g][:], zz[g][:], b4(ident[:]), ALU.add).then_inc(s["d_init"], 1)
                dve.wait_ge(s["d_init"], 2 * n + 2)
                for l in range(NL):
                    for g in range(2):
                        dve.wait_ge(s["d_P"], 2 * NL * n + 2 * l + g + 1)
                        dve.tensor_tensor(pm[g][:], q4(bank[g][0]), b4(beside[:, g, l + 1:l + 2, :]), ALU.mult).then_inc(s["d_Pe"], 1)
                    for g in range(2):
                        dve.wait_ge(s["d_ZY"], 2 * NL * n + 2 * l + g + 1)
                        if l < NL - 1:
                            dve.tensor_tensor(zz[g][:], zz[g][:], q4(bank[g][1]), ALU.add)
                        dve.tensor_tensor(yy[g][:], yy[g][:], q4(bank[g][2]), ALU.add).then_inc(s["d_ZYe"], 1)
                for g in range(2):
                    dve.wait_ge(s["d_sn"], 2 * n + g + 1)
                    dve.tensor_tensor(tmp[g][:], st[g][:], q4(bank[g][2]), ALU.add).then_inc(s["d_tmp"], 1)
                    dve.wait_ge(s["d_tmp"], 2 * n + g + 1)
                    w = n if g == 0 else NCH - 1 - n
                    dve.sem_inc(s["d_seen"], 1)
                    dve.tensor_tensor(st[g][:], tmp[g][:], bc(decay[:, g, bass.ds(w, 1), :].rearrange("p o j -> p j o"), [P, RT, P]), ALU.mult).then_inc(s["d_S"], 1)

        @block.tensor
        def _(pe):
            pe.wait_ge(s["d_z"], 1)
            pe.wait_ge(s["d_dm"], 1)
            with pe.Fori(0, NCH // 2) as i:
                for par in range(2):
                    n = 2 * i + par
                    ln = 2 * NL * n
                    op = [[bd[:, par, g, k, :, :] for k in range(5)] for g in range(2)]

                    def products(g, to, pairs):
                        for j in range(RT):
                            for k, (l, r) in enumerate(pairs):
                                mm = pe.matmul(bank[g][to][:, j * P:(j + 1) * P], l[:, j, :], r[:, j, :], start=(k == 0), stop=(k == len(pairs) - 1))
                        return mm

                    def turned(g, to, a):
                        for j in range(RT):
                            mm = pe.transpose(bank[g][to][:, j * P:(j + 1) * P], a[:, j, :], ident[:, 0, :])
                        return mm

                    for g in range(2):
                        pe.wait_ge(s[f"d_ld{par}{g}"], 64 * (i + 1))
                        pe.wait_ge(s["d_ye"], 2 * n + g + 1)
                        pe.wait_ge(s["d_S"], 2 * n + g + 3)
                        products(g, 0, [(op[g][OP_B], op[g][OP_A])]).then_inc(s["d_ab"], 1)
                        products(g, 1, [(op[g][OP_B], op[g][OP_R])])
                        products(g, 2, [(op[g][OP_K], op[g][OP_A])])
                        products(g, 3, [(op[g][OP_K], op[g][OP_R])]).then_inc(s["d_rest"], 1)
                    for g in range(2):
                        pe.wait_ge(s["d_bm"], 2 * n + g + 1)
                        turned(g, 0, bm[g]).then_inc(s["d_ta"], 1)
                        pe.wait_ge(s["d_craw"], 2 * n + g + 1)
                        turned(g, 1, op[g][OP_B])
                        turned(g, 2, op[g][OP_K])
                        turned(g, 3, op[g][OP_V]).then_inc(s["d_tt"], 1)
                    for g in range(2):
                        pe.wait_ge(s["d_tc"], 2 * n + g + 1)
                        pe.wait_ge(s["d_mask"], 2 * n + g + 1)
                        products(g, 3, [(op[g][OP_A], st[g]), (ak[g], tv[g])]).then_inc(s["d_zs"], 1)
                    for l in range(NL):
                        for g in range(2):
                            if l == 0:
                                pe.wait_ge(s["d_init"], 2 * n + g + 1)
                            else:
                                pe.wait_ge(s["d_ZYe"], ln + 2 * (l - 1) + g + 1)
                            products(g, 0, [(bm[g], zz[g])]).then_inc(s["d_P"], 1)
                        for g in range(2):
                            pe.wait_ge(s["d_Pe"], ln + 2 * l + g + 1)
                            if l < NL - 1:
                                products(g, 1, [(yy[g], pm[g])])
                            products(g, 2, [(pm[g], yy[g])]).then_inc(s["d_ZY"], 1)
                    for g in range(2):
                        pe.wait_ge(s["d_ZYe"], ln + 2 * (NL - 1) + g + 1)
                        pe.wait_ge(s["d_zsc"], 2 * n + g + 1)
                        products(g, 0, [(yy[g], zs[g])]).then_inc(s["d_u"], 1)
                    for g in range(2):
                        pe.wait_ge(s["d_uc"], 2 * n + g + 1)
                        products(g, 1, [(st[g], op[g][OP_R]), (uu[g], rb[g]), (tv[g], rk[g])]).then_inc(s["d_yo"], 1)
                        products(g, 2, [(tb[g], uu[g]), (tk[g], tv[g])]).then_inc(s["d_sn"], 1)


NE = 16
GN_EPS = 64e-5


def mix_and_route(nc, x, w_out, ln_g, ln_b, norm2, w_router, yT, gateT, bonusT, mixT, out, hn_rows, logits):
    with ExitStack() as ctx:
        sb, ps, sems = opened(nc, ctx)
        w_raw = sb("e_wraw", [P, D])
        w_hi = sb("e_whi", [P, DC, D], F32R)
        w_lo = sb("e_wlo", [P, DC, D], F32R)
        gain = sb("e_gain", [P, D])
        wr = sb("e_wr", [P, DC, NE])
        ln = sb("e_ln", [P, 2, RT])
        eps = sb("e_eps", [P, 2])
        ident = sb("e_id", [P, P])
        mean1 = sb("e_mean1", [P, P])
        y2 = sb("e_y2", [P, 2, 2, RT, P])
        gb = sb("e_gb", [P, 2, 2, RT, P])
        at = sb("e_at", [P, 2, RT, P])
        x_in = sb("e_x", [P, 2, D])
        y = sb("e_y", [P, RT, P])
        dv = sb("e_dv", [P, RT, P])
        sq = sb("e_sq", [P, RT, P])
        sdv = sb("e_sdv", [P, RT, P])
        rw = sb("e_rw", [P, RT, P])
        mh = sb("e_mh", [P, 2, DC, P], F32R)
        ml = sb("e_ml", [P, 2, DC, P], F32R)
        h = sb("e_h", [P, 2, D])
        junk = sb("e_junk", [P, D])
        sm = sb("e_sm", [P, 4])
        hn = sb("e_hn", [P, 2, D])
        hT = sb("e_hT", [P, DC, P])
        lt = sb("e_lt", [P, P])
        pM = ps("e_pM")
        pV = ps("e_pV")
        pO = [ps(f"e_pO{k}") for k in range(2)]
        pT = [ps(f"e_pT{k}") for k in range(2)]
        pL = ps("e_pL")
        pR = ps("e_pR")
        s = sems("e_par e_cst e_wr e_hi e_lo e_ld0 e_ld1 e_free e_y e_mean e_dv e_sq e_var e_sd e_d1 e_d2 e_d3 e_d4 e_d5 e_rw e_mh e_ml e_ah e_al"
                 " e_o e_h e_ss e_sd2 e_rs e_hn e_st0 e_st1 e_tr e_hT e_lg e_lt e_lt2 e_lout e_mid e_mc e_x0 e_x1")
        block = ctx.enter_context(nc.Block())
        flat = lambda m: m.rearrange("p j t -> p (j t)")
        pj = lambda k: bc(ln[:, k, :].rearrange("p (j o) -> p j o", o=1), [P, RT, P])

        @block.sync
        def _(sp):
            sp.dma_start(gain[:], norm2.partition_broadcast(P)).then_inc(s["e_par"], 16)
            sp.dma_start(wr[:], w_router.rearrange("(c p) e -> p c e", p=P)).then_inc(s["e_par"], 16)
            for k, v in enumerate((ln_g, ln_b)):
                sp.dma_start(ln[:, k, :], v.rearrange("(j p) -> p j", p=P), allow_slow_non_contiguous=True).then_inc(s["e_par"], 16)
            for c in range(DC):
                if c:
                    sp.wait_ge(s["e_lo"], c)
                sp.dma_start(w_raw[:], w_out[c * P:(c + 1) * P, :]).then_inc(s["e_wr"], 16)

            def load(i, b):
                if live(i):
                    tok = bass.ds((2 * i + b) * P, P)
                    ld = s[f"e_ld{b}"]
                    sp.wait_ge(s["e_free"], 2 * i + b + 1)
                    sp.sem_inc(s["e_mid"], 1)
                    for d in range(2):
                        sp.dma_start(y2[:, b, d, :, :], yT[d, :, :, tok].rearrange("j p t -> p j t")).then_inc(ld, 16)
                    for k, v in enumerate((gateT, bonusT)):
                        sp.dma_start(gb[:, b, k, :, :], v[:, :, tok].rearrange("j p t -> p j t")).then_inc(ld, 16)
                    sp.dma_start(at[:, b, :, :], mixT[RW:, tok].rearrange("(j p) t -> p j t", p=P)).then_inc(ld, 16)

            def step(i, b):
                load(*lag(i, b, -1))
                if live(i):
                    sp.wait_ge(s["e_h"], 2 * i + b + 1)
                    sp.sem_inc(s["e_mid"], 1)
                    sp.dma_start(x_in[:, b, :], x[bass.ds((2 * i + b) * P, P), :]).then_inc(s[f"e_x{b}"], 16)

            load(0, 0)
            steps(sp, step)

        @block.gpsimd
        def _(pool):
            pool.memset(eps[:, 0:1], EPS).then_inc(s["e_cst"], 1)
            pool.memset(eps[:, 1:2], GN_EPS).then_inc(s["e_cst"], 1)
            identity(nc, pool, ident[:], s["e_mc"])
            for c in range(DC):
                pool.wait_ge(s["e_hi"], c + 1)
                pool.tensor_tensor(w_lo[:, c, :], w_raw[:], w_hi[:, c, :].bitcast(F32), ALU.subtract).then_inc(s["e_lo"], 1)

            def step(i, b):
                if live(i):
                    t = 2 * i + b
                    pool.wait_ge(s[f"e_ld{b}"], 80 * (i + 1))
                    pool.tensor_tensor(y[:], y2[:, b, 0, :, :], y2[:, b, 1, :, :], ALU.add).then_inc(s["e_y"], 1)
                    pool.wait_ge(s["e_dv"], t + 1)
                    pool.tensor_tensor(sq[:], dv[:], dv[:], ALU.mult).then_inc(s["e_sq"], 1)
                    pool.wait_ge(s["e_ah"], t + 1)
                    pool.tensor_tensor(ml[:, b, RT:, :], at[:, b, :, :], mh[:, b, RT:, :].bitcast(F32), ALU.subtract).then_inc(s["e_al"], 1)

            steps(pool, step)

        @block.scalar
        def _(act):
            for c in range(DC):
                act.wait_ge(s["e_wr"], 16 * (c + 1))
                act.activation(w_hi[:, c, :], w_raw[:], ACT.Copy).then_inc(s["e_hi"], 1)
            act.wait_ge(s["e_cst"], 2)
            act.wait_ge(s["e_d5"], 1)
            for b in range(2):
                act.sem_inc(s[f"e_st{b}"], 32)

            def square(i, b):
                if live(i):
                    t = 2 * i + b
                    act.wait_ge(s["e_h"], t + 3)
                    act.activation(junk[:], h[:, b, :], ACT.Square, accum_out=sm[:, 0:1]).then_inc(s["e_ss"], 1)
                    act.wait_ge(s["e_ss"], t + 1)
                    act.activation(sm[:, 1:2], sm[:, 0:1], ACT.Sqrt, bias=eps[:, 0:1], scale=1.0 / D).then_inc(s["e_sd2"], 1)

            def attention_high(i, b):
                if live(i):
                    act.wait_ge(s[f"e_ld{b}"], 80 * (i + 1))
                    act.wait_ge(s["e_o"], 2 * i + b + 1)
                    act.activation(mh[:, b, RT:, :], at[:, b, :, :], ACT.Copy).then_inc(s["e_ah"], 1)

            def rwkv_high(i, b):
                if live(i):
                    t = 2 * i + b
                    act.wait_ge(s["e_var"], t + 1)
                    act.activation(flat(sdv[:]), pV[:], ACT.Sqrt, bias=eps[:, 1:2]).then_inc(s["e_sd"], 1)
                    act.wait_ge(s["e_rw"], t + 1)
                    act.activation(mh[:, b, 0:RT, :], rw[:], ACT.Copy).then_inc(s["e_mh"], 1)

            def store(i, b):
                if live(i):
                    t = 2 * i + b
                    act.wait_ge(s["e_hn"], t + 1)
                    tok = bass.ds(t * P, P)
                    act.dma_start(out[tok, :], h[:, b, :]).then_inc(s[f"e_st{b}"], 16)
                    act.dma_start(hn_rows[tok, :], hn[:, b, :]).then_inc(s[f"e_st{b}"], 16)

            def turned(i, b):
                if live(i):
                    t = 2 * i + b
                    act.wait_ge(s["e_tr"], t + 1)
                    for k in range(2):
                        last = act.activation(hT[:, 4 * k:4 * k + 4, :], pT[k][:].rearrange("p (c t) -> p c t", c=4), ACT.Copy)
                    last.then_inc(s["e_hT"], 1)

            def logits_out(i, b):
                if live(i):
                    t = 2 * i + b
                    act.wait_ge(s["e_lg"], t + 1)
                    act.activation(lt[0:NE, :], pL[0:NE, 0:P], ACT.Copy).then_inc(s["e_lt"], 1)

            def step(i, b):
                square(*lag(i, b, 2))
                attention_high(i, b)
                logits_out(*lag(i, b, 3))
                store(*lag(i, b, 2))
                rwkv_high(i, b)
                turned(*lag(i, b, 2))

            steps(act, step)
            for b in range(2):
                act.wait_ge(s[f"e_st{b}"], 32 * (NT // 2 + 1))

        @block.vector
        def _(dve):
            for a in range(2):
                for g in range(2):
                    last = dve.memset(mean1[a * HD:a * HD + HD, g * HD:g * HD + HD], (a == g) / HD)
            dve.memset(lt[:], 0.0)
            last = dve.memset(sm[:], 0.0)
            last.then_inc(s["e_d5"], 1)
            dve.sem_inc(s["e_free"], 2)
            dve.wait_ge(s["e_par"], 64)
            dve.sem_inc(s["e_h"], 2)

            def residual(i, b):
                if live(i):
                    dve.wait_ge(s["e_o"], 2 * i + b + 3)
                    dve.wait_ge(s[f"e_x{b}"], 16 * (i + 1))
                    dve.wait_ge(s[f"e_st{b}"], 32 * (i + 1))
                    for k in range(2):
                        last = dve.tensor_tensor(h[:, b, k * 512:(k + 1) * 512], x_in[:, b, k * 512:(k + 1) * 512], pO[k][:], ALU.add)
                    last.then_inc(s["e_h"], 1)

            def centre(i, b):
                if live(i):
                    dve.wait_ge(s["e_mean"], 2 * i + b + 1)
                    dve.tensor_tensor(flat(dv[:]), flat(y[:]), pM[:], ALU.subtract).then_inc(s["e_dv"], 1)

            def normed(i, b):
                if live(i):
                    t = 2 * i + b
                    dve.wait_ge(s["e_sd2"], t + 1)
                    dve.reciprocal(sm[:, 2:3], sm[:, 1:2]).then_inc(s["e_rs"], 1)
                    dve.wait_ge(s["e_rs"], t + 1)
                    dve.scalar_tensor_tensor(out=hn[:, b, :], in0=h[:, b, :], scalar=sm[:, 2:3], in1=gain[:], op0=ALU.mult, op1=ALU.mult)\
                       .then_inc(s["e_hn"], 1)

            def rwkv(i, b):
                if live(i):
                    t = 2 * i + b
                    dve.wait_ge(s["e_sd"], t + 1)
                    dve.reciprocal(sdv[:], sdv[:]).then_inc(s["e_d1"], 1)
                    dve.wait_ge(s["e_d1"], t + 1)
                    dve.tensor_tensor(rw[:], dv[:], sdv[:], ALU.mult).then_inc(s["e_d2"], 1)
                    dve.wait_ge(s["e_d2"], 4 * t + 1)
                    dve.tensor_tensor(rw[:], rw[:], pj(0), ALU.mult).then_inc(s["e_d2"], 1)
                    dve.wait_ge(s["e_d2"], 4 * t + 2)
                    dve.tensor_tensor(rw[:], rw[:], pj(1), ALU.add).then_inc(s["e_d2"], 1)
                    dve.wait_ge(s["e_d2"], 4 * t + 3)
                    dve.tensor_tensor(rw[:], rw[:], gb[:, b, 1, :, :], ALU.add).then_inc(s["e_d2"], 1)
                    dve.wait_ge(s["e_d2"], 4 * t + 4)
                    dve.tensor_tensor(rw[:], rw[:], gb[:, b, 0, :, :], ALU.mult).then_inc(s["e_rw"], 1)
                    dve.wait_ge(s["e_rw"], t + 1)
                    dve.wait_ge(s["e_al"], t + 1)
                    dve.sem_inc(s["e_free"], 1)
                    dve.wait_ge(s["e_mh"], t + 1)
                    dve.tensor_tensor(ml[:, b, 0:RT, :], rw[:], mh[:, b, 0:RT, :].bitcast(F32), ALU.subtract).then_inc(s["e_ml"], 1)

            def logits_in(i, b):
                if live(i):
                    t = 2 * i + b
                    dve.wait_ge(s["e_lt2"], t + 1)
                    dve.tensor_copy(logits[:, bass.ds(t, 1), :], pR[:, 0:NE].rearrange("p (o e) -> p o e", o=1)).then_inc(s["e_lout"], 1)

            def step(i, b):
                residual(*lag(i, b, 2))
                centre(i, b)
                logits_in(*lag(i, b, 4))
                normed(*lag(i, b, 2))
                rwkv(i, b)

            steps(dve, step)

        @block.tensor
        def _(pe):
            pe.wait_ge(s["e_d5"], 1)
            pe.wait_ge(s["e_mc"], 2)
            pe.wait_ge(s["e_lo"], DC)
            pe.wait_ge(s["e_par"], 64)
            pe.sem_inc(s["e_o"], 2)

            def product(i, b, k):
                if live(i):
                    t = 2 * i + b
                    if k == 0:
                        pe.wait_ge(s["e_ml"], t + 1)
                        pe.wait_ge(s["e_al"], t + 1)
                        pe.wait_ge(s["e_h"], t + 2)
                    for c in range(DC):
                        for q, (l, r) in enumerate(((mh, w_hi), (mh, w_lo), (ml, w_hi))):
                            mm = pe.matmul(pO[k][:], l[:, b, c, :], r[:, c, k * 512:(k + 1) * 512], start=(c == 0 and q == 0), stop=(c == DC - 1 and q == 2))
                    if k:
                        mm.then_inc(s["e_o"], 1)

            def step(i, b):
                if live(i):
                    pe.wait_ge(s["e_y"], 2 * i + b + 1)
                    pe.matmul(pM[:], mean1[:], flat(y[:]), start=True, stop=True).then_inc(s["e_mean"], 1)
                il, bl = lag(i, b, 3)
                if live(il):
                    pe.wait_ge(s["e_hT"], 2 * il + bl + 1)
                    for c in range(DC):
                        mm = pe.matmul(pL[0:NE, 0:P], wr[:, c, :], hT[:, c, :], start=(c == 0), stop=(c == DC - 1))
                    mm.then_inc(s["e_lg"], 1)
                product(*lag(i, b, 1), 0)
                if live(i):
                    pe.wait_ge(s["e_sq"], 2 * i + b + 1)
                    pe.matmul(pV[:], mean1[:], flat(sq[:]), start=True, stop=True).then_inc(s["e_var"], 1)
                product(*lag(i, b, 1), 1)
                if live(il):
                    pe.wait_ge(s["e_lt"], 2 * il + bl + 1)
                    pe.wait_ge(s["e_lout"], 2 * il + bl + 1)
                    pe.transpose(pR[:, 0:P], lt[:], ident[:]).then_inc(s["e_lt2"], 1)
                i2, b2 = lag(i, b, 2)
                if live(i2):
                    pe.wait_ge(s["e_hn"], 2 * i2 + b2 + 1)
                    for c in range(DC):
                        mm = pe.transpose(pT[c // 4][:, (c % 4) * P:(c % 4 + 1) * P], hn[:, b2, c * P:(c + 1) * P], ident[:])
                    mm.then_inc(s["e_tr"], 1)

            pe.sem_inc(s["e_lout"], 1)
            steps(pe, step)


F = 1024
CAP_S, CAP_P = 2 * NS // NE, 2 * NP_ // NE
CAP = CAP_S + CAP_P
TS, TP = NS // P, NP_ // P
G2 = 2 * NE
BITS = 30
FAR = 4096.0


def choose(nc, logits, aff_rows, index):
    with ExitStack() as ctx:
        sb, ps, sems = opened(nc, ctx)
        aff = sb("f_aff", [P, NT, NE])
        mxv = sb("f_mx", [P, NT])
        den = sb("f_den", [P, NT])
        A = sb("f_A", [P, G2, TS])
        cmp_ = sb("f_cmp", [P, G2, TS])
        cnt = sb("f_cnt", [P, G2])
        cap = sb("f_cap", [P, G2])
        low = sb("f_low", [P, G2], I32)
        cand = sb("f_cand", [P, G2], I32)
        bit = sb("f_bit", [P, 2], I32)
        bits = sb("f_bits", [P, G2], I32)
        ge = sb("f_ge", [P, G2])
        mask = sb("f_mask", [P, G2], I32)
        onesf = sb("f_ones", [P, P])
        onesb = sb("f_onesb", [P, P], BF16)
        before = sb("f_before", [P, P], BF16)
        beforef = sb("f_beforef", [P, P])
        notfirst = sb("f_nf", [P, G2 * TS])
        selb = sb("f_selb", [P, G2, TS], BF16)
        cum = sb("f_cum", [P, G2, TS])
        cumb = sb("f_cumb", [P, G2, TS], BF16)
        gt = sb("f_gt", [P, G2, TS])
        eq = sb("f_eq", [P, G2, TS])
        need = sb("f_need", [P, G2])
        pos = sb("f_pos", [P, G2, TS])
        iota_i = sb("f_iota", [P, CAP_S], I32)
        slots = sb("f_slots", [P, CAP_S], BF16)
        ids_i = sb("f_idsi", [P, NT, 2], I32)
        ids = sb("f_ids", [P, NT, 2], BF16)
        hot = sb("f_hot", [P, 2, TS + TP, CAP_S], BF16)
        two = sb("f_two", [P, 3, 2])
        idf = sb("f_idf", [P, 3])
        pC = ps("f_pC")
        pP = ps("f_pP")
        pI = [ps(f"f_pI{k}") for k in range(3)]
        s = sems("f_c f_v f_mx f_sub f_exp f_count f_cnt f_pre f_pos f_hot f_id f_idv f_st f_hused f_idd")
        block = ctx.enter_context(nc.Block())
        g3 = lambda m: bc(m.rearrange("p (g o) -> p g o", o=1), [P, G2, TS])
        fl = lambda m: m[:].rearrange("p g t -> p (g t)")

        @block.gpsimd
        def _(pool):
            pool.iota(iota_i[:], pattern=[[1, CAP_S]], base=0, channel_multiplier=0).then_inc(s["f_c"], 1)
            pool.iota(ids_i[:, :, 0:1], pattern=[[1, NT], [0, 1]], base=0, channel_multiplier=0).then_inc(s["f_c"], 1)
            pool.iota(ids_i[:, :, 1:2], pattern=[[0, NT], [0, 1]], base=0, channel_multiplier=1).then_inc(s["f_c"], 1)
            pool.memset(beforef[:], 1.0).then_inc(s["f_c"], 1)
            pool.wait_ge(s["f_c"], 4)
            pool.affine_select(out=beforef[:], in_=beforef[:], compare_op=ALU.is_gt, fill=0.0, base=0, pattern=[[1, P]], channel_multiplier=-1).then_inc(s["f_c"], 1)

        @block.sync
        def _(sp):
            sp.wait_ge(s["f_sub"], 2)
            sp.dma_start(aff_rows.rearrange("(t p) e -> p t e", p=P), aff[:]).then_inc(s["f_st"], 16)
            sp.wait_ge(s["f_st"], 16)

        @block.scalar
        def _(act):
            act.wait_ge(s["f_sub"], 1)
            act.activation(aff[:], aff[:], ACT.Exp).then_inc(s["f_exp"], 1)

        @block.vector
        def _(dve):
            v = 0

            def did(ins):
                nonlocal v
                v += 1
                ins.then_inc(s["f_v"], 1)
                dve.wait_ge(s["f_v"], v)

            dve.memset(cap[:, 0:NE], float(CAP_S))
            dve.memset(cap[:, NE:], float(CAP_P))
            dve.memset(onesf[:], 1.0)
            dve.memset(low[:], 0)
            dve.memset(bit[:], 1 << (BITS - 1))
            dve.memset(two[:], 0.0)
            dve.memset(notfirst[:].rearrange("p (g t) -> p g t", t=TS)[:, :, 1:], 1.0)
            dve.memset(notfirst[:].rearrange("p (g t) -> p g t", t=TS)[:, :, 0:1], 0.0)
            did(dve.memset(A[:, NE:, TP:], -1.0))
            dve.tensor_copy(onesb[:], onesf[:])
            dve.wait_ge(s["f_c"], 5)
            dve.tensor_copy(before[:], beforef[:])
            dve.tensor_copy(slots[:], iota_i[:])
            dve.tensor_copy(ids[:], ids_i[:])
            did(dve.tensor_reduce(mxv[:], logits[:], AX.X, ALU.max))
            dve.tensor_tensor(aff[:], logits[:], bc(mxv[:].rearrange("p (t o) -> p t o", o=1), [P, NT, NE]), ALU.subtract).then_inc(s["f_sub"], 1)
            dve.wait_ge(s["f_exp"], 1)
            did(dve.tensor_reduce(den[:], aff[:], AX.X, ALU.add))
            did(dve.reciprocal(den[:], den[:]))
            dve.tensor_tensor(aff[:], aff[:], bc(den[:].rearrange("p (t o) -> p t o", o=1), [P, NT, NE]), ALU.mult).then_inc(s["f_sub"], 1)
            dve.wait_ge(s["f_sub"], 2)
            dve.tensor_copy(A[:, 0:NE, :], aff[:, 0:TS, :].rearrange("p t e -> p e t"))
            did(dve.tensor_copy(A[:, NE:, 0:TP], aff[:, TS:, :].rearrange("p t e -> p e t")))
            base = v
            with dve.Fori(0, BITS) as r:
                def at(k):
                    dve.wait_ge(s["f_v"], 8 * r + base + k)
                dve.scalar_tensor_tensor(out=cand[:], in0=low[:], scalar=bit[:, 0:1], in1=low[:], op0=ALU.bitwise_or, op1=ALU.bitwise_or).then_inc(s["f_v"], 1)
                at(1)
                dve.tensor_tensor(cmp_[:], A[:], g3(cand[:].bitcast(F32)), ALU.is_ge).then_inc(s["f_v"], 1)
                at(2)
                dve.tensor_reduce(cnt[:], cmp_[:], AX.X, ALU.add).then_inc(s["f_cnt"], 1)
                dve.wait_ge(s["f_count"], r + 1)
                dve.tensor_tensor(ge[:], pC[:, 0:G2], cap[:], ALU.is_ge).then_inc(s["f_v"], 1)
                at(3)
                dve.tensor_scalar(mask[:], ge[:], -1.0, None, ALU.mult).then_inc(s["f_v"], 1)
                at(4)
                dve.tensor_scalar(bits[:], mask[:], bit[:, 0:1], None, ALU.bitwise_and).then_inc(s["f_v"], 1)
                at(5)
                dve.tensor_tensor(low[:], low[:], bits[:], ALU.bitwise_or).then_inc(s["f_v"], 1)
                at(6)
                dve.tensor_scalar(bit[:, 1:2], bit[:, 0:1], 1, None, ALU.logical_shift_right).then_inc(s["f_v"], 1)
                at(7)
                dve.tensor_copy(bit[:, 0:1], bit[:, 1:2]).then_inc(s["f_v"], 1)
                at(8)
            v = base + 8 * BITS
            least = g3(low[:].bitcast(F32))
            dve.tensor_tensor(gt[:], A[:], least, ALU.is_gt)
            did(dve.tensor_tensor(eq[:], A[:], least, ALU.is_equal))
            dve.tensor_reduce(cnt[:], gt[:], AX.X, ALU.add).then_inc(s["f_cnt"], 1)

            def prefix(m, k):
                did(dve.tensor_tensor_scan(fl(cum), notfirst[:], fl(m), 0.0, ALU.mult, ALU.add))
                dve.tensor_copy(selb[:], m[:])
                dve.tensor_tensor(cumb[:], cum[:], m[:], ALU.subtract).then_inc(s["f_pre"], 1)
                dve.wait_ge(s["f_pos"], k)

            prefix(eq, 1)
            dve.wait_ge(s["f_count"], BITS + 1)
            did(dve.tensor_tensor(need[:], cap[:], pC[:, 0:G2], ALU.subtract))
            did(dve.tensor_tensor(pos[:], g3(need[:]), pP[:].rearrange("p (g t) -> p g t", g=G2), ALU.is_gt))
            did(dve.tensor_tensor(eq[:], eq[:], pos[:], ALU.mult))
            did(dve.tensor_tensor(gt[:], gt[:], eq[:], ALU.add))
            prefix(gt, 2)
            did(dve.tensor_scalar(pos[:], pP[:].rearrange("p (g t) -> p g t", g=G2), -FAR, None, ALU.add))
            did(dve.tensor_tensor(pos[:], pos[:], gt[:], ALU.mult))
            did(dve.tensor_scalar(pos[:], pos[:], FAR, None, ALU.add))
            dve.sem_inc(s["f_idd"], 1)
            with dve.Fori(0, NE // 2) as i:
                for b in range(2):
                    e = 2 * i + b
                    dve.wait_ge(s["f_hused"], e + 1)
                    for t in range(TS):
                        dve.tensor_scalar(hot[:, b, t, :], slots[:], pos[:, bass.ds(e, 1), t:t + 1].rearrange("p a b -> p (a b)"), None, ALU.is_equal)
                    for t in range(TP):
                        last = dve.tensor_scalar(hot[:, b, TS + t, 0:CAP_P], slots[:, 0:CAP_P], pos[:, bass.ds(NE + e, 1), t:t + 1].rearrange("p a b -> p (a b)"), None, ALU.is_equal)
                    last.then_inc(s["f_hot"], 1)
                    dve.wait_ge(s["f_id"], e + 1)
                    dve.tensor_copy(two[:, 0, :], pI[0][:, 0:2])
                    dve.tensor_copy(two[:, 1, :], pI[1][:, 0:2])
                    dve.tensor_copy(two[0:CAP_P, 2, :], pI[2][0:CAP_P, 0:2]).then_inc(s["f_idv"], 1)
                    dve.wait_ge(s["f_idv"], e + 1)
                    dve.scalar_tensor_tensor(out=idf[:], in0=two[:, :, 0], scalar=float(P), in1=two[:, :, 1], op0=ALU.mult, op1=ALU.add).then_inc(s["f_idd"], 1)
                    dve.wait_ge(s["f_idd"], 2 * e + 2)
                    dve.tensor_copy(index[:, bass.ds(e, 1), :], idf[:].rearrange("p (o k) -> p o k", o=1)).then_inc(s["f_idd"], 1)

        @block.tensor
        def _(pe):
            pe.wait_ge(s["f_v"], 1)
            with pe.Fori(0, BITS) as r:
                pe.wait_ge(s["f_cnt"], r + 1)
                pe.matmul(pC[:, 0:G2], onesf[:], cnt[:], start=True, stop=True).then_inc(s["f_count"], 1)
            pe.wait_ge(s["f_cnt"], BITS + 1)
            pe.matmul(pC[:, 0:G2], onesf[:], cnt[:], start=True, stop=True).then_inc(s["f_count"], 1)
            for k in range(2):
                pe.wait_ge(s["f_pre"], k + 1)
                pe.matmul(pP[:], before[:], fl(selb), start=True, stop=False)
                pe.matmul(pP[:], onesb[:], fl(cumb), start=False, stop=True).then_inc(s["f_pos"], 1)
            pe.sem_inc(s["f_hused"], 2)
            with pe.Fori(0, NE // 2) as i:
                for b in range(2):
                    e = 2 * i + b
                    pe.wait_ge(s["f_hot"], e + 1)
                    pe.wait_ge(s["f_idd"], 2 * e + 1)
                    for k in range(2):
                        for t in range(TS):
                            pe.matmul(pI[k][:, 0:2], hot[:, b, t, k * P:(k + 1) * P], ids[:, t, :], start=(t == 0), stop=(t == TS - 1))
                    for t in range(TP):
                        mm = pe.matmul(pI[2][0:CAP_P, 0:2], hot[:, b, TS + t, 0:CAP_P], ids[:, TS + t, :], start=(t == 0), stop=(t == TP - 1))
                    mm.then_inc(s["f_id"], 1)
                    pe.wait_ge(s["f_id"], e + 1)
                    pe.sem_inc(s["f_hused"], 1)


WB = 256
NWB = F // WB
SLOT = [(0, P), (1, P), (2, CAP_P)]


def experts(nc, w_gate, w_up, w_down, hn_rows, aff_rows, index, out):
    with ExitStack() as ctx:
        sb, ps, sems = opened(nc, ctx)
        ident = sb("g_id", [P, P])
        raw = sb("g_raw", [P, 2, DC, WB])
        w_hi = sb("g_whi", [P, 2, DC, WB], F32R)
        w_lo = sb("g_wlo", [P, 2, DC, WB], F32R)
        idx_in = sb("g_idxi", [P, 3], U32)
        idx_out = sb("g_idxo", [P, 3], U32)
        rows = [sb(f"g_x{k}", [P, D]) for k in range(3)]
        gates = [sb(f"g_g{k}", [P, NE]) for k in range(3)]
        gate = sb("g_gate", [P, 2, 3])
        xh = sb("g_xh", [P, DC, CAP], F32R)
        xl = sb("g_xl", [P, DC, CAP], F32R)
        sg = sb("g_sg", [P, 2, CAP])
        hid = sb("g_hid", [P, 2, CAP])
        hh = sb("g_hh", [P, DC, CAP], F32R)
        hl = sb("g_hl", [P, DC, CAP], F32R)
        o = [sb(f"g_o{k}", [P, D]) for k in range(3)]
        pG = [ps(f"g_pG{k}") for k in range(2)]
        pU = [ps(f"g_pU{k}") for k in range(2)]
        pD = [ps(f"g_pD{k}") for k in range(3)]
        pT = pG + pU
        s = sems("g_c g_w0 g_w1 g_hi g_lo g_gu g_sg g_t g_hid g_hh g_hl g_ga g_tr g_xh g_xl g_dn g_dv g_sc g_seen g_idx g_i2 g_gt g_wfree g_ofree g_mark g_pad")
        block = ctx.enter_context(nc.Block())
        mats = (w_gate, w_up, w_down)
        plan = [(m, c) for c in range(NWB) for m in (0, 1)] + [(2, c) for c in range(NWB)]
        NBK = len(plan)
        NTR = 6
        chunks = [(k, n, c) for k, n in SLOT for c in range(DC)]

        @block.sync
        def _(sp):
            with sp.Fori(0, NE) as e:
                for q, (m, c) in enumerate(plan):
                    sp.wait_ge(s["g_wfree"], NBK * e + q + 1)
                    sp.sem_inc(s["g_seen"], 1)
                    sp.dma_start(raw[:, q % 2, :, :], mats[m][bass.ds(e, 1), :, c * WB:(c + 1) * WB].rearrange("o (k p) f -> p (o k) f", p=P))\
                      .then_inc(s[f"g_w{q % 2}"], 16)

        @block.gpsimd
        def _(pool):
            identity(nc, pool, ident[:], s["g_c"])

            def gather(e, before):
                pool.tensor_copy(idx_in[:, :], index[:, bass.ds(e, 1), :].rearrange("p o k -> p (o k)")).then_inc(s["g_idx"], 1)
                pool.wait_ge(s["g_idx"], before + 1)
                pool.sem_inc(s["g_mark"], 1)
                for k, n in SLOT:
                    pool.indirect_dma_start(rows[k][0:n, :], None, hn_rows, bass.IndirectOffsetOnAxis(ap=idx_in[0:n, k:k + 1], axis=0)).then_inc(s["g_ga"], 16)
                for k, n in SLOT:
                    pool.indirect_dma_start(gates[k][0:n, :], None, aff_rows, bass.IndirectOffsetOnAxis(ap=idx_in[0:n, k:k + 1], axis=0)).then_inc(s["g_ga"], 16)

            def scatter(e):
                pool.tensor_copy(idx_out[:, :], index[:, bass.ds(e, 1), :].rearrange("p o k -> p (o k)")).then_inc(s["g_i2"], 1)
                pool.wait_ge(s["g_i2"], e + 1)
                pool.wait_ge(s["g_dv"], 3 * NWB * (e + 1) + 3)
                pool.sem_inc(s["g_mark"], 1)
                for k, n in SLOT:
                    pool.indirect_dma_start(out, bass.IndirectOffsetOnAxis(ap=idx_out[0:n, k:k + 1], axis=0), o[k][0:n, :], None,
                                            compute_op=ALU.add).then_inc(s["g_sc"], 16)
                pool.wait_ge(s["g_sc"], 48 * (e + 1))
                pool.sem_inc(s["g_ofree"], 1)

            gather(0, 0)
            with pool.Fori(0, NE - 1) as e:
                pool.wait_ge(s["g_tr"], NTR * (e + 1))
                pool.wait_ge(s["g_gt"], e + 1)
                gather(e + 1, e + 1)
                scatter(e)
            scatter(NE - 1)

        @block.scalar
        def _(act):
            act.sem_inc(s["g_dv"], 3)
            act.sem_inc(s["g_gu"], 2)
            with act.Fori(0, NE) as e:
                def high(q):
                    act.wait_ge(s[f"g_w{q % 2}"], 16 * (NBK // 2 * e + q // 2 + 1))
                    act.wait_ge(s["g_gu"], NBK * e + q + 1)
                    act.activation(w_hi[:, q % 2, :, :], raw[:, q % 2, :, :], ACT.Copy).then_inc(s["g_hi"], 1)

                high(0)
                for r in range(NTR):
                    act.wait_ge(s["g_tr"], NTR * e + r + 1)
                    k, n, c = chunks[4 * r]
                    act.activation(xh[:, c:c + 4, k * P:k * P + n], pT[r % 4][:].rearrange("p (c t) -> p c t", c=4)[:, :, 0:n], ACT.Copy).then_inc(s["g_xh"], 1)
                for q, (m, c) in enumerate(plan):
                    if q + 1 < NBK:
                        high(q + 1)
                    if m == 1:
                        act.wait_ge(s["g_gu"], NBK * e + q + 2)
                        for k in range(2):
                            last = act.activation(sg[:, k, :], pG[k][:, 0:CAP], ACT.Sigmoid)
                        last.then_inc(s["g_sg"], 1)
                        act.wait_ge(s["g_hid"], NWB * e + c + 2)
                        act.activation(hh[:, 2 * c:2 * c + 2, :], hid[:], ACT.Copy).then_inc(s["g_hh"], 1)
                    if m == 2:
                        if c == 0:
                            act.wait_ge(s["g_ofree"], e + 1)
                            act.wait_ge(s["g_gt"], e + 1)
                        for k, n in SLOT:
                            act.wait_ge(s["g_dn"], 3 * (NWB * e + c) + k + 1)
                            act.activation(o[k][0:n, c * WB:(c + 1) * WB], pD[k][0:n, 0:WB], ACT.Copy, scale=gate[0:n, 0, k:k + 1]).then_inc(s["g_dv"], 1)

        @block.vector
        def _(dve):
            dve.sem_inc(s["g_wfree"], 2)
            dve.sem_inc(s["g_hid"], 1)
            dve.sem_inc(s["g_ofree"], 1)
            dve.memset(rows[2][CAP_P:, :], 0.0).then_inc(s["g_pad"], 1)
            with dve.Fori(0, NE) as e:
                def low(q):
                    dve.wait_ge(s["g_hi"], NBK * e + q + 1)
                    dve.tensor_tensor(w_lo[:, q % 2, :, :], raw[:, q % 2, :, :], w_hi[:, q % 2, :, :].bitcast(F32), ALU.subtract).then_inc(s["g_lo"], 1)
                    dve.wait_ge(s["g_lo"], NBK * e + q + 1)
                    dve.sem_inc(s["g_wfree"], 1)

                low(0)
                dve.wait_ge(s["g_ga"], 96 * (e + 1))
                dve.wait_ge(s["g_dv"], 3 * NWB * e + 3)
                for k, n in SLOT:
                    last = dve.tensor_copy(gate[0:n, 0, k:k + 1], gates[k][0:n, bass.ds(e, 1)])
                last.then_inc(s["g_gt"], 1)
                for r in range(NTR):
                    dve.wait_ge(s["g_xh"], NTR * e + r + 1)
                    k, n, c = chunks[4 * r]
                    dve.tensor_tensor(xl[:, c:c + 4, k * P:k * P + n], pT[r % 4][:].rearrange("p (c t) -> p c t", c=4)[:, :, 0:n],
                                      xh[:, c:c + 4, k * P:k * P + n].bitcast(F32), ALU.subtract).then_inc(s["g_xl"], 1)
                for q, (m, c) in enumerate(plan):
                    if q + 1 < NBK:
                        low(q + 1)
                    if m == 1:
                        dve.wait_ge(s["g_sg"], NWB * e + c + 1)
                        for k in range(2):
                            last = dve.tensor_tensor(sg[:, k, :], sg[:, k, :], pG[k][:, 0:CAP], ALU.mult)
                        last.then_inc(s["g_t"], 1)
                        dve.wait_ge(s["g_t"], NWB * e + c + 1)
                        dve.wait_ge(s["g_gu"], NBK * e + q + 3)
                        for k in range(2):
                            last = dve.tensor_tensor(hid[:, k, :], sg[:, k, :], pU[k][:, 0:CAP], ALU.mult)
                        last.then_inc(s["g_hid"], 1)
                        dve.wait_ge(s["g_hh"], NWB * e + c + 1)
                        dve.tensor_tensor(hl[:, 2 * c:2 * c + 2, :], hid[:], hh[:, 2 * c:2 * c + 2, :].bitcast(F32), ALU.subtract).then_inc(s["g_hl"], 1)

        @block.tensor
        def _(pe):
            pe.wait_ge(s["g_c"], 2)
            pe.wait_ge(s["g_pad"], 1)
            with pe.Fori(0, NE) as e:
                pe.wait_ge(s["g_ga"], 96 * (e + 1))
                pe.wait_ge(s["g_hid"], NWB * e + 1)
                for r in range(NTR):
                    if r >= 4:
                        pe.wait_ge(s["g_xl"], NTR * e + r - 3)
                    for j, (k, n, c) in enumerate(chunks[4 * r:4 * r + 4]):
                        mm = pe.transpose(pT[r % 4][:, j * P:(j + 1) * P], rows[k][:, c * P:(c + 1) * P], ident[:])
                    mm.then_inc(s["g_tr"], 1)
                pe.wait_ge(s["g_xl"], NTR * (e + 1))
                for q, (m, c) in enumerate(plan):
                    pe.wait_ge(s["g_lo"], NBK * e + q + 1)
                    if m < 2:
                        if m == 0:
                            pe.wait_ge(s["g_hid"], NWB * e + c + 1)
                        for k in range(2):
                            for d in range(DC):
                                for j, (w, x) in enumerate(((w_hi, xh), (w_hi, xl), (w_lo, xh))):
                                    mm = pe.matmul((pG, pU)[m][k][:, 0:CAP], w[:, q % 2, d, k * P:(k + 1) * P], x[:, d, :], start=(d == 0 and j == 0),
                                                   stop=(d == DC - 1 and j == 2))
                        mm.then_inc(s["g_gu"], 1)
                    else:
                        if c == 0:
                            pe.wait_ge(s["g_hl"], NWB * (e + 1))
                        for k, n in SLOT:
                            pe.wait_ge(s["g_dv"], 3 * (NWB * e + c) + k + 1)
                            for d in range(DC):
                                for j, (x, w) in enumerate(((hh, w_hi), (hh, w_lo), (hl, w_hi))):
                                    mm = pe.matmul(pD[k][0:n, 0:WB], x[:, d, k * P:k * P + n], w[:, q % 2, d, :], start=(d == 0 and j == 0),
                                                   stop=(d == DC - 1 and j == 2))
                            mm.then_inc(s["g_dn"], 1)
                        pe.wait_ge(s["g_dn"], 3 * (NWB * e + c + 1))
                        pe.sem_inc(s["g_gu"], 1)


def program(nc, ins, out):
    dram = lambda name, shape: nc.dram_tensor(name, list(shape), F32).ap()
    xT_hi, xT_lo = dram("xT_hi", [DC, P, NCOL]), dram("xT_lo", [DC, P, NCOL])
    qT = dram("qT", [NT, P, QH * P])
    mixT = dram("mixT", [D, N])
    ops = dram("ops", [2, NCH, P, 4, RT, C])
    vals = dram("vals", [NCH, P, RT, C])
    gateT, bonusT = dram("gateT", [RT, P, N]), dram("bonusT", [RT, P, N])
    yT = dram("yT", [2, RT, P, N])
    hn_rows = dram("hn_rows", [N, D])
    aff_rows = dram("aff_rows", [N, NE])
    with ExitStack() as ctx:
        KT = ctx.enter_context(nc.sbuf_tensor("KT", [P, 4, N], F32R))
        VS = ctx.enter_context(nc.sbuf_tensor("VS", [P, NT, KVH, P], F32R))
        attention_inputs(nc, ins["x"], ins["norm1"], ins["w_in"], ins["q_norm"], ins["k_norm"], ins["rope"], xT_hi, xT_lo, qT, KT, VS)
        attention(nc, qT, KT, VS, mixT, 0, NS // P, "sa")
        attention(nc, qT, KT, VS, mixT, NS // P, NP_ // P, "pa")
    with ExitStack() as ctx:
        WC = ctx.enter_context(nc.sbuf_tensor("WC", [P, 2, NB, 16], F32))
        rwkv_inputs(nc, ins["w_in"], ins["shift_taps"], ins["w0"], ins["w_lora_up"], ins["a0"], ins["a_lora_up"], ins["k_k"], ins["k_a"],
                    ins["r_k"], ins["g_lora_up"], xT_hi, xT_lo, ops, vals, gateT, bonusT, WC)
        recurrence(nc, ops, vals, WC, yT)
    with ExitStack() as ctx:
        logits = ctx.enter_context(nc.sbuf_tensor("logits", [P, NT, NE], F32))
        index = ctx.enter_context(nc.sbuf_tensor("index", [P, NE, 3], U32))
        mix_and_route(nc, ins["x"], ins["w_out"], ins["ln_g"], ins["ln_b"], ins["norm2"], ins["w_router"], yT, gateT, bonusT, mixT,
                      out, hn_rows, logits)
        choose(nc, logits, aff_rows, index)
        experts(nc, ins["expert_w_gate"], ins["expert_w_up"], ins["expert_w_down"], hn_rows, aff_rows, index, out)


def rope_table():
    inv_freq = np.float32(10000.0) ** (-np.arange(16, dtype=np.float32) / 16)
    tabs = []
    for n in (NS, NP_):
        row = np.repeat(np.arange(n // 64, dtype=np.float32), 64)[:, None] * inv_freq
        col = np.tile(np.arange(64, dtype=np.float32), n // 64)[:, None] * inv_freq
        cos = np.concatenate([np.cos(row), np.cos(row), np.cos(col), np.cos(col)], 1)
        sin = np.concatenate([-np.sin(row), np.sin(row), -np.sin(col), np.sin(col)], 1)
        tabs.append(np.stack([cos, sin], 1))
    return np.concatenate(tabs, 0).astype(np.float32)


def kernel(x_prompt, x_sample, norm1, w_in, shift_taps, w0, w_lora_up, a0, a_lora_up, k_k, k_a, r_k, g_lora_up, ln_g, ln_b,
           q_norm, k_norm, w_out, norm2, w_router, expert_w_gate, expert_w_up, expert_w_down):
    import concourse.bacc as _bacc
    from concourse.bass_utils import run_bass_kernel_spmd as _run

    arrays = dict(norm1=norm1, w_in=w_in, shift_taps=shift_taps, w0=w0, w_lora_up=w_lora_up, a0=a0, a_lora_up=a_lora_up, k_k=k_k,
                  k_a=k_a, r_k=r_k, g_lora_up=g_lora_up, ln_g=ln_g, ln_b=ln_b, q_norm=q_norm, k_norm=k_norm, w_out=w_out, norm2=norm2,
                  w_router=w_router, expert_w_gate=expert_w_gate, expert_w_up=expert_w_up, expert_w_down=expert_w_down)
    arrays = {name: np.ascontiguousarray(np.asarray(a)[0]) for name, a in arrays.items()}
    arrays["r_k"] = arrays["r_k"].reshape(-1)
    arrays["x"] = np.concatenate([np.asarray(x_sample)[0], np.asarray(x_prompt)[0]], 0)
    arrays["rope"] = rope_table()
    nc = _bacc.Bacc("TRN2", target_bir_lowering=False, num_devices=1)
    ins = {name: nc.dram_tensor(name, a.shape, F32, kind="ExternalInput").ap() for name, a in arrays.items()}
    out = nc.dram_tensor("out", [N, D], F32, kind="ExternalOutput").ap()
    program(nc, ins, out)
    y = np.asarray(_run(nc, [arrays], core_ids=[0]).results[0]["out"])
    return y[NS:].reshape(1, NP_, D), y[:NS].reshape(1, NS, D)
```
